# Optimizing a Trainium2 kernel written in Bass

```python
import jax
import jax.numpy as jnp
from jax import lax
import numpy as np
import math
import jax, jax.numpy as jnp

D_MODEL = 1024
BATCH = 1
SEQ = 256
DEPTH = 2

DN_HEADS = 4
DN_DK = 128
DN_DV = 128
DN_CONV = 4
DN_CHUNK = 64
DN_WIDTH = DN_HEADS * DN_DV
POOL_WINDOWS = (2, 4, 8, 16)
POOL_GROUP = 128
POOL_WIDTH = POOL_GROUP * len(POOL_WINDOWS)
SA_HEADS = 4
SA_HEAD_DIM = 128
SA_WIDTH = SA_HEADS * SA_HEAD_DIM
IDX_HEADS = 4
IDX_DIM = 64
TOPK_MAX = 256
Q_BLOCK = 128
ROPE_THETA = 10000.0
NORM_EPS = 1e-6
N_BRANCH = 3
BRANCH_WIDTH = 512
SPLIT_SIZES = (DN_WIDTH, DN_WIDTH, DN_WIDTH, DN_WIDTH, DN_HEADS, DN_HEADS,
               POOL_WIDTH, POOL_WIDTH,
               SA_WIDTH, SA_WIDTH, SA_WIDTH, SA_WIDTH, IDX_HEADS * IDX_DIM, IDX_DIM, IDX_HEADS,
               N_BRANCH * D_MODEL)
IN_WIDTH = sum(SPLIT_SIZES)


def rms_norm(x, g):
    x32 = x.astype(jnp.float32)
    y = x32 * lax.rsqrt(jnp.mean(x32 * x32, axis=-1, keepdims=True) + NORM_EPS)
    return y.astype(x.dtype) * g

def l2_normalize(x):
    x32 = x.astype(jnp.float32)
    return x32 * lax.rsqrt(jnp.sum(x32 * x32, axis=-1, keepdims=True) + NORM_EPS)

def rope_tables(seq_len, dim):
    inv_freq = ROPE_THETA ** (-jnp.arange(0, dim, 2, dtype=jnp.float32) / dim)
    ang = jnp.arange(seq_len, dtype=jnp.float32)[:, None] * inv_freq[None, :]
    return jnp.cos(ang), jnp.sin(ang)

def apply_rope(x, cos, sin):
    x32 = x.astype(jnp.float32)
    x1, x2 = jnp.split(x32, 2, axis=-1)
    c = cos[None, :, None, :]
    s = sin[None, :, None, :]
    return jnp.concatenate([x1 * c - x2 * s, x2 * c + x1 * s], axis=-1).astype(x.dtype)

def split_columns(proj):
    parts = []
    start = 0
    for size in SPLIT_SIZES:
        parts.append(proj[..., start:start + size])
        start += size
    return parts

def causal_depthwise_conv(x, w):
    k = w.shape[0]
    return lax.conv_general_dilated(x, w[:, None, :], window_strides=(1,), padding=((k - 1, 0),),
                                    dimension_numbers=('NWC', 'WIO', 'NWC'),
                                    feature_group_count=x.shape[-1])

def chunk_gated_delta_rule(q, k, v, beta, g):
    b, t, h, dk = q.shape
    dv = v.shape[-1]
    n = t // DN_CHUNK
    c = DN_CHUNK
    to_chunks4 = lambda a: a.reshape(b, n, c, h, a.shape[-1]).transpose(1, 0, 3, 2, 4)
    to_chunks3 = lambda a: a.reshape(b, n, c, h).transpose(1, 0, 3, 2)
    qc = to_chunks4(q * (dk ** -0.5))
    kc = to_chunks4(k)
    vc = to_chunks4(v)
    bc = to_chunks3(beta)
    gc = jnp.cumsum(to_chunks3(g), axis=-1)
    tril = jnp.tril(jnp.ones((c, c), dtype=bool))
    strict = jnp.tril(jnp.ones((c, c), dtype=bool), -1)
    decay = jnp.exp(jnp.where(tril, gc[..., :, None] - gc[..., None, :], -jnp.inf))
    k_beta = kc * bc[..., None]
    v_beta = vc * bc[..., None]
    lmat = jnp.where(strict, jnp.einsum('nbhid,nbhjd->nbhij', k_beta, kc) * decay, 0.0)
    eye = jnp.eye(c, dtype=jnp.float32)
    tmat = lax.linalg.triangular_solve(eye + lmat, jnp.broadcast_to(eye, lmat.shape),
                                       left_side=True, lower=True, unit_diagonal=True)
    u = jnp.einsum('nbhij,nbhjd->nbhid', tmat, v_beta)
    w = jnp.einsum('nbhij,nbhjd->nbhid', tmat, k_beta * jnp.exp(gc)[..., None])
    attn_intra = jnp.where(tril, jnp.einsum('nbhid,nbhjd->nbhij', qc, kc) * decay, 0.0)

    def step(state, xs):
        q_i, k_i, u_i, w_i, g_i, a_i = xs
        v_new = u_i - jnp.einsum('bhck,bhkv->bhcv', w_i, state)
        o = (jnp.einsum('bhck,bhkv->bhcv', q_i * jnp.exp(g_i)[..., None], state)
             + jnp.einsum('bhij,bhjv->bhiv', a_i, v_new))
        g_last = g_i[..., -1:]
        state = (state * jnp.exp(g_last)[..., None]
                 + jnp.einsum('bhck,bhcv->bhkv', k_i * jnp.exp(g_last - g_i)[..., None], v_new))
        return state, o

    state0 = jnp.zeros((b, h, dk, dv), dtype=jnp.float32)
    _, o = lax.scan(step, state0, (qc, kc, u, w, gc, attn_intra))
    return o.transpose(1, 0, 3, 2, 4).reshape(b, t, h, dv)

def deltanet_branch(qa, ka, va, za, ba, aa, conv_w, a_log, dt_bias, o_norm):
    b, t, _ = qa.shape
    qkv = jax.nn.silu(causal_depthwise_conv(jnp.concatenate([qa, ka, va], axis=-1), conv_w))
    q, k, v = jnp.split(qkv, 3, axis=-1)
    q = l2_normalize(q.reshape(b, t, DN_HEADS, DN_DK))
    k = l2_normalize(k.reshape(b, t, DN_HEADS, DN_DK))
    v = v.reshape(b, t, DN_HEADS, DN_DV).astype(jnp.float32)
    beta = jax.nn.sigmoid(ba.astype(jnp.float32))
    g = -jnp.exp(a_log.astype(jnp.float32)) * jax.nn.softplus(aa.astype(jnp.float32) + dt_bias.astype(jnp.float32))
    o = chunk_gated_delta_rule(q, k, v, beta, g)
    o = rms_norm(o, o_norm) * jax.nn.silu(za.reshape(b, t, DN_HEADS, DN_DV))
    return o.reshape(b, t, DN_WIDTH)

def pooling_branch(u, z, pool_w, pool_scale):
    b, t, _ = u.shape
    u32 = u.astype(jnp.float32)
    cs = jnp.cumsum(u32, axis=1)
    pos_count = jnp.arange(1, t + 1, dtype=jnp.int32)
    groups = []
    for gi, win in enumerate(POOL_WINDOWS):
        sl = slice(gi * POOL_GROUP, (gi + 1) * POOL_GROUP)
        cs_g = cs[..., sl]
        lagged = jnp.pad(cs_g, ((0, 0), (win, 0), (0, 0)))[:, :t]
        count = jnp.minimum(pos_count, win).astype(jnp.float32)[None, :, None]
        groups.append((cs_g - lagged) / count - u32[..., sl])
    pooled = jnp.stack(groups, axis=2)
    mixed = jnp.einsum('btgc,gcd->btgd', pooled.astype(pool_w.dtype), pool_w).reshape(b, t, POOL_WIDTH)
    return mixed * pool_scale * jax.nn.silu(z)

def sparse_attention_branch(qc, kc, vc, zc, iq, ik, iw, q_norm, k_norm, cos_a, sin_a, cos_i, sin_i):
    b, t, _ = qc.shape
    q = apply_rope(rms_norm(qc.reshape(b, t, SA_HEADS, SA_HEAD_DIM), q_norm), cos_a, sin_a)
    k = apply_rope(rms_norm(kc.reshape(b, t, SA_HEADS, SA_HEAD_DIM), k_norm), cos_a, sin_a)
    v = vc.reshape(b, t, SA_HEADS, SA_HEAD_DIM)
    qi = apply_rope(iq.reshape(b, t, IDX_HEADS, IDX_DIM), cos_i, sin_i)
    ki = apply_rope(ik.reshape(b, t, 1, IDX_DIM), cos_i, sin_i)[:, :, 0].astype(jnp.float32)
    wi = iw.astype(jnp.float32) * (IDX_HEADS ** -0.5 * IDX_DIM ** -0.5)
    topk = min(TOPK_MAX, t // 4)
    nb = t // Q_BLOCK
    to_blocks = lambda a: a.reshape((b, nb, Q_BLOCK) + a.shape[2:]).swapaxes(0, 1)
    key_pos = jnp.arange(t, dtype=jnp.int32)
    gather_rows = jax.vmap(lambda src, idx: src[idx])

    def attend(xs):
        q_b, qi_b, wi_b, start = xs
        q_pos = start + jnp.arange(Q_BLOCK, dtype=jnp.int32)
        causal = key_pos[None, :] <= q_pos[:, None]
        dots = jnp.einsum('bqhd,bsd->bqhs', qi_b.astype(jnp.float32), ki)
        score = jnp.einsum('bqh,bqhs->bqs', wi_b, jax.nn.relu(dots))
        score = jnp.where(causal[None], score, -jnp.inf)
        _, idx = lax.top_k(score, topk)
        k_sel = gather_rows(k, idx)
        v_sel = gather_rows(v, idx)
        logits = jnp.einsum('bqhd,bqkhd->bhqk', q_b.astype(jnp.float32), k_sel.astype(jnp.float32)) * (SA_HEAD_DIM ** -0.5)
        valid = idx <= q_pos[None, :, None]
        logits = jnp.where(valid[:, None], logits, -jnp.inf)
        p = jax.nn.softmax(logits, axis=-1)
        return jnp.einsum('bhqk,bqkhd->bqhd', p.astype(v_sel.dtype), v_sel)

    starts = jnp.arange(nb, dtype=jnp.int32) * Q_BLOCK
    o = lax.map(attend, (to_blocks(q), to_blocks(qi), to_blocks(wi), starts))
    o = o.swapaxes(0, 1).reshape(b, t, SA_WIDTH)
    return o * jax.nn.silu(zc)

def hybrid_layer(x, norm_g, w_in, gate_b, conv_w, a_log, dt_bias, dn_onorm, pool_w, pool_scale,
                 q_norm, k_norm, w_branch, w_out, cos_a, sin_a, cos_i, sin_i):
    b, t, _ = x.shape
    h = rms_norm(x, norm_g)
    proj = jnp.einsum('btd,de->bte', h, w_in)
    (qa, ka, va, za, ba, aa, ub, zb, qc, kc, vc, zc, iq, ik, iw, gates) = split_columns(proj)
    ya = deltanet_branch(qa, ka, va, za, ba, aa, conv_w, a_log, dt_bias, dn_onorm)
    yb = pooling_branch(ub, zb, pool_w, pool_scale)
    yc = sparse_attention_branch(qc, kc, vc, zc, iq, ik, iw, q_norm, k_norm, cos_a, sin_a, cos_i, sin_i)
    branches = jnp.stack([ya, yb, yc], axis=2).astype(w_branch.dtype)
    projected = jnp.einsum('btnc,ncd->btnd', branches, w_branch)
    gate = jax.nn.sigmoid(gates.reshape(b, t, N_BRANCH, D_MODEL).astype(jnp.float32) + gate_b.astype(jnp.float32))
    merged = jnp.sum(gate * projected, axis=2).astype(w_out.dtype)
    return x + jnp.einsum('btd,de->bte', merged, w_out).astype(x.dtype)

def first_inputs(seed: int = 0) -> dict:
    key = jax.random.key(seed)
    ks = jax.random.split(key, 16)
    f32 = jnp.float32
    x = jax.random.normal(ks[0], (BATCH, SEQ, D_MODEL), f32)
    norm_g = 1.0 + 0.02 * jax.random.normal(ks[1], (DEPTH, D_MODEL), f32)
    w_in = jax.random.normal(ks[2], (DEPTH, D_MODEL, IN_WIDTH), f32) * D_MODEL ** -0.5
    gate_b = 0.02 * jax.random.normal(ks[3], (DEPTH, N_BRANCH, D_MODEL), f32)
    conv_w = jax.random.normal(ks[4], (DEPTH, DN_CONV, 3 * DN_WIDTH), f32) * DN_CONV ** -0.5
    a_log = jnp.log(jax.random.uniform(ks[5], (DEPTH, DN_HEADS), f32, minval=1.0, maxval=16.0))
    dt = jnp.exp(jax.random.uniform(ks[6], (DEPTH, DN_HEADS), f32, minval=float(np.log(1e-3)), maxval=float(np.log(1e-1))))
    dt_bias = dt + jnp.log(-jnp.expm1(-dt))
    dn_onorm = 1.0 + 0.02 * jax.random.normal(ks[7], (DEPTH, DN_DV), f32)
    pool_w = jax.random.normal(ks[8], (DEPTH, len(POOL_WINDOWS), POOL_GROUP, POOL_GROUP), f32) * POOL_GROUP ** -0.5
    pool_scale = 1.0 + 0.1 * jax.random.normal(ks[9], (DEPTH, POOL_WIDTH), f32)
    q_norm = 1.0 + 0.02 * jax.random.normal(ks[10], (DEPTH, SA_HEAD_DIM), f32)
    k_norm = 1.0 + 0.02 * jax.random.normal(ks[11], (DEPTH, SA_HEAD_DIM), f32)
    w_branch = jax.random.normal(ks[12], (DEPTH, N_BRANCH, BRANCH_WIDTH, D_MODEL), f32) * BRANCH_WIDTH ** -0.5
    w_out = jax.random.normal(ks[13], (DEPTH, D_MODEL, D_MODEL), f32) * D_MODEL ** -0.5
    return {'x': x, 'norm_g': norm_g, 'w_in': w_in, 'gate_b': gate_b, 'conv_w': conv_w,
            'a_log': a_log, 'dt_bias': dt_bias, 'dn_onorm': dn_onorm, 'pool_w': pool_w,
            'pool_scale': pool_scale, 'q_norm': q_norm, 'k_norm': k_norm,
            'w_branch': w_branch, 'w_out': w_out}

def first_block(x, norm_g, w_in, gate_b, conv_w, a_log, dt_bias, dn_onorm, pool_w, pool_scale,
              q_norm, k_norm, w_branch, w_out):
    t = x.shape[1]
    cos_a, sin_a = rope_tables(t, SA_HEAD_DIM)
    cos_i, sin_i = rope_tables(t, IDX_DIM)
    for layer in range(DEPTH):
        x = hybrid_layer(x, norm_g[layer], w_in[layer], gate_b[layer], conv_w[layer], a_log[layer],
                         dt_bias[layer], dn_onorm[layer], pool_w[layer], pool_scale[layer],
                         q_norm[layer], k_norm[layer], w_branch[layer], w_out[layer],
                         cos_a, sin_a, cos_i, sin_i)
    return x


HEAD_DIM = 64
H_SB = 4
H_FOX = 4
H_MLA = 4
H_DIL = 4
N_HEADS_OUT = H_SB + H_FOX + H_MLA + H_DIL
D_MIX = N_HEADS_OUT * HEAD_DIM
MLA_Q_LORA = 256
MLA_KV_LORA = 128
MLA_NOPE = 64
MLA_ROPE = 32
MLA_V = HEAD_DIM
DIL_BRANCHES = ((128, 1), (512, 4), (2048, 16))
N_BR = len(DIL_BRANCHES)
N_SB = 3 * H_SB * HEAD_DIM
N_FOX = 3 * H_FOX * HEAD_DIM + H_FOX
N_MLA = MLA_Q_LORA + MLA_KV_LORA + MLA_ROPE
N_DIL = 3 * N_BR * H_DIL * HEAD_DIM
N_IN = N_SB + N_FOX + N_MLA + N_DIL
N_GROUPS = 4
EXPERTS_PER_GROUP = 4
N_EXPERTS = N_GROUPS * EXPERTS_PER_GROUP
TOP_K = 2
D_EXPERT = 512
MOE_BLOCK = 256
LN_EPS = 1e-5
RMS_EPS = 1e-6


def _layernorm(x, g, b):
    xf = x.astype(jnp.float32)
    mu = jnp.mean(xf, -1, keepdims=True)
    var = jnp.mean(jnp.square(xf - mu), -1, keepdims=True)
    return ((xf - mu) * lax.rsqrt(var + LN_EPS) * g + b).astype(x.dtype)

def _rmsnorm(x, g):
    xf = x.astype(jnp.float32)
    return (xf * lax.rsqrt(jnp.mean(jnp.square(xf), -1, keepdims=True) + RMS_EPS) * g).astype(x.dtype)

def _rope(x, pos):
    half = x.shape[-1] // 2
    inv_freq = ROPE_THETA ** (-jnp.arange(half, dtype=jnp.float32) / half)
    ang = pos.astype(jnp.float32)[:, None] * inv_freq[None, :]
    cos = jnp.cos(ang)[None, :, None, :]
    sin = jnp.sin(ang)[None, :, None, :]
    xf = x.astype(jnp.float32)
    x1, x2 = xf[..., :half], xf[..., half:]
    return jnp.concatenate([x1 * cos - x2 * sin, x2 * cos + x1 * sin], -1).astype(x.dtype)

def _sweep(block_fn, seq):
    out = lax.map(block_fn, jnp.arange(seq // Q_BLOCK, dtype=jnp.int32) * Q_BLOCK)
    nb, b, h, blk, dv = out.shape
    return out.transpose(1, 2, 0, 3, 4).reshape(b, h, nb * blk, dv)

def _causal_softmax_sweep(logits_fn, v):
    seq = v.shape[2]
    kpos = jnp.arange(seq)

    def block(t0):
        logits = logits_fn(t0)
        qpos = t0 + jnp.arange(Q_BLOCK)
        mask = kpos[None, :] <= qpos[:, None]
        p = jax.nn.softmax(jnp.where(mask, logits, -jnp.inf), axis=-1)
        return jnp.einsum('bhqk,bhkd->bhqd', p.astype(v.dtype), v)

    return _sweep(block, seq)

def _stick_breaking_attention(q, k, v):
    seq = q.shape[2]
    scale = q.shape[-1] ** -0.5
    kpos = jnp.arange(seq)

    def block(t0):
        qb = lax.dynamic_slice_in_dim(q, t0, Q_BLOCK, axis=2)
        z = jnp.einsum('bhqd,bhkd->bhqk', qb, k).astype(jnp.float32) * scale
        qpos = t0 + jnp.arange(Q_BLOCK)
        before = kpos[None, :] < qpos[:, None]
        log_keep = jnp.where(before, jax.nn.log_sigmoid(-z), 0.0)
        log_after = lax.cumsum(log_keep, axis=3, reverse=True) - log_keep
        w = jnp.where(before, jnp.exp(jax.nn.log_sigmoid(z) + log_after), 0.0)
        return jnp.einsum('bhqk,bhkd->bhqd', w.astype(v.dtype), v)

    return _sweep(block, seq)

def _forgetting_attention(q, k, v, log_f):
    scale = q.shape[-1] ** -0.5
    c = jnp.cumsum(log_f, axis=-1)

    def logits(t0):
        qb = lax.dynamic_slice_in_dim(q, t0, Q_BLOCK, axis=2)
        cb = lax.dynamic_slice_in_dim(c, t0, Q_BLOCK, axis=2)
        s = jnp.einsum('bhqd,bhkd->bhqk', qb, k).astype(jnp.float32) * scale
        return s + cb[..., :, None] - c[..., None, :]

    return _causal_softmax_sweep(logits, v)

def _mla_attention(q_nope, q_rope, k_nope, k_rope, v):
    scale = (q_nope.shape[-1] + q_rope.shape[-1]) ** -0.5

    def logits(t0):
        qn = lax.dynamic_slice_in_dim(q_nope, t0, Q_BLOCK, axis=2)
        qr = lax.dynamic_slice_in_dim(q_rope, t0, Q_BLOCK, axis=2)
        s = (jnp.einsum('bhqd,bhkd->bhqk', qn, k_nope).astype(jnp.float32)
             + jnp.einsum('bhqr,bkr->bhqk', qr, k_rope).astype(jnp.float32))
        return s * scale

    return _causal_softmax_sweep(logits, v)

def _dilated_attention(qs, ks, vs):
    seq = qs[0].shape[1]
    scale = qs[0].shape[-1] ** -0.5

    def block(t0):
        qpos = t0 + jnp.arange(Q_BLOCK)
        outs, lses = [], []
        for (window, dil), q, k, v in zip(DIL_BRANCHES, qs, ks, vs):
            n_keys = window // dil + 1
            idx = qpos[:, None] - dil * jnp.arange(n_keys)[None, :]
            valid = idx >= 0
            idx = jnp.maximum(idx, 0)
            qb = lax.dynamic_slice_in_dim(q, t0, Q_BLOCK, axis=1)
            kb = jnp.take(k, idx, axis=1)
            vb = jnp.take(v, idx, axis=1)
            z = jnp.einsum('bqhd,bqnhd->bhqn', qb, kb).astype(jnp.float32) * scale
            z = jnp.where(valid[None, None], z, -jnp.inf)
            m = jnp.max(z, -1, keepdims=True)
            p = jnp.exp(z - m)
            den = jnp.sum(p, -1, keepdims=True)
            outs.append(jnp.einsum('bhqn,bqnhd->bhqd', (p / den).astype(v.dtype), vb).astype(jnp.float32))
            lses.append(m + jnp.log(den))
        mix = jax.nn.softmax(jnp.stack(lses), axis=0)
        return jnp.sum(mix * jnp.stack(outs), axis=0).astype(vs[0].dtype)

    return _sweep(block, seq)

def _mixing(x, w_in, b_forget, g_cq, g_ckv, w_uq, w_ukv, g_head, w_out):
    bsz, seq, _ = x.shape
    pos = jnp.arange(seq)
    proj = x @ w_in
    p_sb, p_fox, p_mla, p_dil = jnp.split(proj, [N_SB, N_SB + N_FOX, N_SB + N_FOX + N_MLA], axis=-1)

    def heads(t, n):
        return t.reshape(bsz, seq, n, -1).transpose(0, 2, 1, 3)

    q, k, v = jnp.split(p_sb, 3, axis=-1)
    o_sb = _stick_breaking_attention(heads(q, H_SB), heads(k, H_SB), heads(v, H_SB))

    hd = H_FOX * HEAD_DIM
    q, k, v, f = jnp.split(p_fox, [hd, 2 * hd, 3 * hd], axis=-1)
    log_f = jax.nn.log_sigmoid((f + b_forget).astype(jnp.float32)).transpose(0, 2, 1)
    o_fox = _forgetting_attention(heads(q, H_FOX), heads(k, H_FOX), heads(v, H_FOX), log_f)

    c_q, c_kv, k_r = jnp.split(p_mla, [MLA_Q_LORA, MLA_Q_LORA + MLA_KV_LORA], axis=-1)
    q = (_rmsnorm(c_q, g_cq) @ w_uq).reshape(bsz, seq, H_MLA, MLA_NOPE + MLA_ROPE)
    kv = (_rmsnorm(c_kv, g_ckv) @ w_ukv).reshape(bsz, seq, H_MLA, MLA_NOPE + MLA_V)
    q_rope = _rope(q[..., MLA_NOPE:], pos)
    k_rope = _rope(k_r[:, :, None, :], pos)[:, :, 0]
    tr = lambda a: a.transpose(0, 2, 1, 3)
    o_mla = _mla_attention(tr(q[..., :MLA_NOPE]), tr(q_rope), tr(kv[..., :MLA_NOPE]), k_rope,
                           tr(kv[..., MLA_NOPE:]))

    q, k, v = jnp.split(p_dil, 3, axis=-1)
    br = lambda a: a.reshape(bsz, seq, N_BR, H_DIL, HEAD_DIM)
    flat = lambda a: a.reshape(bsz, seq, N_BR * H_DIL, HEAD_DIM)
    q = br(_rope(flat(q), pos))
    k = br(_rope(flat(k), pos))
    v = br(v)
    o_dil = _dilated_attention([q[:, :, i] for i in range(N_BR)],
                               [k[:, :, i] for i in range(N_BR)],
                               [v[:, :, i] for i in range(N_BR)])

    o = jnp.concatenate([o_sb, o_fox, o_mla, o_dil], axis=1)
    o = _rmsnorm(o, g_head[None, :, None, :])
    return o.transpose(0, 2, 1, 3).reshape(bsz, seq, D_MIX) @ w_out

def _hier_moe(x, w_group, b_group, w_expert, b_expert, w1, w3, w2):
    n_tok, d = x.shape
    xf = x.astype(jnp.float32)
    g_logits = xf @ w_group.astype(jnp.float32) + b_group.astype(jnp.float32)
    g_sel = jnp.argmax(g_logits, axis=-1)
    g_w = jnp.take_along_axis(jax.nn.softmax(g_logits, -1), g_sel[:, None], axis=-1)
    e_logits = (xf @ w_expert.astype(jnp.float32) + b_expert.astype(jnp.float32)).reshape(
        n_tok, N_GROUPS, EXPERTS_PER_GROUP)
    e_in_group = jnp.take_along_axis(e_logits, g_sel[:, None, None], axis=1)[:, 0]
    top_logit, top_idx = lax.top_k(e_in_group, TOP_K)
    gate = jax.nn.softmax(top_logit, -1) * g_w
    expert_id = (g_sel[:, None] * EXPERTS_PER_GROUP + top_idx).reshape(-1).astype(jnp.int32)

    n_assign = n_tok * TOP_K
    n_slots = n_assign + N_EXPERTS * MOE_BLOCK
    n_chunks = n_slots // MOE_BLOCK
    tok_id = jnp.repeat(jnp.arange(n_tok, dtype=jnp.int32), TOP_K)
    order = jnp.argsort(expert_id)
    e_sorted = expert_id[order]
    counts = jnp.bincount(expert_id, length=N_EXPERTS)
    start = jnp.cumsum(counts) - counts
    padded = (counts + MOE_BLOCK - 1) // MOE_BLOCK * MOE_BLOCK
    pad_end = jnp.cumsum(padded)
    pad_start = pad_end - padded
    dest = pad_start[e_sorted] + jnp.arange(n_assign) - start[e_sorted]
    slot_tok = jnp.full((n_slots,), n_tok, jnp.int32).at[dest].set(tok_id[order])
    slot_gate = jnp.zeros((n_slots,), jnp.float32).at[dest].set(gate.reshape(-1)[order])
    chunk_expert = jnp.minimum(
        jnp.searchsorted(pad_end, jnp.arange(n_chunks) * MOE_BLOCK, side='right'), N_EXPERTS - 1)
    x_pad = jnp.concatenate([x, jnp.zeros((1, d), x.dtype)], axis=0)
    xs = x_pad[slot_tok].reshape(n_chunks, MOE_BLOCK, d)

    def expert_block(args):
        xb, e = args
        h = jax.nn.silu(xb @ w1[e]) * (xb @ w3[e])
        return h @ w2[e]

    ys = lax.map(expert_block, (xs, chunk_expert)).reshape(n_slots, d)
    ys = ys * slot_gate[:, None].astype(ys.dtype)
    return jax.ops.segment_sum(ys, slot_tok, num_segments=n_tok + 1)[:n_tok]

def second_inputs(seed: int = 0) -> dict:
    key = jax.random.key(seed)
    ks = jax.random.split(key, 20)
    L = DEPTH
    beta = (8.0 * DEPTH) ** -0.25
    f32 = jnp.float32

    def normal(k, shape, scale):
        return jax.random.normal(k, shape, f32) * scale

    return {
        'x': normal(ks[0], (BATCH, SEQ, D_MODEL), 1.0),
        'w_in': normal(ks[1], (L, D_MODEL, N_IN), D_MODEL ** -0.5),
        'b_forget': normal(ks[2], (L, H_FOX), 0.1),
        'g_cq': 1.0 + normal(ks[3], (L, MLA_Q_LORA), 0.02),
        'g_ckv': 1.0 + normal(ks[4], (L, MLA_KV_LORA), 0.02),
        'w_uq': normal(ks[5], (L, MLA_Q_LORA, H_MLA * (MLA_NOPE + MLA_ROPE)), MLA_Q_LORA ** -0.5),
        'w_ukv': normal(ks[6], (L, MLA_KV_LORA, H_MLA * (MLA_NOPE + MLA_V)), MLA_KV_LORA ** -0.5),
        'g_head': 1.0 + normal(ks[7], (L, N_HEADS_OUT, HEAD_DIM), 0.02),
        'w_out': normal(ks[8], (L, D_MIX, D_MODEL), beta * D_MIX ** -0.5),
        'ln1_g': 1.0 + normal(ks[9], (L, D_MODEL), 0.02),
        'ln1_b': normal(ks[10], (L, D_MODEL), 0.02),
        'w_group': normal(ks[11], (L, D_MODEL, N_GROUPS), D_MODEL ** -0.5),
        'b_group': normal(ks[12], (L, N_GROUPS), 0.01),
        'w_expert': normal(ks[13], (L, D_MODEL, N_EXPERTS), D_MODEL ** -0.5),
        'b_expert': normal(ks[14], (L, N_EXPERTS), 0.01),
        'w1': normal(ks[15], (L, N_EXPERTS, D_MODEL, D_EXPERT), D_MODEL ** -0.5),
        'w3': normal(ks[16], (L, N_EXPERTS, D_MODEL, D_EXPERT), D_MODEL ** -0.5),
        'w2': normal(ks[17], (L, N_EXPERTS, D_EXPERT, D_MODEL), beta * D_EXPERT ** -0.5),
        'ln2_g': 1.0 + normal(ks[18], (L, D_MODEL), 0.02),
        'ln2_b': normal(ks[19], (L, D_MODEL), 0.02),
    }

def second_block(x, w_in, b_forget, g_cq, g_ckv, w_uq, w_ukv, g_head, w_out, ln1_g, ln1_b,
              w_group, b_group, w_expert, b_expert, w1, w3, w2, ln2_g, ln2_b):
    alpha = (2.0 * DEPTH) ** 0.25
    bsz, seq, d = x.shape
    for l in range(DEPTH):
        h = _mixing(x, w_in[l], b_forget[l], g_cq[l], g_ckv[l], w_uq[l], w_ukv[l], g_head[l], w_out[l])
        x = _layernorm(alpha * x + h, ln1_g[l], ln1_b[l])
        m = _hier_moe(x.reshape(bsz * seq, d), w_group[l], b_group[l], w_expert[l], b_expert[l],
                      w1[l], w3[l], w2[l]).reshape(bsz, seq, d)
        x = _layernorm(alpha * x + m, ln2_g[l], ln2_b[l])
    return x


def setup_inputs(seed=0):
    out = dict(first_inputs(seed))
    for name, value in second_inputs(seed + 1).items():
        if name != "x":
            out[name + "_2"] = value
    return out


def reference(
    x, norm_g, w_in, gate_b, conv_w, a_log, dt_bias, dn_onorm, pool_w, pool_scale, q_norm,
    k_norm, w_branch, w_out, w_in_2, b_forget_2, g_cq_2, g_ckv_2, w_uq_2, w_ukv_2, g_head_2,
    w_out_2, ln1_g_2, ln1_b_2, w_group_2, b_group_2, w_expert_2, b_expert_2, w1_2, w3_2, w2_2,
    ln2_g_2, ln2_b_2,
):
    x = first_block(
        x, norm_g, w_in, gate_b, conv_w, a_log, dt_bias, dn_onorm, pool_w, pool_scale, q_norm,
        k_norm, w_branch, w_out,
    )
    return second_block(
        x, w_in_2, b_forget_2, g_cq_2, g_ckv_2, w_uq_2, w_ukv_2, g_head_2, w_out_2, ln1_g_2,
        ln1_b_2, w_group_2, b_group_2, w_expert_2, b_expert_2, w1_2, w3_2, w2_2, ln2_g_2,
        ln2_b_2,
    )


_drawn_inputs = setup_inputs


def setup_inputs(seed=0):
    import zlib

    import numpy as np

    out = dict(_drawn_inputs(seed))
    spreads = {}
    factors = {'gate_b': 7.077,
     'dn_onorm': 4.514,
     'q_norm': 8.0,
     'k_norm': 8.0,
     'b_forget_2': 8.0,
     'g_cq_2': 8.0,
     'g_ckv_2': 8.0,
     'g_head_2': 5.798,
     'b_group_2': 8.0,
     'b_expert_2': 6.697}
    for name, (base, spread) in spreads.items():
        noise = np.random.default_rng([zlib.crc32(name.encode()), seed]).standard_normal(out[name].shape)
        drawn = base * np.exp(spread * noise) if base else spread * noise
        out[name] = jnp.asarray(drawn.astype(out[name].dtype))
    for name, factor in factors.items():
        out[name] = (out[name] * factor).astype(out[name].dtype)
    return out
```

```python
from contextlib import ExitStack

import numpy as np

import concourse.bass as bass
from concourse import mybir

F32 = mybir.dt.float32
ALU = mybir.AluOpType
ACT = mybir.ActivationFunctionType
AX = mybir.AxisListType

P = 128
T = 256
NT = T // P
D = 1024
KD = D // P
DEPTH = 2
H = 4
CHUNK = 64
TOPK = 64
WINDOWS = (2, 4, 8, 16)
PAD = 16
CONV = 4
NEG = -1.0e30
TAKEN = -3.0e38
EXPERTS = 16
GROUPS = 4
SLOT = 4096
NSLOT = 4
W_A = 8524
W_B = 4260
ALPHA = float((2.0 * DEPTH) ** 0.25)

A_QKV, A_ZA, A_BA, A_UB, A_ZB = 0, 1536, 2048, 2056, 2568
A_QC, A_KC, A_VC, A_ZC, A_IQ, A_GATE = 3080, 3592, 4104, 4616, 5128, 5452
B_SBQK, B_SBV, B_FOXQ, B_FOXK, B_FOXV, B_F = 0, 512, 768, 1024, 1280, 1536
B_CQ, B_CKV, B_KR, B_DQ, B_DK, B_DV = 1540, 1796, 1924, 1956, 2724, 3492


def layout(parts):
    at, where = 0, {}
    for name, width in parts:
        where[name] = (at, at + width)
        at += width
    return where, at


CONST_A, WIDTH_CA = layout([
    ("ident", P), ("cumsum", P), ("chunk", P), ("later", P), ("strict", P), ("merge", 6 * P),
    ("rot_head", P), ("rot_index", P), ("cos_head", T), ("sin_head", T), ("cos_index", T), ("sin_index", T),
    ("count", len(WINDOWS) * T), ("causal", NT * T)])
CONST_B, WIDTH_CB = layout([
    ("ident", P), ("upto", P), ("after", P), ("pair", P), ("rot64", P), ("rot_mla", P),
    ("cos64", T), ("sin64", T), ("cos_mla", T), ("sin_mla", T), ("before", NT * T), ("causal", NT * T),
    ("dilated", 3 * NT * T)])
PARAM_A, WIDTH_PA = layout([
    ("norm_g", KD), ("conv_w", 12 * CONV), ("gate_b", 24), ("o_norm", 1), ("pool_scale", 4),
    ("q_norm", 1), ("k_norm", 1), ("a_log", H), ("dt_bias", H), ("pool_w", 4 * P)])
PARAM_B, WIDTH_PB = layout([
    ("b_forget", H), ("g_cq", 2), ("g_ckv", 1), ("g_head", 8), ("b_router", 20), ("w_router", KD * 20),
    ("w_uq", 2 * 384), ("w_ukv", 512)])


def rotation(n, half, first=0, size=P):
    m = np.zeros((P, size), np.float32)
    for at in range(first, n, 2 * half):
        for i in range(half):
            m[at + half + i, at + i] = -1.0
            m[at + i, at + half + i] = 1.0
    return m


def rope(half, copies):
    freq = np.float32(10000.0) ** (-np.arange(half, dtype=np.float32) / np.float32(half))
    angle = (np.arange(T, dtype=np.float32)[:, None] * freq[None, :].astype(np.float32)).T
    return np.tile(np.cos(angle), (copies, 1)).astype(np.float32), np.tile(np.sin(angle), (copies, 1)).astype(np.float32)


def constants():
    a = np.zeros((P, WIDTH_CA), np.float32)
    b = np.zeros((P, WIDTH_CB), np.float32)

    def put(to, where, name, value):
        lo, hi = where[name]
        to[:value.shape[0], lo:hi] = value.reshape(value.shape[0], hi - lo)

    r, c = np.arange(P)[:, None], np.arange(P)[None, :]
    same = (r // CHUNK) == (c // CHUNK)
    q = np.arange(P)[:, None, None] + P * np.arange(NT)[None, :, None]
    k = np.arange(T)[None, None, :]
    causal = np.where(k <= q, 0.0, NEG)
    put(a, CONST_A, "ident", np.eye(P))
    put(a, CONST_A, "cumsum", (same & (r <= c)) * 1.0)
    put(a, CONST_A, "chunk", same * 1.0)
    put(a, CONST_A, "later", np.where(same & (r <= c), 0.0, NEG))
    put(a, CONST_A, "strict", (same & (r < c)) * 1.0)
    merge = [((r // (2 * s)) == (c // (2 * s))) & ((r // s) % 2 == 0) & ((c // s) % 2 == 1) for s in (1, 2, 4, 8, 16, 32)]
    put(a, CONST_A, "merge", np.stack(merge, 1) * 1.0)
    put(a, CONST_A, "rot_head", rotation(P, 64))
    put(a, CONST_A, "rot_index", rotation(64, 32))
    cos, sin = rope(64, 2)
    put(a, CONST_A, "cos_head", cos)
    put(a, CONST_A, "sin_head", sin)
    cos, sin = rope(32, 4)
    put(a, CONST_A, "cos_index", cos)
    put(a, CONST_A, "sin_index", sin)
    count = np.stack([1.0 / np.minimum(np.arange(1, T + 1), w).astype(np.float32) for w in WINDOWS])
    put(a, CONST_A, "count", np.tile(count.reshape(1, -1), (P, 1)))
    put(a, CONST_A, "causal", causal)
    put(b, CONST_B, "ident", np.eye(P))
    put(b, CONST_B, "upto", (r <= c) * 1.0)
    put(b, CONST_B, "after", (r > c) * 1.0)
    put(b, CONST_B, "pair", same * 1.0)
    put(b, CONST_B, "rot64", rotation(P, 32))
    put(b, CONST_B, "rot_mla", rotation(96, 16, 64))
    put(b, CONST_B, "cos64", cos)
    put(b, CONST_B, "sin64", sin)
    cos, sin = rope(16, 2)
    put(b, CONST_B, "cos_mla", np.concatenate([np.ones((64, T), np.float32), cos]))
    put(b, CONST_B, "sin_mla", np.concatenate([np.zeros((64, T), np.float32), sin]))
    key = np.arange(P)[:, None, None] + P * np.arange(NT)[None, :, None]
    put(b, CONST_B, "before", (key < k) * 1.0)
    put(b, CONST_B, "causal", causal)
    dilated = [np.where((k <= q) & (q - k <= window) & ((q - k) % dil == 0), 0.0, NEG)
               for window, dil in ((128, 1), (512, 4), (2048, 16))]
    put(b, CONST_B, "dilated", np.stack(dilated, 1))
    return a, b


class Ring:

    def __init__(self, banks, full, empty):
        self.banks, self.full, self.empty = banks, full, empty
        self.filled = self.taken = 0

    def fill(self, pe):
        n = self.filled
        if n >= len(self.banks):
            pe.wait_ge(self.empty, n - len(self.banks) + 1)
        self.filled += 1
        return self.banks[n % len(self.banks)]

    def take(self, eng):
        self.taken += 1
        eng.wait_ge(self.full, self.taken)
        return self.banks[(self.taken - 1) % len(self.banks)]


class Count:

    def __init__(self):
        self.of = {}

    def __call__(self, sem):
        self.of[sem.name] = self.of.get(sem.name, 0) + 1
        return self.of[sem.name]


class Arena:

    def __init__(self, tensor, at=0):
        self.tensor, self.at, self.most = tensor, at, at

    def take(self, *shape):
        n = int(np.prod(shape))
        v = self.tensor[:, self.at:self.at + n]
        self.at += n
        self.most = max(self.most, self.at)
        if len(shape) == 2:
            v = v.rearrange("p (a b) -> p a b", a=shape[0])
        if len(shape) == 3:
            v = v.rearrange("p (a b c) -> p a b c", a=shape[0], b=shape[1])
        return v


def over_last(ap, n):
    return ap.unsqueeze(len(ap.shape)).to_broadcast([*ap.shape, n])


def over_mid(ap, n):
    return ap.unsqueeze(1).to_broadcast([ap.shape[0], n, ap.shape[1]])


def build_program(nc, a):
    ctx = ExitStack()
    with ctx:
        def sem(name):
            return ctx.enter_context(nc.semaphore(name))

        def sb(name, n):
            return ctx.enter_context(nc.sbuf_tensor(name, [P, n], F32))

        slots = [sb(f"weights{i}", SLOT) for i in range(NSLOT)]
        x_t = sb("x", NT * D)
        xT_t = sb("xT", KD * T)
        const_t = sb("const", max(WIDTH_CA, WIDTH_CB))
        param_t = sb("param", max(WIDTH_PA, WIDTH_PB))
        ones_t = sb("ones", P)
        small_t = sb("small", 1024)
        work_t = sb("work", 25100)
        x = x_t[:, :].rearrange("p (t d) -> p t d", t=NT)
        xT = xT_t[:, :].rearrange("p (k t) -> p k t", k=KD)
        ones = ones_t[:, :]

        vbanks = [ctx.enter_context(nc.psum_tensor(f"to_vector{i}", [P, 512], F32))[:, :] for i in range(4)]
        sbanks = [ctx.enter_context(nc.psum_tensor(f"to_scalar{i}", [P, 512], F32))[:, :] for i in range(4)]
        vring = Ring(vbanks, sem("vector_bank_full"), sem("vector_bank_empty"))
        sring = Ring(sbanks, sem("scalar_bank_full"), sem("scalar_bank_empty"))

        const_in, param_in, x_in = sem("const_in"), sem("param_in"), sem("x_in")
        norms_in, out_done = sem("ln_rows_in"), sem("out_done")
        weights_in = [sem(f"weights{i}_in") for i in range(NSLOT)]
        slot_used = sem("slot_used")
        vector_step, scalar_step, gpsimd_step = sem("vector_step"), sem("scalar_step"), sem("gpsimd_step")
        sem_attention_inputs = sem("attention_inputs")
        sem_beta_exps = sem("beta_exps")
        sem_beta_inputs = sem("beta_inputs")
        sem_branches_ready = sem("branches_ready")
        sem_centred = sem("centred")
        sem_conv_in = sem("conv_in")
        sem_convolved = sem("convolved")
        sem_decay_logs = sem("decay_logs")
        sem_decays = sem("decays")
        sem_dens = sem("dens")
        sem_dil_raw = sem("dil_raw")
        sem_dn_normed1 = sem("dn_normed1")
        sem_dn_qk_normed = sem("dn_qk_normed")
        sem_dn_rstd = sem("dn_rstd")
        sem_dn_squares = sem("dn_squares")
        sem_exped = sem("exped")
        sem_forget_exps = sem("forget_exps")
        sem_forget_inputs = sem("forget_inputs")
        sem_forget_rows = sem("forget_rows")
        sem_g_ready = sem("g_ready")
        sem_g_rows = sem("g_rows")
        sem_gate_sigmoid = sem("gate_sigmoid")
        sem_gate_used = sem("gate_used")
        sem_gc_exps = sem("gc_exps")
        sem_gc_ready = sem("gc_ready")
        sem_group_exps = sem("group_exps")
        sem_group_shifted = sem("group_shifted")
        sem_head_normed = sem("head_normed")
        sem_head_rstd = sem("head_rstd")
        sem_head_squares = sem("head_squares")
        sem_head_turned = sem("head_turned")
        sem_hidden_ready = sem("hidden_ready")
        sem_hidden_silu = sem("hidden_silu")
        sem_hidden_used = sem("hidden_used")
        sem_index_dots = sem("index_dots")
        sem_index_raw = sem("index_raw")
        sem_index_ready = sem("index_ready")
        sem_inverse_ready = sem("inverse_ready")
        sem_inverse_started = sem("inverse_started")
        sem_layer_out = sem("layer_out")
        sem_ln_rstd = sem("ln_rstd")
        sem_log_dens = sem("log_dens")
        sem_log_keep = sem("log_keep")
        sem_logf_ready = sem("logf_ready")
        sem_logf_rows = sem("logf_rows")
        sem_lora_normed = sem("lora_normed")
        sem_lora_rstd = sem("lora_rstd")
        sem_lora_squares = sem("lora_squares")
        sem_merged_ready = sem("merged_ready")
        sem_mix_exps = sem("mix_exps")
        sem_mix_shifted = sem("mix_shifted")
        sem_mla_raw = sem("mla_raw")
        sem_o_all = sem("o_all")
        sem_o_ready_b = sem("o_ready_b")
        sem_o_rstd = sem("o_rstd")
        sem_o_rstd_b = sem("o_rstd_b")
        sem_o_scaled = sem("o_scaled")
        sem_o_squares = sem("o_squares")
        sem_o_squares_b = sem("o_squares_b")
        sem_off_block = sem("off_block")
        sem_off_times_T = sem("off_times_T")
        sem_ones_ready = sem("ones_ready")
        sem_pair_exps = sem("pair_exps")
        sem_pair_shifted = sem("pair_shifted")
        sem_pool_in = sem("pool_in")
        sem_pooled = sem("pooled")
        sem_prob_free = sem("prob_free")
        sem_probs_ready = sem("probs_ready")
        sem_probs_turned = sem("probs_turned")
        sem_qk_ready = sem("qk_ready")
        sem_scored = sem("scored")
        sem_shifted = sem("shifted")
        sem_state_ready = sem("state_ready")
        sem_stick_exp = sem("stick_exp")
        sem_stick_logs = sem("stick_logs")
        sem_stick_sum = sem("stick_sum")
        sem_stick_weights = sem("stick_weights")
        sem_u_w_ready = sem("u_w_ready")
        sem_v_new = sem("v_new")
        sem_xT_ready = sem("xT_ready")
        sem_x_normed = sem("x_normed")
        sem_x_scaled = sem("x_scaled")
        sem_y_pooled = sem("y_pooled")
        sem_z_ready = sem("z_ready")

        def cols(w, l, lo, n, at=0, rows=KD):
            src = w[l, :, lo:lo + n].rearrange("(k p) n -> p k n", p=P)
            return (at, rows, n, src)

        loads = []
        for l in range(DEPTH):
            wa = a["w_in"]
            loads.append([cols(wa, l, A_IQ, 324), cols(wa, l, A_BA, 8, 324)])
            for lo in (A_QC, A_KC, A_VC, A_ZC, A_UB, A_ZB, A_QKV, A_QKV + 512, A_QKV + 1024, A_ZA):
                loads.append([cols(wa, l, lo, 512)])
            for n in range(3):
                loads.append([cols(wa, l, A_GATE + n * D, 512)])
                loads.append([(0, 4, D, a["w_branch"][l, n].rearrange("(k p) d -> p k d", p=P))])
                loads.append([cols(wa, l, A_GATE + n * D + 512, 512)])
            for c in range(2):
                loads.append([cols(a["w_out"], l, c * 512, 512)])
        for l in range(DEPTH):
            wb = a["w_in_2"]
            for lo, n in ((B_SBQK, 512), (B_SBV, 512), (B_FOXK, 512), (B_F, 420), (B_DQ, 512), (B_DQ + 512, 512),
                          (B_DK + 256, 512), (B_DV, 512), (B_DV + 512, 256)):
                loads.append([cols(wb, l, lo, n)])
            for c in range(2):
                loads.append([cols(a["w_out_2"], l, c * 512, 512)])
            for e in range(EXPERTS):
                loads.append([(0, KD, 512, a["w1_2"][l, e].rearrange("(k p) n -> p k n", p=P))])
                loads.append([(0, KD, 512, a["w3_2"][l, e].rearrange("(k p) n -> p k n", p=P))])
                loads.append([(0, 4, D, a["w2_2"][l, e].rearrange("(k p) n -> p k n", p=P))])

        def width(parts):
            return sum(n for _, _, n, _ in parts)

        arrived, per_slot = [], [0] * NSLOT
        for i, parts in enumerate(loads):
            per_slot[i % NSLOT] += len(parts)
            arrived.append(per_slot[i % NSLOT])

        def slot_view(i):
            parts = loads[i]
            rows = parts[0][1]
            w = width(parts)
            return slots[i % NSLOT][:, 0:rows * w].rearrange("p (k n) -> p k n", k=rows)

        def ca(name, rows=P):
            lo, hi = CONST_A[name]
            return const_t[0:rows, lo:hi]

        def cb(name, rows=P):
            lo, hi = CONST_B[name]
            return const_t[0:rows, lo:hi]

        def pa(name):
            lo, hi = PARAM_A[name]
            return param_t[:, lo:hi]

        def pb(name):
            lo, hi = PARAM_B[name]
            return param_t[:, lo:hi]

        sm = Arena(small_t)
        eps = sm.take(1)
        eps5 = sm.take(1)
        stat = sm.take(NT)
        rstd = sm.take(NT)
        mean = sm.take(NT)
        ba = sm.take(NT, 12)
        beta = sm.take(NT * H)
        g = sm.take(NT * H)
        exp_a = sm.take(H)
        tmp8 = sm.take(4, NT * H)
        gc = sm.take(NT, 8)
        kb_scale = sm.take(NT * H)
        kd_scale = sm.take(NT * H)
        wi = sm.take(NT, H)
        best = sm.take(8)
        rowmax = sm.take(12)
        rowsum = sm.take(12)
        lse = sm.take(12)
        mixw = sm.take(12)
        mix1 = sm.take(H)
        mix2 = sm.take(H)
        logf = sm.take(NT, H)
        cq_tok = sm.take(NT, H)
        router = sm.take(NT, 20)
        rt = sm.take(16, 16)
        gates = sm.take(NT, EXPERTS)

        wk = Arena(work_t)
        y = wk.take(3, H, T)
        silu_z = wk.take(H, T)
        s12_at = wk.at
        s1, s2, s3, s4 = (wk.take(H, T) for _ in range(4))
        scaled_x = work_t[:, s12_at:s12_at + NT * D].rearrange("p (t d) -> p t d", t=NT)
        phase = wk.at
        qa_, ka_ = wk.take(H, T), wk.take(H, T)
        va_ = wk.take(NT, 512)
        idx_raw, idx = wk.take(5, T), wk.take(5, T)
        score, sel = wk.take(T), wk.take(NT, T)
        logit = wk.take(H, T)
        pT = wk.take(NT, 512)
        wk.at = phase + 12000
        pool_u, pool_1, pool_2 = (wk.take(4, PAD + T) for _ in range(3))
        wk.at = phase
        qkv = wk.take(12, T)
        conv_in = wk.take(12, T + CONV - 1)
        wk.at = phase + 12 * T
        kbe, kdec, vbeta, attnT, qe, expg, TT, Tm, X, U, DT = (wk.take(NT, 512) for _ in range(11))
        vnew, state = wk.take(H, P), wk.take(H, P)
        oT = wk.take(H, T)
        wk.at = phase
        merged = wk.take(KD, T)
        msig = wk.take(2, T)
        most_a = wk.most

        wb_ = Arena(work_t)
        ln_rows = wb_.take(4, D)
        oall = wb_.take(8, T)
        phase_b = wb_.at
        sbqk, foxq, foxk = wb_.take(4, T), wb_.take(2, T), wb_.take(2, T)
        dq, dk = wb_.take(6, T), wb_.take(6, T)
        mq, mk = wb_.take(4, T), wb_.take(4, T)
        sbv, foxv, mv, dv = wb_.take(NT, 256), wb_.take(NT, 256), wb_.take(NT, 256), wb_.take(NT, 768)
        cdiff = wb_.take(H, T)
        big = wb_.at
        prob = wb_.take(12, T)
        pTb = wb_.take(NT, 512)
        b1, b2 = wb_.take(4, T), wb_.take(4, T)
        wb_.at = big
        sz, sp, slk = wb_.take(8, T), wb_.take(8, T), wb_.take(8, T)
        crs8, sq8 = sp, slk
        f_row = b1.rearrange("p h (t c) -> p (h t) c", t=2).rearrange("p (t h) c -> p t h c", t=NT)
        wb_.at = big
        cqkv = wb_.take(3, T)
        csq = wb_.take(3, T)
        crs = wb_.take(3, T)
        wb_.at = phase_b
        ymoe = wb_.take(NT, D)
        hh = [wb_.take(4, T) for _ in range(2)]
        xc = wb_.take(NT, D)
        sq_scr = wb_.take(D)
        assert max(most_a, wb_.most) <= 25100 and sm.most <= 1024, (most_a, wb_.most, sm.most)

        block = ctx.enter_context(nc.Block())

        @block.sync
        def _(sp_):
            sp_.dma_start(x_t[:, :].rearrange("p (t d) -> p t d", t=NT),
                          a["x"][0].rearrange("(t p) d -> p t d", p=P)).then_inc(x_in, 16)
            at = 0
            for i, parts in enumerate(loads):
                if i >= NSLOT:
                    sp_.wait_ge(slot_used, i - NSLOT + 1)
                w = width(parts)
                for off, rows, n, src in parts:
                    dst = slots[i % NSLOT][:, 0:rows * w].rearrange("p (k n) -> p k n", k=rows)[:, :, off:off + n]
                    sp_.dma_start(dst, src).then_inc(weights_in[i % NSLOT], 16)
            sp_.wait_ge(sem_layer_out, 2 * DEPTH)
            sp_.dma_start(a["out"][0].rearrange("(t p) d -> p t d", p=P), x).then_inc(out_done, 16)
            sp_.wait_ge(out_done, 16)

        @block.gpsimd
        def _(pool):
            c = Count()
            for l in range(2 * DEPTH):
                if l:
                    pool.wait_ge(sem_layer_out, l)
                if l == 0:
                    pool.dma_start(const_t[:, 0:WIDTH_CA], a["const_a"]).then_inc(const_in, 16)
                if l == DEPTH:
                    pool.dma_start(const_t[:, 0:WIDTH_CB], a["const_b"]).then_inc(const_in, 16)
                if l < DEPTH:
                    pool.dma_start(param_t[:, 0:WIDTH_PA], a["param_a"][l]).then_inc(param_in, 16)
                    pool.memset(pool_1[:, :, 0:PAD], 0.0).then_inc(gpsimd_step, 1)
                    pool.wait_ge(gpsimd_step, c(gpsimd_step))
                    pool.memset(pool_2[:, :, 0:PAD], 0.0).then_inc(gpsimd_step, 1)
                    pool.wait_ge(gpsimd_step, c(gpsimd_step))
                    pool.wait_ge(const_in, 16)
                    pool.wait_ge(sem_pool_in, c(sem_pool_in))
                    src, dst = pool_u, pool_1
                    for i, w in enumerate(WINDOWS):
                        s = w // 2
                        pool.tensor_tensor(dst[:, i:4, PAD:PAD + T], src[:, i:4, PAD:PAD + T],
                                           src[:, i:4, PAD - s:PAD - s + T], ALU.add).then_inc(gpsimd_step, 1)
                        pool.wait_ge(gpsimd_step, c(gpsimd_step))
                        src, dst = dst, (pool_2 if dst is pool_1 else pool_1)
                    for i in range(4):
                        s = (pool_1, pool_2)[i % 2]
                        pool.tensor_tensor(s3[:, i, :], s[:, i, PAD:PAD + T],
                                           ca("count").rearrange("p (g t) -> p g t", g=4)[:, i, :], ALU.mult).then_inc(gpsimd_step, 1)
                        pool.wait_ge(gpsimd_step, c(gpsimd_step))
                    pool.tensor_tensor(s3, s3, pool_u[:, :, PAD:PAD + T], ALU.subtract).then_inc(sem_pooled, 1)
                    pool.wait_ge(sem_pooled, c(sem_pooled))
                else:
                    pool.dma_start(param_t[:, 0:WIDTH_PB], a["param_b"][l - DEPTH]).then_inc(param_in, 16)
                    for i, name in enumerate(("ln1_g_2", "ln1_b_2", "ln2_g_2", "ln2_b_2")):
                        pool.dma_start(ln_rows[:, i, :], a[name][l - DEPTH].partition_broadcast(P)).then_inc(norms_in, 16)

        @block.tensor
        def _(pe):
            c = Count()
            release = [0]
            nload = [0]

            def mm(out, lhsT, rhs, start=True, stop=True, inc=None):
                ins = nc.tensor.matmul(out, lhsT, rhs, start=start, stop=stop)
                if inc is not None:
                    ins.then_inc(inc, 1)
                elif release[0]:
                    ins.then_inc(slot_used, 1)
                    release[0] -= 1

            def tr(out, in_, ident, inc=None):
                ins = nc.tensor.transpose(out, in_, ident)
                if inc is not None:
                    ins.then_inc(inc, 1)

            def weights():
                i = nload[0]
                nload[0] += 1
                pe.wait_ge(weights_in[i % NSLOT], 16 * arrived[i])
                return slot_view(i)

            def used():
                release[0] += 1

            def channels(ring, w, tiles, m=P, rhs=None):
                for j in range(0, len(tiles), 2):
                    bank = ring.fill(pe)
                    pair = tiles[j:j + 2]
                    for i, lo in enumerate(pair):
                        for k in range(KD):
                            mm(bank[0:m, i * T:(i + 1) * T], w[:, k, lo:lo + m], xT[:, k, :], k == 0, k == KD - 1,
                               ring.full if i == len(pair) - 1 and k == KD - 1 else None)

            def tokens(ring, w, lo, n):
                per = 512 // n
                for t in range(NT):
                    if t % per == 0:
                        bank = ring.fill(pe)
                    for k in range(KD):
                        mm(bank[:, (t % per) * n:(t % per + 1) * n], xT[:, k, t * P:(t + 1) * P], w[:, k, lo:lo + n],
                           k == 0, k == KD - 1, ring.full if (t % per == per - 1 or t == NT - 1) and k == KD - 1 else None)

            def heads(ring, fn, n=H, size=P, rows=P):
                bank = ring.fill(pe)
                for h in range(n):
                    pairs = fn(h)
                    for i, (lhsT, rhs) in enumerate(pairs):
                        mm(bank[0:rows, h * size:h * size + rhs.shape[-1]], lhsT, rhs, i == 0, i == len(pairs) - 1,
                           ring.full if h == n - 1 and i == len(pairs) - 1 else None)

            def column_sums(ring, sq, matrix=None, parts=2):
                for j in range(parts):
                    bank = ring.fill(pe)
                    mm(bank, ones if matrix is None else matrix, sq[:, 2 * j:2 * j + 2, :].rearrange("p a b -> p (a b)"),
                       inc=ring.full)

            def transposed(src, ident):
                for t in range(NT):
                    for j in range(2):
                        bank = vring.fill(pe)
                        for i in range(4):
                            k = 4 * j + i
                            tr(bank[:, i * P:(i + 1) * P], src[:, t, k * P:(k + 1) * P], ident,
                               vring.full if i == 3 else None)

            def attention_scores(t, q_of, k_of):
                nk = (t + 1) * P
                for r in range(2):
                    bank = vring.fill(pe)
                    for h in (r, r + 2):
                        mm(bank[:, (h - r) * P:(h - r) * P + nk], q_of(h)[:, t * P:(t + 1) * P], k_of(h)[:, 0:nk],
                           inc=vring.full if h == r + 2 else None)

            def attention_turn(t, p_of, ident):
                for kt in range(t + 1):
                    bank = sring.fill(pe)
                    for h in range(H):
                        tr(bank[:, h * P:(h + 1) * P], p_of(h)[:, kt * P:(kt + 1) * P], ident,
                           sring.full if h == H - 1 else None)

            pe.wait_ge(sem_ones_ready, 1)
            for l in range(DEPTH):
                ident = ca("ident")
                if l == 0:
                    pe.wait_ge(const_in, 16)
                pe.wait_ge(param_in, 16 * (l + 1))
                pe.wait_ge(sem_x_scaled, c(sem_x_scaled))
                transposed(scaled_x, ident)
                pe.wait_ge(sem_xT_ready, c(sem_xT_ready))
                w = weights()
                channels(sring, w, [0, 64, 128, 192, 256], 64)
                tokens(vring, w, 320, 12)
                used()
                pe.wait_ge(sem_index_raw, c(sem_index_raw))
                for j in (0, 2, 4):
                    bank = vring.fill(pe)
                    n = min(2, 5 - j)
                    mm(bank[0:64, 0:n * T], ca("rot_index", 64)[:, 0:64],
                       idx_raw[0:64, j:j + n, :].rearrange("p a b -> p (a b)"), inc=vring.full)
                for i in range(2):
                    w = weights()
                    channels(sring, w, [0, 128, 256, 384])
                    used()
                    pe.wait_ge(sem_head_squares, c(sem_head_squares))
                    column_sums(sring, s1)
                    pe.wait_ge(sem_head_normed, c(sem_head_normed))
                    for j in (0, 2):
                        bank = vring.fill(pe)
                        mm(bank, ca("rot_head"), s3[:, j:j + 2, :].rearrange("p a b -> p (a b)"), inc=vring.full)
                w = weights()
                tokens(sring, w, 0, 512)
                used()
                w = weights()
                channels(sring, w, [0, 128, 256, 384])
                used()
                pe.wait_ge(sem_index_ready, c(sem_index_ready))
                for t in range(NT):
                    for h0 in (0, 2):
                        bank = sring.fill(pe)
                        for h in (h0, h0 + 1):
                            mm(bank[:, (h - h0) * T:(h - h0) * T + (t + 1) * P], idx[0:64, h, t * P:(t + 1) * P],
                               idx[0:64, 4, 0:(t + 1) * P], inc=sring.full if h == h0 + 1 else None)
                pe.wait_ge(sem_qk_ready, c(sem_qk_ready))
                for t in range(NT):
                    attention_scores(t, lambda h: qa_[:, h, :], lambda h: ka_[:, h, :])
                    pe.wait_ge(sem_probs_ready, c(sem_probs_ready))
                    attention_turn(t, lambda h: logit[:, h, :], ident)
                    pe.wait_ge(sem_probs_turned, c(sem_probs_turned))
                    heads(vring, lambda h: [(va_[:, kt, h * P:(h + 1) * P], pT[:, kt, h * P:(h + 1) * P])
                                            for kt in range(t + 1)])
                w = weights()
                channels(sring, w, [0, 128, 256, 384])
                used()
                w = weights()
                channels(sring, w, [0, 128, 256, 384])
                used()
                pe.wait_ge(sem_pooled, c(sem_pooled))
                for j in (0, 2):
                    bank = vring.fill(pe)
                    for i in (j, j + 1):
                        mm(bank[:, (i - j) * T:(i - j + 1) * T], pa("pool_w")[:, i * P:(i + 1) * P], s3[:, i, :],
                           inc=vring.full if i == j + 1 else None)
                for i in range(3):
                    w = weights()
                    channels(sring, w, [0, 128, 256, 384])
                    used()
                for i in range(2):
                    pe.wait_ge(sem_dn_squares, c(sem_dn_squares))
                    column_sums(sring, s1)
                w = weights()
                channels(sring, w, [0, 128, 256, 384])
                used()
                pe.wait_ge(sem_g_ready, c(sem_g_ready))
                bank = vring.fill(pe)
                for t in range(NT):
                    for j, m in enumerate(("cumsum", "chunk")):
                        mm(bank[:, t * 8 + j * 4:t * 8 + j * 4 + 4], ca(m), g[:, t * H:(t + 1) * H],
                           inc=vring.full if t == NT - 1 and j == 1 else None)
                pe.wait_ge(sem_g_rows, c(sem_g_rows))
                g_row = s3.rearrange("p a b -> p (a b)")
                beta_row = s4.rearrange("p a b -> p (a b)")

                def tile_of(v, t, h):
                    return v[:, h, t * P:(t + 1) * P]
                for t in range(NT):
                    heads(vring, lambda h: [(g_row[:, (t * H + h) * P:(t * H + h + 1) * P], ca("cumsum"))])
                pe.wait_ge(sem_dn_qk_normed, c(sem_dn_qk_normed))
                for t in range(NT):
                    for v in (4, 8):
                        bank = vring.fill(pe)
                        for h in range(H):
                            tr(bank[:, h * P:(h + 1) * P], qkv[:, v + h, t * P:(t + 1) * P], ident,
                               vring.full if h == H - 1 else None)
                for t in range(NT):
                    heads(vring, lambda h: [(qkv[:, 4 + h, t * P:(t + 1) * P], qkv[:, 4 + h, t * P:(t + 1) * P])])
                    heads(vring, lambda h: [(beta_row[:, (t * H + h) * P:(t * H + h + 1) * P], ident)])
                    heads(vring, lambda h: [(qkv[:, 4 + h, t * P:(t + 1) * P], qkv[:, h, t * P:(t + 1) * P])])
                pe.wait_ge(sem_inverse_started, c(sem_inverse_started))
                for t in range(NT):
                    bank = vring.fill(pe)
                    for h in range(H):
                        tr(bank[:, h * P:(h + 1) * P], TT[:, t, h * P:(h + 1) * P], ident, vring.full if h == H - 1 else None)
                for s in range(1, 6):
                    pe.wait_ge(sem_off_block, c(sem_off_block))
                    for t in range(NT):
                        heads(sring, lambda h: [(DT[:, t, h * P:(h + 1) * P], Tm[:, t, h * P:(h + 1) * P])])
                    for t in range(NT):
                        pe.wait_ge(sem_off_times_T, c(sem_off_times_T))
                        heads(vring, lambda h: [(TT[:, t, h * P:(h + 1) * P], X[:, t, h * P:(h + 1) * P])])
                        heads(vring, lambda h: [(X[:, t, h * P:(h + 1) * P], TT[:, t, h * P:(h + 1) * P])])
                pe.wait_ge(sem_inverse_ready, c(sem_inverse_ready))
                for t in range(NT):
                    heads(sring, lambda h: [(TT[:, t, h * P:(h + 1) * P], vbeta[:, t, h * P:(h + 1) * P])])
                    heads(sring, lambda h: [(kbe[:, t, h * P:(h + 1) * P], TT[:, t, h * P:(h + 1) * P])])
                pe.wait_ge(sem_u_w_ready, c(sem_u_w_ready))
                for n in range(T // CHUNK):
                    t, r = n // 2, CHUNK * (n % 2)
                    if n:
                        pe.wait_ge(sem_state_ready, c(sem_state_ready))
                        heads(vring, lambda h: [(X[:, t, h * P:(h + 1) * P], state[:, h, :])])
                    pe.wait_ge(sem_v_new, c(sem_v_new))
                    rows = slice(r, r + CHUNK)

                    def o_parts(h):
                        first = [(state[:, h, :], qe[:, t, h * P + r:h * P + r + CHUNK])] if n else []
                        return first + [(vnew[rows, h, :], attnT[rows, t, h * P + r:h * P + r + CHUNK])]
                    heads(sring, o_parts, size=CHUNK)
                    if n < T // CHUNK - 1:
                        heads(vring, lambda h: [(kdec[rows, t, h * P:(h + 1) * P], vnew[rows, h, :])])
                pe.wait_ge(sem_o_squares, c(sem_o_squares))
                column_sums(sring, s1)
                pe.wait_ge(sem_branches_ready, c(sem_branches_ready))
                for n in range(3):
                    for m in range(KD):
                        if m % 4 == 0:
                            wg = weights()
                        bank = sring.fill(pe)
                        for k in range(KD):
                            mm(bank[:, 0:T], wg[:, k, (m % 4) * P:(m % 4 + 1) * P], xT[:, k, :], k == 0, k == KD - 1,
                               sring.full if k == KD - 1 else None)
                        if m == 0:
                            wbr = weights()
                        if m == 3:
                            used()
                        bank = vring.fill(pe)
                        for k in range(4):
                            mm(bank[:, 0:T], wbr[:, k, m * P:(m + 1) * P], y[:, n, k, :], k == 0, k == 3,
                               vring.full if k == 3 else None)
                    used()
                    used()
                pe.wait_ge(sem_merged_ready, c(sem_merged_ready))
                for cc in range(2):
                    w = weights()
                    for t in range(NT):
                        bank = vring.fill(pe)
                        for k in range(KD):
                            mm(bank, merged[:, k, t * P:(t + 1) * P], w[:, k, :], k == 0, k == KD - 1,
                               vring.full if k == KD - 1 else None)
                    used()

            for l in range(DEPTH):
                ident = cb("ident")
                if l == 0:
                    pe.wait_ge(const_in, 32)
                pe.wait_ge(param_in, 16 * (DEPTH + l + 1))
                pe.wait_ge(sem_layer_out, DEPTH + l)
                transposed(x, ident)
                pe.wait_ge(sem_xT_ready, c(sem_xT_ready))
                w = weights()
                channels(sring, w, [0, 128, 256, 384])
                used()
                w = weights()
                tokens(sring, w, 0, 256)
                channels(sring, w, [256, 384])
                used()
                w = weights()
                channels(sring, w, [0, 128])
                tokens(sring, w, 256, 256)
                used()
                w = weights()
                tokens(vring, w, 0, 4)
                channels(sring, w, [4, 132, 260])
                channels(sring, w, [420 - 96], 96)
                used()
                pe.wait_ge(sem_lora_squares, c(sem_lora_squares))
                bank = sring.fill(pe)
                for i in range(2):
                    mm(bank[:, 0:T], ones, csq[:, i, :], i == 0, i == 1)
                mm(bank[:, T:2 * T], ones, csq[:, 2, :], inc=sring.full)
                pe.wait_ge(sem_lora_normed, c(sem_lora_normed))
                wuq = pb("w_uq").rearrange("p (k n) -> p k n", k=2)
                wukv = pb("w_ukv").rearrange("p (h n) -> p h n", h=H)
                for h0 in (0, 2):
                    heads(sring, lambda h: [(wuq[:, k, (h0 + h) * 96:(h0 + h + 1) * 96], cqkv[:, k, :]) for k in range(2)],
                          2, T, 96)
                for h0 in (0, 2):
                    heads(sring, lambda h: [(wukv[:, h0 + h, 0:64], cqkv[:, 2, :])], 2, T, 64)
                bank = sring.fill(pe)
                for t in range(NT):
                    for h in range(H):
                        mm(bank[:, t * 256 + h * 64:t * 256 + h * 64 + 64], cqkv[:, 2, t * P:(t + 1) * P], wukv[:, h, 64:128],
                           inc=sring.full if t == NT - 1 and h == H - 1 else None)
                for v in (mq, mk):
                    pe.wait_ge(sem_mla_raw, c(sem_mla_raw))
                    for j in (0, 2):
                        bank = vring.fill(pe)
                        mm(bank[0:96, :], cb("rot_mla", 96)[:, 0:96],
                           v[0:96, j:j + 2, :].rearrange("p a b -> p (a b)"), inc=vring.full)
                w = weights()
                channels(sring, w, [0, 128, 256, 384])
                used()
                w = weights()
                channels(sring, w, [0, 128, 256, 384])
                used()
                w = weights()
                channels(sring, w, [0, 128, 256, 384])
                used()
                pe.wait_ge(sem_dil_raw, c(sem_dil_raw))
                for v in (dq, dk):
                    for j in (0, 2, 4):
                        bank = vring.fill(pe)
                        mm(bank, cb("rot64"), v[:, j:j + 2, :].rearrange("p a b -> p (a b)"), inc=vring.full)
                w = weights()
                tokens(sring, w, 0, 512)
                used()
                w = weights()
                tokens(sring, w, 0, 256)
                used()
                pe.wait_ge(sem_logf_ready, c(sem_logf_ready))
                bank = vring.fill(pe)
                mm(bank[:, 0:H], cb("upto"), logf[:, 0, :])
                mm(bank[:, H:2 * H], ones, logf[:, 0, :], True, False)
                mm(bank[:, H:2 * H], cb("upto"), logf[:, 1, :], False, True, vring.full)
                pe.wait_ge(sem_logf_rows, c(sem_logf_rows))
                for h0 in (0, 2):
                    bank = sring.fill(pe)
                    for h in (h0, h0 + 1):
                        o = (h - h0) * T
                        mm(bank[:, o:o + P], f_row[:, 0, h, :], cb("upto"))
                        mm(bank[:, o + P:o + T], f_row[:, 0, h, :], ones, True, False)
                        mm(bank[:, o + P:o + T], f_row[:, 1, h, :], cb("upto"), False, True,
                           sring.full if h == h0 + 1 else None)

                def halves(v, at=0):
                    return lambda h: v[64 * (h % 2):64 * (h % 2) + 64, at + h // 2, :]

                pe.wait_ge(sem_attention_inputs, c(sem_attention_inputs))
                for group in ("fox", "mla"):
                    for t in range(NT):
                        if group == "fox":
                            attention_scores(t, halves(foxq), halves(foxk))
                        else:
                            attention_scores(t, lambda h: mq[0:96, h, :], lambda h: mk[0:96, h, :])
                        pe.wait_ge(sem_probs_ready, c(sem_probs_ready))
                        attention_turn(t, lambda h: prob[:, h, :], ident)
                        pe.wait_ge(sem_probs_turned, c(sem_probs_turned))
                        v = foxv if group == "fox" else mv
                        heads(vring, lambda h: [(v[:, kt, (h // 2) * P:(h // 2 + 1) * P], pTb[:, kt, h * P:(h + 1) * P])
                                                for kt in range(t + 1)])
                for t in range(NT):
                    for br in range(3):
                        attention_scores(t, halves(dq, 2 * br), halves(dk, 2 * br))
                    pe.wait_ge(sem_probs_ready, c(sem_probs_ready))
                    for br in range(3):
                        attention_turn(t, lambda h: prob[:, 4 * br + h, :], ident)
                        pe.wait_ge(sem_probs_turned, c(sem_probs_turned))
                        heads(vring, lambda h: [(dv[:, kt, br * 256 + (h // 2) * P:br * 256 + (h // 2 + 1) * P],
                                                 pTb[:, kt, h * P:(h + 1) * P]) for kt in range(t + 1)])
                for kt in range(NT):
                    for r in range(2):
                        heads(sring, lambda h: [(halves(sbqk, 2)(r + 2 * h)[:, kt * P:(kt + 1) * P], halves(sbqk)(r + 2 * h))],
                              2, T)
                pe.wait_ge(sem_log_keep, c(sem_log_keep))
                for kt in range(NT):
                    for h0 in (0, 2):
                        heads(vring, lambda h: [(cb("after"), slk[:, kt * 4 + h0 + h, :])]
                              + ([(ones, slk[:, 4 + h0 + h, :])] if kt == 0 else []), 2, T)
                pe.wait_ge(sem_stick_weights, c(sem_stick_weights))
                for h0 in (0, 2):
                    heads(vring, lambda h: [(sbv[:, kt, (h0 // 2) * P:(h0 // 2 + 1) * P], sz[:, kt * 4 + h0 + h, :])
                                            for kt in range(NT)], 2, T)
                pe.wait_ge(sem_o_squares_b, c(sem_o_squares_b))
                column_sums(sring, sq8, cb("pair"), 4)
                pe.wait_ge(sem_o_ready_b, c(sem_o_ready_b))
                for cc in range(2):
                    w = weights()
                    for t in range(NT):
                        bank = vring.fill(pe)
                        for k in range(KD):
                            mm(bank, oall[:, k, t * P:(t + 1) * P], w[:, k, :], k == 0, k == KD - 1,
                               vring.full if k == KD - 1 else None)
                    used()
                pe.wait_ge(sem_x_normed, c(sem_x_normed))
                transposed(x, ident)
                pe.wait_ge(sem_xT_ready, c(sem_xT_ready))
                bank = vring.fill(pe)
                wr = pb("w_router").rearrange("p (k n) -> p k n", k=KD)
                for t in range(NT):
                    for k in range(KD):
                        mm(bank[:, t * 20:(t + 1) * 20], xT[:, k, t * P:(t + 1) * P], wr[:, k, :], k == 0, k == KD - 1,
                           vring.full if t == NT - 1 and k == KD - 1 else None)
                w1 = weights()
                w3 = weights()
                for e in range(EXPERTS):
                    for m in range(4):
                        for ring, w in ((sring, w1), (vring, w3)):
                            bank = ring.fill(pe)
                            for k in range(KD):
                                mm(bank[:, 0:T], w[:, k, m * P:(m + 1) * P], xT[:, k, :], k == 0, k == KD - 1,
                                   ring.full if k == KD - 1 else None)
                    used()
                    used()
                    w2 = weights()
                    pe.wait_ge(sem_hidden_ready, c(sem_hidden_ready))
                    for t in range(NT):
                        for cc in range(2):
                            bank = vring.fill(pe)
                            for k in range(4):
                                mm(bank, hh[e % 2][:, k, t * P:(t + 1) * P], w2[:, k, cc * 512:(cc + 1) * 512], k == 0, k == 3,
                                   vring.full if k == 3 else None)
                    used()
                    if e + 1 < EXPERTS:
                        w1 = weights()
                        w3 = weights()

        @block.scalar
        def _(act):
            c = Count()
            A = nc.scalar.activation

            def move(dst, n=512, rows=P, scale=1.0, event=None):
                bank = sring.take(act)
                A(dst, bank[0:rows, 0:n].rearrange("p (a b) -> p a b", a=dst.shape[1]) if len(dst.shape) == 3
                  else bank[0:rows, 0:n], ACT.Copy, scale=scale).then_inc(sring.empty, 1)
                act.wait_ge(sring.empty, c(sring.empty))
                if event is not None:
                    act.sem_inc(event, 1)
                    c(event)

            def rsqrt_bank(dst, n=512, scale=1.0, bias=None, rows=P):
                bank = sring.take(act)
                A(dst, bank[0:rows, 0:n], ACT.Ln, scale=scale, bias=(eps if bias is None else bias)[0:rows]).then_inc(sring.empty, 1)
                act.wait_ge(sring.empty, c(sring.empty))
                A(dst, dst, ACT.Exp, scale=-0.5).then_inc(scalar_step, 1)
                act.wait_ge(scalar_step, c(scalar_step))

            def flat(v):
                return v.rearrange("p a b -> p (a b)")

            def tables(name):
                act.preload_act_table_set(name)

            def silu_z_in(dst):
                for j in (0, 2):
                    bank = sring.take(act)
                    A(flat(dst[:, j:j + 2, :]), bank, ACT.Silu).then_inc(sring.empty, 1)
                    act.wait_ge(sring.empty, c(sring.empty))
                act.sem_inc(sem_z_ready, 1)
                c(sem_z_ready)

            act.wait_ge(sem_ones_ready, 1)
            act.wait_ge(x_in, 16)
            for l in range(DEPTH):
                tables("natural_log_exp_and_others")
                for t in range(NT):
                    A(flat(s3), x[:, t, :], ACT.Square, accum_out=stat[:, t:t + 1]).then_inc(scalar_step, 1)
                    act.wait_ge(scalar_step, c(scalar_step))
                A(rstd, stat, ACT.Ln, scale=1.0 / D, bias=eps).then_inc(scalar_step, 1)
                act.wait_ge(scalar_step, c(scalar_step))
                A(rstd, rstd, ACT.Exp, scale=-0.5).then_inc(scalar_step, 1)
                act.wait_ge(scalar_step, c(scalar_step))
                sx = scaled_x
                A(sx[:, 0, :], x[:, 0, :], ACT.Copy, scale=rstd[:, 0:1]).then_inc(scalar_step, 1)
                act.wait_ge(scalar_step, c(scalar_step))
                A(sx[:, 1, :], x[:, 1, :], ACT.Copy, scale=rstd[:, 1:2]).then_inc(sem_x_scaled, 1)
                act.wait_ge(sem_x_scaled, c(sem_x_scaled))
                act.wait_ge(param_in, 16 * (l + 1))
                A(exp_a, pa("a_log"), ACT.Exp).then_inc(scalar_step, 1)
                act.wait_ge(scalar_step, c(scalar_step))
                for j in (0, 2, 4):
                    n = min(2, 5 - j)
                    bank = sring.take(act)
                    A(flat(idx_raw[0:64, j:j + n, :]), bank[0:64, 0:n * T], ACT.Copy).then_inc(sring.empty, 1)
                    act.wait_ge(sring.empty, c(sring.empty))
                act.sem_inc(sem_index_raw, 1)
                c(sem_index_raw)
                for i in range(2):
                    if i:
                        act.wait_ge(sem_head_turned, c(sem_head_turned))
                    for j in (0, 2):
                        move(s2[:, j:j + 2, :])
                    A(s1, s2, ACT.Square).then_inc(sem_head_squares, 1)
                    act.wait_ge(sem_head_squares, c(sem_head_squares))
                    for j in (0, 2):
                        rsqrt_bank(flat(s4[:, j:j + 2, :]), scale=1.0 / P)
                    act.sem_inc(sem_head_rstd, 1)
                    c(sem_head_rstd)
                for t in range(NT):
                    move(va_[:, t, :])
                act.wait_ge(sem_head_turned, c(sem_head_turned))
                tables("silu_and_others")
                silu_z_in(silu_z)
                tables("natural_log_exp_and_others")
                for t in range(NT):
                    if t:
                        act.wait_ge(sem_scored, c(sem_scored))
                    for j in (0, 2):
                        bank = sring.take(act)
                        nk = (t + 1) * P
                        A(s1[:, j:j + 2, 0:nk], bank.rearrange("p (a b) -> p a b", a=2)[:, :, 0:nk], ACT.Relu).then_inc(sring.empty, 1)
                        act.wait_ge(sring.empty, c(sring.empty))
                    act.sem_inc(sem_index_dots, 1)
                    c(sem_index_dots)
                for t in range(NT):
                    act.wait_ge(sem_shifted, c(sem_shifted))
                    A(logit[:, :, 0:(t + 1) * P], logit[:, :, 0:(t + 1) * P], ACT.Exp).then_inc(sem_exped, 1)
                    act.wait_ge(sem_exped, c(sem_exped))
                    for kt in range(t + 1):
                        move(pT[:, kt, :])
                    act.sem_inc(sem_probs_turned, 1)
                    c(sem_probs_turned)
                A(pool_u[:, :, 0:PAD], over_mid(ones[:, 0:PAD], 4), ACT.Copy, scale=0.0).then_inc(scalar_step, 1)
                act.wait_ge(scalar_step, c(scalar_step))
                for j in (0, 2):
                    move(pool_u[:, j:j + 2, PAD:PAD + T])
                act.sem_inc(sem_pool_in, 1)
                c(sem_pool_in)
                tables("silu_and_others")
                silu_z_in(s4)
                act.wait_ge(sem_y_pooled, c(sem_y_pooled))
                A(conv_in[:, :, 0:CONV - 1], over_mid(ones[:, 0:CONV - 1], 12), ACT.Copy, scale=0.0).then_inc(scalar_step, 1)
                act.wait_ge(scalar_step, c(scalar_step))
                for i in range(3):
                    for j in (0, 2):
                        move(conv_in[:, 4 * i + j:4 * i + j + 2, CONV - 1:CONV - 1 + T])
                    act.sem_inc(sem_conv_in, 1)
                    c(sem_conv_in)
                for i in range(3):
                    act.wait_ge(sem_convolved, c(sem_convolved))
                    A(qkv[:, 4 * i:4 * i + 4, :], qkv[:, 4 * i:4 * i + 4, :], ACT.Silu).then_inc(scalar_step, 1)
                    act.wait_ge(scalar_step, c(scalar_step))
                tables("natural_log_exp_and_others")
                for i in range(2):
                    A(s1, qkv[:, 4 * i:4 * i + 4, :], ACT.Square).then_inc(sem_dn_squares, 1)
                    act.wait_ge(sem_dn_squares, c(sem_dn_squares))
                    for j in (0, 2):
                        rsqrt_bank(flat(s2[:, j:j + 2, :]))
                    act.sem_inc(sem_dn_rstd, 1)
                    c(sem_dn_rstd)
                    act.wait_ge(sem_dn_normed1, c(sem_dn_normed1))
                tables("silu_and_others")
                silu_z_in(silu_z)
                tables("natural_log_exp_and_others")
                act.wait_ge(sem_beta_inputs, c(sem_beta_inputs))
                z8 = [tmp8[:, i, :] for i in range(4)]
                A(z8[0], z8[0], ACT.Exp, scale=-1.0).then_inc(scalar_step, 1)
                act.wait_ge(scalar_step, c(scalar_step))
                A(z8[2], z8[1], ACT.Abs).then_inc(scalar_step, 1)
                act.wait_ge(scalar_step, c(scalar_step))
                A(z8[2], z8[2], ACT.Exp, scale=-1.0).then_inc(scalar_step, 1)
                act.wait_ge(scalar_step, c(scalar_step))
                A(z8[2], z8[2], ACT.Ln, bias=ones[:, 0:1]).then_inc(sem_beta_exps, 1)
                act.wait_ge(sem_beta_exps, c(sem_beta_exps))
                act.wait_ge(sem_gc_ready, c(sem_gc_ready))
                A(kb_scale, kb_scale, ACT.Exp).then_inc(scalar_step, 1)
                act.wait_ge(scalar_step, c(scalar_step))
                A(kd_scale, kd_scale, ACT.Exp).then_inc(sem_gc_exps, 1)
                act.wait_ge(sem_gc_exps, c(sem_gc_exps))
                for t in range(NT):
                    act.wait_ge(sem_decay_logs, c(sem_decay_logs))
                    A(DT[:, t, :], DT[:, t, :], ACT.Exp).then_inc(scalar_step, 1)
                    act.wait_ge(scalar_step, c(scalar_step))
                    A(expg[:, t, :], expg[:, t, :], ACT.Exp).then_inc(sem_decays, 1)
                    act.wait_ge(sem_decays, c(sem_decays))
                for s in range(1, 6):
                    for t in range(NT):
                        move(X[:, t, :], event=sem_off_times_T)
                for t in range(NT):
                    move(Tm[:, t, :])
                    move(X[:, t, :])
                act.sem_inc(sem_u_w_ready, 1)
                c(sem_u_w_ready)
                for n in range(T // CHUNK):
                    bank = sring.take(act)
                    A(oT[:, :, n * CHUNK:(n + 1) * CHUNK], bank[:, 0:H * CHUNK].rearrange("p (a b) -> p a b", a=H),
                      ACT.Copy).then_inc(sring.empty, 1)
                    act.wait_ge(sring.empty, c(sring.empty))
                A(s1, oT, ACT.Square).then_inc(sem_o_squares, 1)
                act.wait_ge(sem_o_squares, c(sem_o_squares))
                for j in (0, 2):
                    rsqrt_bank(flat(s2[:, j:j + 2, :]), scale=1.0 / P)
                act.sem_inc(sem_o_rstd, 1)
                c(sem_o_rstd)
                tables("sigmoid_and_others")
                for n in range(3):
                    for m in range(KD):
                        i = n * KD + m
                        if i == 0:
                            act.wait_ge(sem_o_scaled, c(sem_o_scaled))
                        if i >= 2:
                            act.wait_ge(sem_gate_used, c(sem_gate_used))
                        bank = sring.take(act)
                        A(msig[:, i % 2, :], bank[:, 0:T], ACT.Sigmoid, bias=pa("gate_b")[:, i:i + 1]).then_inc(sring.empty, 1)
                        act.wait_ge(sring.empty, c(sring.empty))
                        act.sem_inc(sem_gate_sigmoid, 1)
                        c(sem_gate_sigmoid)
                for _ in range(2):
                    act.wait_ge(sem_gate_used, c(sem_gate_used))
                act.wait_ge(sem_layer_out, c(sem_layer_out))

            for l in range(DEPTH):
                tables("natural_log_exp_and_others")
                for j in (0, 2):
                    move(sbqk[:, j:j + 2, :])
                move(sbv)
                move(foxq)
                move(foxk)
                move(foxv)
                move(cqkv[:, 0:2, :])
                bank = sring.take(act)
                A(cqkv[:, 2, :], bank[:, 0:T], ACT.Copy).then_inc(sring.empty, 1)
                act.wait_ge(sring.empty, c(sring.empty))
                bank = sring.take(act)
                A(mk[64:96, :, :], bank[64:96, 0:T].unsqueeze(1).to_broadcast([32, H, T]), ACT.Copy).then_inc(sring.empty, 1)
                act.wait_ge(sring.empty, c(sring.empty))
                A(csq[:, 0:3, :], cqkv, ACT.Square).then_inc(sem_lora_squares, 1)
                act.wait_ge(sem_lora_squares, c(sem_lora_squares))
                bank = sring.take(act)
                A(crs[:, 0, :], bank[:, 0:T], ACT.Ln, scale=1.0 / 256, bias=eps).then_inc(scalar_step, 1)
                act.wait_ge(scalar_step, c(scalar_step))
                A(crs[:, 1, :], bank[:, T:2 * T], ACT.Ln, scale=1.0 / 128, bias=eps).then_inc(sring.empty, 1)
                act.wait_ge(sring.empty, c(sring.empty))
                A(crs[:, 0:2, :], crs[:, 0:2, :], ACT.Exp, scale=-0.5).then_inc(sem_lora_rstd, 1)
                act.wait_ge(sem_lora_rstd, c(sem_lora_rstd))
                for j in (0, 2):
                    move(mq[0:96, j:j + 2, :], rows=96)
                act.sem_inc(sem_mla_raw, 1)
                c(sem_mla_raw)
                for j in (0, 2):
                    move(mk[0:64, j:j + 2, :], rows=64)
                act.sem_inc(sem_mla_raw, 1)
                c(sem_mla_raw)
                move(mv)
                for v in (dq, dk):
                    for j in (0, 2, 4):
                        move(v[:, j:j + 2, :])
                act.sem_inc(sem_dil_raw, 1)
                c(sem_dil_raw)
                for t in range(NT):
                    move(dv[:, t, 0:512])
                move(dv[:, :, 512:768])
                act.wait_ge(sem_forget_inputs, c(sem_forget_inputs))
                z8 = [tmp8[:, i, :] for i in range(4)]
                A(z8[1], z8[0], ACT.Abs).then_inc(scalar_step, 1)
                act.wait_ge(scalar_step, c(scalar_step))
                A(z8[1], z8[1], ACT.Exp, scale=-1.0).then_inc(scalar_step, 1)
                act.wait_ge(scalar_step, c(scalar_step))
                A(z8[1], z8[1], ACT.Ln, bias=ones[:, 0:1]).then_inc(sem_forget_exps, 1)
                act.wait_ge(sem_forget_exps, c(sem_forget_exps))
                for j in (0, 2):
                    move(cdiff[:, j:j + 2, :])
                act.sem_inc(sem_forget_rows, 1)
                c(sem_forget_rows)
                for group in range(2):
                    for t in range(NT):
                        act.wait_ge(sem_shifted, c(sem_shifted))
                        A(prob[:, 0:4, 0:(t + 1) * P], prob[:, 0:4, 0:(t + 1) * P], ACT.Exp).then_inc(sem_exped, 1)
                        act.wait_ge(sem_exped, c(sem_exped))
                        for kt in range(t + 1):
                            move(pTb[:, kt, :])
                        act.sem_inc(sem_probs_turned, 1)
                        c(sem_probs_turned)
                for t in range(NT):
                    for br in range(3):
                        act.wait_ge(sem_shifted, c(sem_shifted))
                        p = prob[:, 4 * br:4 * br + 4, 0:(t + 1) * P]
                        A(p, p, ACT.Exp).then_inc(sem_exped, 1)
                        act.wait_ge(sem_exped, c(sem_exped))
                    act.wait_ge(sem_dens, c(sem_dens))
                    A(lse, rowsum, ACT.Ln).then_inc(sem_log_dens, 1)
                    act.wait_ge(sem_log_dens, c(sem_log_dens))
                    act.wait_ge(sem_mix_shifted, c(sem_mix_shifted))
                    A(mixw, mixw, ACT.Exp).then_inc(sem_mix_exps, 1)
                    act.wait_ge(sem_mix_exps, c(sem_mix_exps))
                    for br in range(3):
                        for kt in range(t + 1):
                            move(pTb[:, kt, :])
                        act.sem_inc(sem_probs_turned, 1)
                        c(sem_probs_turned)
                act.wait_ge(sem_prob_free, c(sem_prob_free))
                for i in range(4):
                    kt, r = i // 2, i % 2
                    move(sz[:, 4 * kt + r:4 * kt + 4:2, :], scale=0.125)
                A(sp, sz, ACT.Abs).then_inc(scalar_step, 1)
                act.wait_ge(scalar_step, c(scalar_step))
                A(sp, sp, ACT.Exp, scale=-1.0).then_inc(scalar_step, 1)
                act.wait_ge(scalar_step, c(scalar_step))
                A(sp, sp, ACT.Ln, bias=ones[:, 0:1]).then_inc(sem_stick_logs, 1)
                act.wait_ge(sem_stick_logs, c(sem_stick_logs))
                act.wait_ge(sem_stick_sum, c(sem_stick_sum))
                A(sz, sz, ACT.Exp).then_inc(sem_stick_exp, 1)
                act.wait_ge(sem_stick_exp, c(sem_stick_exp))
                act.wait_ge(sem_o_all, c(sem_o_all))
                A(sq8, oall, ACT.Square).then_inc(sem_o_squares_b, 1)
                act.wait_ge(sem_o_squares_b, c(sem_o_squares_b))
                for j in range(4):
                    rsqrt_bank(flat(crs8[:, 2 * j:2 * j + 2, :]), scale=1.0 / 64)
                act.sem_inc(sem_o_rstd_b, 1)
                c(sem_o_rstd_b)
                for part in range(2):
                    act.wait_ge(sem_centred, c(sem_centred))
                    for t in range(NT):
                        A(sq_scr, xc[:, t, :], ACT.Square, accum_out=stat[:, t:t + 1]).then_inc(scalar_step, 1)
                        act.wait_ge(scalar_step, c(scalar_step))
                    A(rstd, stat, ACT.Ln, scale=1.0 / D, bias=eps5).then_inc(scalar_step, 1)
                    act.wait_ge(scalar_step, c(scalar_step))
                    A(rstd, rstd, ACT.Exp, scale=-0.5).then_inc(sem_ln_rstd, 1)
                    act.wait_ge(sem_ln_rstd, c(sem_ln_rstd))
                    if part:
                        break
                    act.wait_ge(sem_group_shifted, c(sem_group_shifted))
                    A(rt[:, 1, 0:8], rt[:, 1, 0:8], ACT.Exp).then_inc(sem_group_exps, 1)
                    act.wait_ge(sem_group_exps, c(sem_group_exps))
                    act.wait_ge(sem_pair_shifted, c(sem_pair_shifted))
                    A(rt[:, 9, 0:2], rt[:, 9, 0:2], ACT.Exp).then_inc(sem_pair_exps, 1)
                    act.wait_ge(sem_pair_exps, c(sem_pair_exps))
                    tables("silu_and_others")
                    for e in range(EXPERTS):
                        if e >= 2:
                            act.wait_ge(sem_hidden_used, c(sem_hidden_used))
                        for m in range(4):
                            bank = sring.take(act)
                            A(hh[e % 2][:, m, :], bank[:, 0:T], ACT.Silu).then_inc(sring.empty, 1)
                            act.wait_ge(sring.empty, c(sring.empty))
                            act.sem_inc(sem_hidden_silu, 1)
                            c(sem_hidden_silu)
                    for _ in range(2):
                        act.wait_ge(sem_hidden_used, c(sem_hidden_used))
                    tables("natural_log_exp_and_others")
                act.wait_ge(sem_layer_out, c(sem_layer_out))

        @block.vector
        def _(dve):
            c = Count()
            V = nc.vector
            V.memset(ones, 1.0).then_inc(vector_step, 1)
            dve.wait_ge(vector_step, c(vector_step))
            V.memset(eps, 1e-6).then_inc(vector_step, 1)
            dve.wait_ge(vector_step, c(vector_step))
            V.memset(eps5, 1e-5).then_inc(sem_ones_ready, 1)
            dve.wait_ge(sem_ones_ready, c(sem_ones_ready))

            def take2(fn, rows=P, n=512):
                bank = vring.take(dve)
                fn(bank[0:rows, 0:n]).then_inc(vring.empty, 1)
                dve.wait_ge(vring.empty, c(vring.empty))

            def split(bank, n=2):
                return bank.rearrange("p (a b) -> p a b", a=n)

            def turn(dst, src, cos, sin, tiles, rows=P, group=2):
                V.tensor_tensor(dst[0:rows], src[0:rows], over_mid(cos, tiles), ALU.mult).then_inc(vector_step, 1)
                dve.wait_ge(vector_step, c(vector_step))
                for j in range(0, tiles, 2):
                    n = min(2, tiles - j)
                    bank = vring.take(dve)
                    tmp = turn_tmp[0:rows, 0:n, :]
                    V.tensor_tensor(tmp, split(bank[0:rows, 0:n * T], n), over_mid(sin, n), ALU.mult).then_inc(vring.empty, 1)
                    dve.wait_ge(vring.empty, c(vring.empty))
                    V.tensor_tensor(dst[0:rows, j:j + n, :], dst[0:rows, j:j + n, :], tmp, ALU.add).then_inc(vector_step, 1)
                    dve.wait_ge(vector_step, c(vector_step))

            def softmax_logits(dst, t, scale, mask, more=None):
                nk = (t + 1) * P
                for j in range(2):
                    bank = vring.take(dve)
                    V.scalar_tensor_tensor(out=dst[:, j:4:2, 0:nk], in0=split(bank)[:, :, 0:nk], scalar=scale,
                                           in1=over_mid(mask[:, 0:nk], 2) if more is None else more[:, j:4:2, 0:nk],
                                           op0=ALU.mult, op1=ALU.add).then_inc(vring.empty, 1)
                    dve.wait_ge(vring.empty, c(vring.empty))
                if more is not None:
                    V.tensor_tensor(dst[:, 0:4, 0:nk], dst[:, 0:4, 0:nk], over_mid(mask[:, 0:nk], 4), ALU.add).then_inc(vector_step, 1)
                    dve.wait_ge(vector_step, c(vector_step))

            def shift(dst, nk, m):
                V.tensor_reduce(m, dst[:, 0:4, 0:nk], AX.X, ALU.max).then_inc(vector_step, 1)
                dve.wait_ge(vector_step, c(vector_step))
                V.tensor_tensor(dst[:, 0:4, 0:nk], dst[:, 0:4, 0:nk], over_last(m, nk), ALU.subtract).then_inc(sem_shifted, 1)
                dve.wait_ge(sem_shifted, c(sem_shifted))

            def normalise(dst, nk, s):
                dve.wait_ge(sem_exped, c(sem_exped))
                V.tensor_reduce(s, dst[:, 0:4, 0:nk], AX.X, ALU.add).then_inc(vector_step, 1)
                dve.wait_ge(vector_step, c(vector_step))
                V.reciprocal(s, s).then_inc(vector_step, 1)
                dve.wait_ge(vector_step, c(vector_step))
                V.tensor_tensor(dst[:, 0:4, 0:nk], dst[:, 0:4, 0:nk], over_last(s, nk), ALU.mult).then_inc(sem_probs_ready, 1)
                dve.wait_ge(sem_probs_ready, c(sem_probs_ready))

            dve.wait_ge(const_in, 16)
            for l in range(DEPTH):
                dve.wait_ge(param_in, 16 * (l + 1))
                for t in range(NT):
                    for j in range(2):
                        bank = vring.take(dve)
                        V.tensor_tensor(xT[:, 4 * j:4 * j + 4, t * P:(t + 1) * P], split(bank, 4),
                                        over_last(pa("norm_g")[:, 4 * j:4 * j + 4], P), ALU.mult).then_inc(vring.empty, 1)
                        dve.wait_ge(vring.empty, c(vring.empty))
                dve.sem_inc(sem_xT_ready, 1)
                c(sem_xT_ready)
                bank = vring.take(dve)
                V.tensor_copy(ba, split(bank[:, 0:24])).then_inc(vring.empty, 1)
                dve.wait_ge(vring.empty, c(vring.empty))
                V.tensor_scalar(wi, ba[:, :, 0:H], 1.0 / 16.0, None, ALU.mult).then_inc(vector_step, 1)
                dve.wait_ge(vector_step, c(vector_step))
                turn_tmp = s3
                dve.wait_ge(sem_index_raw, c(sem_index_raw))
                turn(idx, idx_raw, ca("cos_index", 64), ca("sin_index", 64), 5, 64)
                dve.sem_inc(sem_index_ready, 1)
                c(sem_index_ready)
                for i, (dst, gain) in enumerate(((qa_, "q_norm"), (ka_, "k_norm"))):
                    dve.wait_ge(sem_head_rstd, c(sem_head_rstd))
                    V.scalar_tensor_tensor(out=s3, in0=s2, scalar=pa(gain), in1=s4, op0=ALU.mult, op1=ALU.mult).then_inc(sem_head_normed, 1)
                    dve.wait_ge(sem_head_normed, c(sem_head_normed))
                    turn_tmp = logit
                    turn(dst, s3, ca("cos_head"), ca("sin_head"), 4)
                    dve.sem_inc(sem_head_turned, 1)
                    c(sem_head_turned)
                    if i:
                        dve.sem_inc(sem_qk_ready, 1)
                        c(sem_qk_ready)
                causal = ca("causal").rearrange("p (t k) -> p t k", t=NT)
                for t in range(NT):
                    nk = (t + 1) * P
                    dve.wait_ge(sem_index_dots, c(sem_index_dots))
                    V.tensor_scalar(score[:, 0:nk], s1[:, 0, 0:nk], wi[:, t, 0:1], None, ALU.mult).then_inc(vector_step, 1)
                    dve.wait_ge(vector_step, c(vector_step))
                    for h in range(1, H):
                        V.scalar_tensor_tensor(out=score[:, 0:nk], in0=s1[:, h, 0:nk], scalar=wi[:, t, h:h + 1],
                                               in1=score[:, 0:nk], op0=ALU.mult, op1=ALU.add).then_inc(vector_step, 1)
                        dve.wait_ge(vector_step, c(vector_step))
                    V.tensor_tensor(score[:, 0:nk], score[:, 0:nk], causal[:, t, 0:nk], ALU.add).then_inc(vector_step, 1)
                    dve.wait_ge(vector_step, c(vector_step))
                    if t == 0:
                        dve.sem_inc(sem_scored, 1)
                        c(sem_scored)
                    for r in range(TOPK // 8):
                        V.max(best, score[:, 0:nk]).then_inc(vector_step, 1)
                        dve.wait_ge(vector_step, c(vector_step))
                        V.match_replace(out=score[:, 0:nk], in_to_replace=best, in_values=score[:, 0:nk],
                                        imm_value=TAKEN).then_inc(vector_step, 1)
                        dve.wait_ge(vector_step, c(vector_step))
                    V.tensor_scalar(sel[:, t, 0:nk], score[:, 0:nk], -2.0e38, NEG, ALU.is_ge, ALU.mult).then_inc(vector_step, 1)
                    dve.wait_ge(vector_step, c(vector_step))
                    V.tensor_tensor(sel[:, t, 0:nk], sel[:, t, 0:nk], causal[:, t, 0:nk], ALU.add).then_inc(vector_step, 1)
                    dve.wait_ge(vector_step, c(vector_step))
                dve.wait_ge(sem_z_ready, c(sem_z_ready))
                for t in range(NT):
                    nk = (t + 1) * P
                    softmax_logits(logit, t, float(P) ** -0.5, sel[:, t, :])
                    shift(logit, nk, rowmax[:, 0:4])
                    normalise(logit, nk, rowsum[:, 0:4])
                    bank = vring.take(dve)
                    V.tensor_tensor(y[:, 2, :, t * P:(t + 1) * P], split(bank, 4), silu_z[:, :, t * P:(t + 1) * P],
                                    ALU.mult).then_inc(vring.empty, 1)
                    dve.wait_ge(vring.empty, c(vring.empty))
                dve.wait_ge(sem_z_ready, c(sem_z_ready))
                for j in (0, 2):
                    bank = vring.take(dve)
                    V.tensor_tensor(y[:, 1, j:j + 2, :], split(bank), s4[:, j:j + 2, :], ALU.mult).then_inc(vring.empty, 1)
                    dve.wait_ge(vring.empty, c(vring.empty))
                V.tensor_tensor(y[:, 1, :, :], y[:, 1, :, :], over_last(pa("pool_scale"), T), ALU.mult).then_inc(sem_y_pooled, 1)
                dve.wait_ge(sem_y_pooled, c(sem_y_pooled))
                for i in range(3):
                    dve.wait_ge(sem_conv_in, c(sem_conv_in))
                    for m in range(4 * i, 4 * i + 4):
                        cw = pa("conv_w")[:, CONV * m:CONV * m + CONV]
                        V.tensor_scalar(qkv[:, m, :], conv_in[:, m, 0:T], cw[:, 0:1], None, ALU.mult).then_inc(vector_step, 1)
                        dve.wait_ge(vector_step, c(vector_step))
                        for j in range(1, CONV):
                            V.scalar_tensor_tensor(out=qkv[:, m, :], in0=conv_in[:, m, j:j + T],
                                                   scalar=cw[:, j:j + 1], in1=qkv[:, m, :],
                                                   op0=ALU.mult, op1=ALU.add).then_inc(vector_step, 1)
                            dve.wait_ge(vector_step, c(vector_step))
                    dve.sem_inc(sem_convolved, 1)
                    c(sem_convolved)
                for i in range(2):
                    dve.wait_ge(sem_dn_rstd, c(sem_dn_rstd))
                    v = qkv[:, 4 * i:4 * i + 4, :]
                    V.scalar_tensor_tensor(out=v, in0=v, scalar=float(P) ** -0.5 if i == 0 else 1.0, in1=s2,
                                           op0=ALU.mult, op1=ALU.mult).then_inc(sem_dn_normed1, 1)
                    dve.wait_ge(sem_dn_normed1, c(sem_dn_normed1))
                dve.sem_inc(sem_dn_qk_normed, 1)
                c(sem_dn_qk_normed)
                z8 = [tmp8[:, i, :] for i in range(4)]
                V.tensor_copy(split(z8[0]), ba[:, :, 4:8]).then_inc(vector_step, 1)
                dve.wait_ge(vector_step, c(vector_step))
                V.tensor_tensor(split(z8[1]), ba[:, :, 8:12], over_mid(pa("dt_bias"), NT), ALU.add).then_inc(sem_beta_inputs, 1)
                dve.wait_ge(sem_beta_inputs, c(sem_beta_inputs))
                dve.wait_ge(sem_beta_exps, c(sem_beta_exps))
                V.tensor_scalar(z8[0], z8[0], 1.0, None, ALU.add).then_inc(vector_step, 1)
                dve.wait_ge(vector_step, c(vector_step))
                V.reciprocal(beta, z8[0]).then_inc(vector_step, 1)
                dve.wait_ge(vector_step, c(vector_step))
                V.scalar_tensor_tensor(out=z8[1], in0=z8[1], scalar=0.0, in1=z8[2], op0=ALU.max, op1=ALU.add).then_inc(vector_step, 1)
                dve.wait_ge(vector_step, c(vector_step))
                V.scalar_tensor_tensor(out=split(g), in0=split(z8[1]), scalar=-1.0, in1=over_mid(exp_a, NT),
                                       op0=ALU.mult, op1=ALU.mult).then_inc(sem_g_ready, 1)
                dve.wait_ge(sem_g_ready, c(sem_g_ready))
                bank = vring.take(dve)
                V.tensor_copy(gc, split(bank[:, 0:16])).then_inc(vring.empty, 1)
                dve.wait_ge(vring.empty, c(vring.empty))
                V.tensor_copy(s3.rearrange("p a (b c) -> p (a b) c", c=P), over_last(g, P)).then_inc(vector_step, 1)
                dve.wait_ge(vector_step, c(vector_step))
                V.tensor_copy(s4.rearrange("p a (b c) -> p (a b) c", c=P), over_last(beta, P)).then_inc(sem_g_rows, 1)
                dve.wait_ge(sem_g_rows, c(sem_g_rows))
                V.tensor_copy(split(kb_scale), gc[:, :, 0:4]).then_inc(vector_step, 1)
                dve.wait_ge(vector_step, c(vector_step))
                V.tensor_tensor(split(kd_scale), gc[:, :, 4:8], gc[:, :, 0:4], ALU.subtract).then_inc(sem_gc_ready, 1)
                dve.wait_ge(sem_gc_ready, c(sem_gc_ready))
                dve.wait_ge(sem_gc_exps, c(sem_gc_exps))
                V.tensor_tensor(kb_scale, kb_scale, beta, ALU.mult).then_inc(vector_step, 1)
                dve.wait_ge(vector_step, c(vector_step))
                for t in range(NT):
                    bank = vring.take(dve)
                    V.tensor_copy(expg[:, t, :], bank).then_inc(vring.empty, 1)
                    dve.wait_ge(vring.empty, c(vring.empty))
                    dt4, eg4 = split(DT[:, t, :], 4), split(expg[:, t, :], 4)
                    V.tensor_tensor(dt4, eg4, over_last(gc[:, t, 0:4], P), ALU.subtract).then_inc(vector_step, 1)
                    dve.wait_ge(vector_step, c(vector_step))
                    V.tensor_tensor(dt4, dt4, over_mid(ca("later"), 4), ALU.add).then_inc(sem_decay_logs, 1)
                    dve.wait_ge(sem_decay_logs, c(sem_decay_logs))
                for t in range(NT):
                    h4 = slice(t * H, (t + 1) * H)
                    bank = vring.take(dve)
                    V.tensor_tensor(split(kbe[:, t, :], 4), split(bank, 4), over_last(kb_scale[:, h4], P), ALU.mult).then_inc(vector_step, 1)
                    dve.wait_ge(vector_step, c(vector_step))
                    V.tensor_tensor(split(kdec[:, t, :], 4), split(bank, 4), over_last(kd_scale[:, h4], P), ALU.mult).then_inc(vring.empty, 1)
                    dve.wait_ge(vring.empty, c(vring.empty))
                    bank = vring.take(dve)
                    V.tensor_tensor(split(vbeta[:, t, :], 4), split(bank, 4), over_last(beta[:, h4], P), ALU.mult).then_inc(vring.empty, 1)
                    dve.wait_ge(vring.empty, c(vring.empty))
                for t in range(NT):
                    dve.wait_ge(sem_decays, c(sem_decays))
                    V.tensor_tensor(split(qe[:, t, :], 4), qkv[:, 0:4, t * P:(t + 1) * P], split(expg[:, t, :], 4), ALU.mult).then_inc(vector_step, 1)
                    dve.wait_ge(vector_step, c(vector_step))
                    bank = vring.take(dve)
                    V.tensor_tensor(U[:, t, :], bank, DT[:, t, :], ALU.mult).then_inc(vring.empty, 1)
                    dve.wait_ge(vring.empty, c(vring.empty))
                    V.tensor_tensor(split(U[:, t, :], 4), split(U[:, t, :], 4), over_mid(ca("strict"), 4), ALU.mult).then_inc(vector_step, 1)
                    dve.wait_ge(vector_step, c(vector_step))
                    bank = vring.take(dve)
                    V.tensor_tensor(U[:, t, :], bank, U[:, t, :], ALU.mult).then_inc(vring.empty, 1)
                    dve.wait_ge(vring.empty, c(vring.empty))
                    bank = vring.take(dve)
                    V.tensor_tensor(attnT[:, t, :], bank, DT[:, t, :], ALU.mult).then_inc(vring.empty, 1)
                    dve.wait_ge(vring.empty, c(vring.empty))
                merge = ca("merge").rearrange("p (s c) -> p s c", s=6)
                for t in range(NT):
                    tt = split(TT[:, t, :], 4)
                    V.tensor_tensor(tt, split(U[:, t, :], 4), over_mid(merge[:, 0, :], 4), ALU.mult).then_inc(vector_step, 1)
                    dve.wait_ge(vector_step, c(vector_step))
                    V.tensor_tensor(tt, over_mid(ca("ident"), 4), tt, ALU.subtract).then_inc(vector_step, 1)
                    dve.wait_ge(vector_step, c(vector_step))
                dve.sem_inc(sem_inverse_started, 1)
                c(sem_inverse_started)
                for t in range(NT):
                    bank = vring.take(dve)
                    V.tensor_copy(Tm[:, t, :], bank).then_inc(vring.empty, 1)
                    dve.wait_ge(vring.empty, c(vring.empty))
                for s in range(1, 6):
                    for t in range(NT):
                        V.tensor_tensor(split(DT[:, t, :], 4), split(U[:, t, :], 4), over_mid(merge[:, s, :], 4), ALU.mult).then_inc(vector_step, 1)
                        dve.wait_ge(vector_step, c(vector_step))
                    dve.sem_inc(sem_off_block, 1)
                    c(sem_off_block)
                    for t in range(NT):
                        bank = vring.take(dve)
                        V.tensor_tensor(Tm[:, t, :], Tm[:, t, :], bank, ALU.subtract).then_inc(vring.empty, 1)
                        dve.wait_ge(vring.empty, c(vring.empty))
                        bank = vring.take(dve)
                        V.tensor_tensor(TT[:, t, :], TT[:, t, :], bank, ALU.subtract).then_inc(vring.empty, 1)
                        dve.wait_ge(vring.empty, c(vring.empty))
                dve.sem_inc(sem_inverse_ready, 1)
                c(sem_inverse_ready)
                for n in range(T // CHUNK):
                    t, r = n // 2, CHUNK * (n % 2)
                    rows = slice(r, r + CHUNK)
                    if n == 0:
                        dve.wait_ge(sem_u_w_ready, c(sem_u_w_ready))
                        V.tensor_copy(vnew[rows], split(Tm[rows, t, :], 4)).then_inc(sem_v_new, 1)
                        dve.wait_ge(sem_v_new, c(sem_v_new))
                    else:
                        bank = vring.take(dve)
                        V.tensor_tensor(vnew[rows], split(Tm[rows, t, :], 4), split(bank[rows], 4), ALU.subtract).then_inc(vring.empty, 1)
                        dve.wait_ge(vring.empty, c(vring.empty))
                        dve.sem_inc(sem_v_new, 1)
                        c(sem_v_new)
                        if n == T // CHUNK - 1:
                            break
                        last = split(expg[:, t, :], 4)[:, :, r + CHUNK - 1]
                        bank = vring.take(dve)
                        V.tensor_tensor(state, state, over_last(last, P), ALU.mult).then_inc(vector_step, 1)
                        dve.wait_ge(vector_step, c(vector_step))
                        V.tensor_tensor(state, state, split(bank, 4), ALU.add).then_inc(vring.empty, 1)
                        dve.wait_ge(vring.empty, c(vring.empty))
                        dve.sem_inc(sem_state_ready, 1)
                        c(sem_state_ready)
                        continue
                    bank = vring.take(dve)
                    V.tensor_copy(state, split(bank, 4)).then_inc(vring.empty, 1)
                    dve.wait_ge(vring.empty, c(vring.empty))
                    dve.sem_inc(sem_state_ready, 1)
                    c(sem_state_ready)
                dve.wait_ge(sem_z_ready, c(sem_z_ready))
                dve.wait_ge(sem_o_rstd, c(sem_o_rstd))
                V.scalar_tensor_tensor(out=oT, in0=oT, scalar=pa("o_norm"), in1=s2, op0=ALU.mult, op1=ALU.mult).then_inc(vector_step, 1)
                dve.wait_ge(vector_step, c(vector_step))
                V.tensor_tensor(y[:, 0, :, :], oT, silu_z, ALU.mult).then_inc(sem_branches_ready, 1)
                dve.wait_ge(sem_branches_ready, c(sem_branches_ready))
                dve.sem_inc(sem_o_scaled, 1)
                c(sem_o_scaled)
                for n in range(3):
                    for m in range(KD):
                        i = n * KD + m
                        dve.wait_ge(sem_gate_sigmoid, c(sem_gate_sigmoid))
                        bank = vring.take(dve)
                        sig = msig[:, i % 2, :]
                        if n == 0:
                            V.tensor_tensor(merged[:, m, :], bank[:, 0:T], sig, ALU.mult).then_inc(vring.empty, 1)
                            dve.wait_ge(vring.empty, c(vring.empty))
                        else:
                            V.tensor_tensor(sig, bank[:, 0:T], sig, ALU.mult).then_inc(vring.empty, 1)
                            dve.wait_ge(vring.empty, c(vring.empty))
                            V.tensor_tensor(merged[:, m, :], merged[:, m, :], sig, ALU.add).then_inc(vector_step, 1)
                            dve.wait_ge(vector_step, c(vector_step))
                        dve.sem_inc(sem_gate_used, 1)
                        c(sem_gate_used)
                dve.sem_inc(sem_merged_ready, 1)
                c(sem_merged_ready)
                for cc in range(2):
                    for t in range(NT):
                        bank = vring.take(dve)
                        xs = x[:, t, cc * 512:(cc + 1) * 512]
                        V.tensor_tensor(xs, xs, bank, ALU.add).then_inc(vring.empty, 1)
                        dve.wait_ge(vring.empty, c(vring.empty))
                dve.sem_inc(sem_layer_out, 1)
                c(sem_layer_out)

            dve.wait_ge(const_in, 32)
            for l in range(DEPTH):
                dve.wait_ge(param_in, 16 * (DEPTH + l + 1))
                for t in range(NT):
                    for j in range(2):
                        bank = vring.take(dve)
                        V.tensor_copy(xT[:, 4 * j:4 * j + 4, t * P:(t + 1) * P], split(bank, 4)).then_inc(vring.empty, 1)
                        dve.wait_ge(vring.empty, c(vring.empty))
                dve.sem_inc(sem_xT_ready, 1)
                c(sem_xT_ready)
                z8 = [tmp8[:, i, :] for i in range(4)]
                bank = vring.take(dve)
                V.tensor_tensor(split(z8[0]), split(bank[:, 0:8]), over_mid(pb("b_forget"), NT), ALU.add).then_inc(vring.empty, 1)
                dve.wait_ge(vring.empty, c(vring.empty))
                V.tensor_scalar(z8[0], z8[0], -1.0, None, ALU.mult).then_inc(sem_forget_inputs, 1)
                dve.wait_ge(sem_forget_inputs, c(sem_forget_inputs))
                dve.wait_ge(sem_lora_rstd, c(sem_lora_rstd))
                for i in range(3):
                    gain = pb("g_cq")[:, i:i + 1] if i < 2 else pb("g_ckv")
                    V.scalar_tensor_tensor(out=cqkv[:, i, :], in0=cqkv[:, i, :], scalar=gain, in1=crs[:, i // 2, :],
                                           op0=ALU.mult, op1=ALU.mult).then_inc(vector_step, 1)
                    dve.wait_ge(vector_step, c(vector_step))
                dve.sem_inc(sem_lora_normed, 1)
                c(sem_lora_normed)
                for v in (mq, mk):
                    dve.wait_ge(sem_mla_raw, c(sem_mla_raw))
                    turn_tmp = b1
                    bank0 = vring.take(dve)
                    bank1 = vring.take(dve)
                    V.tensor_tensor(v[0:96], v[0:96], over_mid(cb("cos_mla", 96), 4), ALU.mult).then_inc(vector_step, 1)
                    dve.wait_ge(vector_step, c(vector_step))
                    for j, bank in ((0, bank0), (2, bank1)):
                        V.tensor_tensor(b1[0:96, 0:2, :], split(bank[0:96]), over_mid(cb("sin_mla", 96), 2), ALU.mult).then_inc(vring.empty, 1)
                        dve.wait_ge(vring.empty, c(vring.empty))
                        V.tensor_tensor(v[0:96, j:j + 2, :], v[0:96, j:j + 2, :], b1[0:96, 0:2, :], ALU.add).then_inc(vector_step, 1)
                        dve.wait_ge(vector_step, c(vector_step))
                dve.wait_ge(sem_dil_raw, c(sem_dil_raw))
                for v in (dq, dk):
                    banks = [vring.take(dve) for _ in range(3)]
                    V.tensor_tensor(v, v, over_mid(cb("cos64"), 6), ALU.mult).then_inc(vector_step, 1)
                    dve.wait_ge(vector_step, c(vector_step))
                    for j, bank in enumerate(banks):
                        V.tensor_tensor(b1[:, 0:2, :], split(bank), over_mid(cb("sin64"), 2), ALU.mult).then_inc(vring.empty, 1)
                        dve.wait_ge(vring.empty, c(vring.empty))
                        V.tensor_tensor(v[:, 2 * j:2 * j + 2, :], v[:, 2 * j:2 * j + 2, :], b1[:, 0:2, :], ALU.add).then_inc(vector_step, 1)
                        dve.wait_ge(vector_step, c(vector_step))
                dve.wait_ge(sem_forget_exps, c(sem_forget_exps))
                V.scalar_tensor_tensor(out=z8[2], in0=z8[0], scalar=0.0, in1=z8[1], op0=ALU.max, op1=ALU.add).then_inc(vector_step, 1)
                dve.wait_ge(vector_step, c(vector_step))
                V.tensor_scalar(logf, split(z8[2]), -1.0, None, ALU.mult).then_inc(sem_logf_ready, 1)
                dve.wait_ge(sem_logf_ready, c(sem_logf_ready))
                bank = vring.take(dve)
                V.tensor_copy(cq_tok, split(bank[:, 0:8])).then_inc(vring.empty, 1)
                dve.wait_ge(vring.empty, c(vring.empty))
                V.tensor_copy(f_row[:, 0], over_last(logf[:, 0, :], P)).then_inc(vector_step, 1)
                dve.wait_ge(vector_step, c(vector_step))
                V.tensor_copy(f_row[:, 1], over_last(logf[:, 1, :], P)).then_inc(sem_logf_rows, 1)
                dve.wait_ge(sem_logf_rows, c(sem_logf_rows))
                dve.wait_ge(sem_forget_rows, c(sem_forget_rows))
                dve.sem_inc(sem_attention_inputs, 1)
                c(sem_attention_inputs)
                causal = cb("causal").rearrange("p (t k) -> p t k", t=NT)

                def gather(group, t, add=False):
                    bank = vring.take(dve)
                    for r in range(2):
                        rows = slice(64 * r, 64 * r + 64)
                        src = split(bank[rows], 4)[:, r:4:2, :]
                        dst = oall[rows, 2 * group:2 * group + 2, t * P:(t + 1) * P]
                        op = V.tensor_tensor(dst, dst, src, ALU.add) if add else V.tensor_copy(dst, src)
                        last = vring.empty if r else vector_step
                        op.then_inc(last, 1)
                        dve.wait_ge(last, c(last))

                for group in (1, 2):
                    for t in range(NT):
                        nk = (t + 1) * P
                        if group == 1:
                            V.tensor_tensor(b2[:, :, 0:nk], over_last(cq_tok[:, t, :], nk), cdiff[:, :, 0:nk], ALU.subtract).then_inc(vector_step, 1)
                            dve.wait_ge(vector_step, c(vector_step))
                            softmax_logits(prob, t, 0.125, causal[:, t, :], b2)
                        else:
                            softmax_logits(prob, t, 96.0 ** -0.5, causal[:, t, :])
                        shift(prob, nk, rowmax[:, 0:4])
                        normalise(prob, nk, rowsum[:, 0:4])
                        gather(group, t)
                dil = cb("dilated").rearrange("p (b t k) -> p b t k", b=3, t=NT)
                for t in range(NT):
                    nk = (t + 1) * P
                    for br in range(3):
                        v = prob[:, 4 * br:4 * br + 4, :]
                        softmax_logits(v, t, 0.125, dil[:, br, t, :])
                        shift(v, nk, rowmax[:, 4 * br:4 * br + 4])
                    for br in range(3):
                        dve.wait_ge(sem_exped, c(sem_exped))
                        last = sem_dens if br == 2 else vector_step
                        V.tensor_reduce(rowsum[:, 4 * br:4 * br + 4], prob[:, 4 * br:4 * br + 4, 0:nk], AX.X, ALU.add).then_inc(last, 1)
                        dve.wait_ge(last, c(last))
                    dve.wait_ge(sem_log_dens, c(sem_log_dens))
                    V.tensor_tensor(mixw, lse, rowmax, ALU.add).then_inc(vector_step, 1)
                    dve.wait_ge(vector_step, c(vector_step))
                    by_head = mixw.rearrange("p (b h) -> p h b", b=3)
                    V.tensor_reduce(mix1, by_head, AX.X, ALU.max).then_inc(vector_step, 1)
                    dve.wait_ge(vector_step, c(vector_step))
                    V.tensor_tensor(split(mixw, 3), split(mixw, 3), over_mid(mix1, 3), ALU.subtract).then_inc(sem_mix_shifted, 1)
                    dve.wait_ge(sem_mix_shifted, c(sem_mix_shifted))
                    dve.wait_ge(sem_mix_exps, c(sem_mix_exps))
                    V.tensor_reduce(mix1, by_head, AX.X, ALU.add).then_inc(vector_step, 1)
                    dve.wait_ge(vector_step, c(vector_step))
                    V.tensor_tensor(split(rowsum, 3), split(rowsum, 3), over_mid(mix1, 3), ALU.mult).then_inc(vector_step, 1)
                    dve.wait_ge(vector_step, c(vector_step))
                    V.reciprocal(rowsum, rowsum).then_inc(vector_step, 1)
                    dve.wait_ge(vector_step, c(vector_step))
                    V.tensor_tensor(mixw, mixw, rowsum, ALU.mult).then_inc(vector_step, 1)
                    dve.wait_ge(vector_step, c(vector_step))
                    V.tensor_tensor(prob[:, :, 0:nk], prob[:, :, 0:nk], over_last(mixw, nk), ALU.mult).then_inc(sem_probs_ready, 1)
                    dve.wait_ge(sem_probs_ready, c(sem_probs_ready))
                    for br in range(3):
                        gather(3, t, br > 0)
                dve.sem_inc(sem_prob_free, 1)
                c(sem_prob_free)
                before = cb("before").rearrange("p (t k) -> p t k", t=NT)
                dve.wait_ge(sem_stick_logs, c(sem_stick_logs))
                V.scalar_tensor_tensor(out=sp, in0=sz, scalar=0.0, in1=sp, op0=ALU.max, op1=ALU.add).then_inc(vector_step, 1)
                dve.wait_ge(vector_step, c(vector_step))
                for kt in range(NT):
                    V.scalar_tensor_tensor(out=slk[:, 4 * kt:4 * kt + 4, :], in0=sp[:, 4 * kt:4 * kt + 4, :], scalar=-1.0,
                                           in1=over_mid(before[:, kt, :], 4), op0=ALU.mult, op1=ALU.mult).then_inc(vector_step, 1)
                    dve.wait_ge(vector_step, c(vector_step))
                dve.sem_inc(sem_log_keep, 1)
                c(sem_log_keep)
                V.tensor_tensor(sz, sz, sp, ALU.subtract).then_inc(vector_step, 1)
                dve.wait_ge(vector_step, c(vector_step))
                for i in range(4):
                    bank = vring.take(dve)
                    v = sz[:, 2 * i:2 * i + 2, :]
                    V.tensor_tensor(v, v, split(bank), ALU.add).then_inc(vring.empty, 1)
                    dve.wait_ge(vring.empty, c(vring.empty))
                dve.sem_inc(sem_stick_sum, 1)
                c(sem_stick_sum)
                dve.wait_ge(sem_stick_exp, c(sem_stick_exp))
                for kt in range(NT):
                    v = sz[:, 4 * kt:4 * kt + 4, :]
                    V.tensor_tensor(v, v, over_mid(before[:, kt, :], 4), ALU.mult).then_inc(vector_step, 1)
                    dve.wait_ge(vector_step, c(vector_step))
                dve.sem_inc(sem_stick_weights, 1)
                c(sem_stick_weights)
                for tile in range(2):
                    bank = vring.take(dve)
                    for r in range(2):
                        rows = slice(64 * r, 64 * r + 64)
                        last = vring.empty if r else vector_step
                        V.tensor_copy(oall[rows, tile, :], bank[rows, r * T:(r + 1) * T]).then_inc(last, 1)
                        dve.wait_ge(last, c(last))
                dve.sem_inc(sem_o_all, 1)
                c(sem_o_all)
                dve.wait_ge(sem_o_rstd_b, c(sem_o_rstd_b))
                V.tensor_tensor(oall, oall, crs8, ALU.mult).then_inc(vector_step, 1)
                dve.wait_ge(vector_step, c(vector_step))
                V.tensor_tensor(oall, oall, over_last(pb("g_head"), T), ALU.mult).then_inc(sem_o_ready_b, 1)
                dve.wait_ge(sem_o_ready_b, c(sem_o_ready_b))
                dve.wait_ge(norms_in, 64 * (l + 1))
                for part in range(2):
                    if part == 0:
                        for cc in range(2):
                            for t in range(NT):
                                bank = vring.take(dve)
                                xs = x[:, t, cc * 512:(cc + 1) * 512]
                                V.scalar_tensor_tensor(out=xs, in0=xs, scalar=ALPHA, in1=bank, op0=ALU.mult, op1=ALU.add).then_inc(vring.empty, 1)
                                dve.wait_ge(vring.empty, c(vring.empty))
                    else:
                        V.scalar_tensor_tensor(out=x, in0=x, scalar=ALPHA, in1=ymoe, op0=ALU.mult, op1=ALU.add).then_inc(vector_step, 1)
                        dve.wait_ge(vector_step, c(vector_step))
                    V.tensor_reduce(mean, x, AX.X, ALU.add).then_inc(vector_step, 1)
                    dve.wait_ge(vector_step, c(vector_step))
                    V.tensor_scalar(mean, mean, 1.0 / D, None, ALU.mult).then_inc(vector_step, 1)
                    dve.wait_ge(vector_step, c(vector_step))
                    for t in range(NT):
                        last = sem_centred if t else vector_step
                        V.tensor_scalar(xc[:, t, :], x[:, t, :], mean[:, t:t + 1], None, ALU.subtract).then_inc(last, 1)
                        dve.wait_ge(last, c(last))
                    dve.wait_ge(sem_ln_rstd, c(sem_ln_rstd))
                    for t in range(NT):
                        V.scalar_tensor_tensor(out=x[:, t, :], in0=xc[:, t, :], scalar=rstd[:, t:t + 1],
                                               in1=ln_rows[:, 2 * part, :], op0=ALU.mult, op1=ALU.mult).then_inc(vector_step, 1)
                        dve.wait_ge(vector_step, c(vector_step))
                    last = sem_layer_out if part else sem_x_normed
                    V.tensor_tensor(x, x, over_mid(ln_rows[:, 2 * part + 1, :], NT), ALU.add).then_inc(last, 1)
                    dve.wait_ge(last, c(last))
                    if part:
                        break
                    for t in range(NT):
                        for j in range(2):
                            bank = vring.take(dve)
                            V.tensor_copy(xT[:, 4 * j:4 * j + 4, t * P:(t + 1) * P], split(bank, 4)).then_inc(vring.empty, 1)
                            dve.wait_ge(vring.empty, c(vring.empty))
                    dve.sem_inc(sem_xT_ready, 1)
                    c(sem_xT_ready)
                    bank = vring.take(dve)
                    V.tensor_tensor(router, split(bank[:, 0:40]), over_mid(pb("b_router"), NT), ALU.add).then_inc(vring.empty, 1)
                    dve.wait_ge(vring.empty, c(vring.empty))

                    def first_max(out, values, top, a_, b_):
                        V.tensor_reduce(top, values, AX.X, ALU.max).then_inc(vector_step, 1)
                        dve.wait_ge(vector_step, c(vector_step))
                        V.tensor_tensor(a_, values, over_last(top, 4), ALU.is_equal).then_inc(vector_step, 1)
                        dve.wait_ge(vector_step, c(vector_step))
                        V.memset(b_[:, :, 0:1], 0.0).then_inc(vector_step, 1)
                        dve.wait_ge(vector_step, c(vector_step))
                        for i in range(1, 4):
                            V.tensor_tensor(b_[:, :, i:i + 1], b_[:, :, i - 1:i], a_[:, :, i - 1:i], ALU.max).then_inc(vector_step, 1)
                            dve.wait_ge(vector_step, c(vector_step))
                        V.tensor_tensor(b_, b_, a_, ALU.mult).then_inc(vector_step, 1)
                        dve.wait_ge(vector_step, c(vector_step))
                        V.tensor_tensor(out, a_, b_, ALU.subtract).then_inc(vector_step, 1)
                        dve.wait_ge(vector_step, c(vector_step))

                    def r8(i):
                        return split(rt[:, i, 0:8])

                    top_g, top_1, top_2 = rt[:, 10, 0:2], rt[:, 10, 2:4], rt[:, 10, 4:6]
                    first_max(r8(0), router[:, :, 0:4], top_g, r8(2), r8(3))
                    V.tensor_tensor(r8(1), router[:, :, 0:4], over_last(top_g, 4), ALU.subtract).then_inc(sem_group_shifted, 1)
                    dve.wait_ge(sem_group_shifted, c(sem_group_shifted))
                    e_sel = r8(4)
                    V.tensor_tensor(e_sel, router[:, :, 4:8], over_last(r8(0)[:, :, 0], 4), ALU.mult).then_inc(vector_step, 1)
                    dve.wait_ge(vector_step, c(vector_step))
                    for gi in range(1, GROUPS):
                        V.tensor_tensor(r8(5), router[:, :, 4 + 4 * gi:8 + 4 * gi], over_last(r8(0)[:, :, gi], 4), ALU.mult).then_inc(vector_step, 1)
                        dve.wait_ge(vector_step, c(vector_step))
                        V.tensor_tensor(e_sel, e_sel, r8(5), ALU.add).then_inc(vector_step, 1)
                        dve.wait_ge(vector_step, c(vector_step))
                    first_max(r8(6), e_sel, top_1, r8(2), r8(3))
                    V.scalar_tensor_tensor(out=r8(5), in0=r8(6), scalar=NEG, in1=e_sel, op0=ALU.mult, op1=ALU.add).then_inc(vector_step, 1)
                    dve.wait_ge(vector_step, c(vector_step))
                    first_max(r8(7), r8(5), top_2, r8(2), r8(3))
                    V.tensor_tensor(rt[:, 9, 0:2], top_2, top_1, ALU.subtract).then_inc(sem_pair_shifted, 1)
                    dve.wait_ge(sem_pair_shifted, c(sem_pair_shifted))
                    dve.wait_ge(sem_group_exps, c(sem_group_exps))
                    V.tensor_reduce(rt[:, 11, 0:2], r8(1), AX.X, ALU.add).then_inc(vector_step, 1)
                    dve.wait_ge(vector_step, c(vector_step))
                    dve.wait_ge(sem_pair_exps, c(sem_pair_exps))
                    V.tensor_scalar(rt[:, 12, 0:2], rt[:, 9, 0:2], 1.0, None, ALU.add).then_inc(vector_step, 1)
                    dve.wait_ge(vector_step, c(vector_step))
                    V.tensor_tensor(rt[:, 12, 0:2], rt[:, 12, 0:2], rt[:, 11, 0:2], ALU.mult).then_inc(vector_step, 1)
                    dve.wait_ge(vector_step, c(vector_step))
                    V.reciprocal(rt[:, 12, 0:2], rt[:, 12, 0:2]).then_inc(vector_step, 1)
                    dve.wait_ge(vector_step, c(vector_step))
                    V.tensor_tensor(rt[:, 13, 0:2], rt[:, 12, 0:2], rt[:, 9, 0:2], ALU.mult).then_inc(vector_step, 1)
                    dve.wait_ge(vector_step, c(vector_step))
                    V.tensor_tensor(r8(6), r8(6), over_last(rt[:, 12, 0:2], 4), ALU.mult).then_inc(vector_step, 1)
                    dve.wait_ge(vector_step, c(vector_step))
                    V.tensor_tensor(r8(7), r8(7), over_last(rt[:, 13, 0:2], 4), ALU.mult).then_inc(vector_step, 1)
                    dve.wait_ge(vector_step, c(vector_step))
                    V.tensor_tensor(r8(6), r8(6), r8(7), ALU.add).then_inc(vector_step, 1)
                    dve.wait_ge(vector_step, c(vector_step))
                    for gi in range(GROUPS):
                        V.tensor_tensor(gates[:, :, 4 * gi:4 * gi + 4], r8(6), over_last(r8(0)[:, :, gi], 4), ALU.mult).then_inc(vector_step, 1)
                        dve.wait_ge(vector_step, c(vector_step))
                    for e in range(EXPERTS):
                        for m in range(4):
                            dve.wait_ge(sem_hidden_silu, c(sem_hidden_silu))
                            bank = vring.take(dve)
                            hv = hh[e % 2][:, m, :]
                            V.tensor_tensor(hv, hv, bank[:, 0:T], ALU.mult).then_inc(vring.empty, 1)
                            dve.wait_ge(vring.empty, c(vring.empty))
                        dve.sem_inc(sem_hidden_ready, 1)
                        c(sem_hidden_ready)
                        for t in range(NT):
                            for cc in range(2):
                                bank = vring.take(dve)
                                ys = ymoe[:, t, cc * 512:(cc + 1) * 512]
                                if e == 0:
                                    V.tensor_scalar(ys, bank, gates[:, t, e:e + 1], None, ALU.mult).then_inc(vring.empty, 1)
                                    dve.wait_ge(vring.empty, c(vring.empty))
                                else:
                                    V.scalar_tensor_tensor(out=ys, in0=bank, scalar=gates[:, t, e:e + 1], in1=ys,
                                                           op0=ALU.mult, op1=ALU.add).then_inc(vring.empty, 1)
                                    dve.wait_ge(vring.empty, c(vring.empty))
                        dve.sem_inc(sem_hidden_used, 1)
                        c(sem_hidden_used)


def pack(inputs):
    f = {k: np.asarray(v) for k, v in inputs.items()}

    def channels(v):
        return v.reshape(-1, P).T

    def rows(v):
        return np.broadcast_to(v.reshape(1, -1), (P, v.size))

    a, b = [], []
    for l in range(DEPTH):
        conv = f["conv_w"][l].reshape(CONV, 12, P).transpose(2, 1, 0).reshape(P, -1)
        a.append(np.concatenate([
            channels(f["norm_g"][l]), conv, channels(f["gate_b"][l]), channels(f["dn_onorm"][l]),
            channels(f["pool_scale"][l]), channels(f["q_norm"][l]), channels(f["k_norm"][l]), rows(f["a_log"][l]),
            rows(f["dt_bias"][l]), f["pool_w"][l].transpose(1, 0, 2).reshape(P, -1)], 1))
        router = np.concatenate([f["w_group_2"][l], f["w_expert_2"][l]], 1).reshape(KD, P, 20).transpose(1, 0, 2)
        b.append(np.concatenate([
            rows(f["b_forget_2"][l]), channels(f["g_cq_2"][l]), channels(f["g_ckv_2"][l]), channels(f["g_head_2"][l]),
            rows(np.concatenate([f["b_group_2"][l], f["b_expert_2"][l]])), router.reshape(P, -1),
            f["w_uq_2"][l].reshape(2, P, -1).transpose(1, 0, 2).reshape(P, -1), f["w_ukv_2"][l]], 1))
    return np.ascontiguousarray(np.stack(a)), np.ascontiguousarray(np.stack(b))


_STREAMED = ["x", "w_in", "w_branch", "w_out", "w_in_2", "w_out_2", "w1_2", "w3_2", "w2_2",
             "ln1_g_2", "ln1_b_2", "ln2_g_2", "ln2_b_2"]


def kernel(**inputs):
    import concourse.bacc as bacc
    from concourse.bass_utils import run_bass_kernel_spmd

    nc = bacc.Bacc("TRN2", target_bir_lowering=False, num_devices=1)
    arrays = {name: np.ascontiguousarray(inputs[name]) for name in _STREAMED}
    arrays["param_a"], arrays["param_b"] = pack(inputs)
    arrays["const_a"], arrays["const_b"] = constants()
    dram = {name: nc.dram_tensor(f"in_{name}", v.shape, F32, kind="ExternalInput").ap() for name, v in arrays.items()}
    dram["out"] = nc.dram_tensor("out", (1, T, D), F32, kind="ExternalOutput").ap()
    build_program(nc, dram)
    r = run_bass_kernel_spmd(nc, [{f"in_{name}": v for name, v in arrays.items()}], core_ids=[0])
    return r.results[0]["out"]
```

```python
from contextlib import ExitStack

import numpy as np

import concourse.bass as bass
from concourse import mybir

F32 = mybir.dt.float32
ALU = mybir.AluOpType
ACT = mybir.ActivationFunctionType
AX = mybir.AxisListType

P = 128
T = 256
NT = T // P
D = 1024
KD = D // P
DEPTH = 2
H = 4
CHUNK = 64
TOPK = 64
WINDOWS = (2, 4, 8, 16)
PAD = 16
CONV = 4
CROWD = 128.0
NEG = -1.0e30
TAKEN = -3.0e38
EXPERTS = 16
GROUPS = 4
SLOT = 4096
NSLOT = 4
W_A = 8524
W_B = 4260
ALPHA = float((2.0 * DEPTH) ** 0.25)

A_QKV, A_ZA, A_BA, A_UB, A_ZB = 0, 1536, 2048, 2056, 2568
A_QC, A_KC, A_VC, A_ZC, A_IQ, A_GATE = 3080, 3592, 4104, 4616, 5128, 5452
B_SBQK, B_SBV, B_FOXQ, B_FOXK, B_FOXV, B_F = 0, 512, 768, 1024, 1280, 1536
B_CQ, B_CKV, B_KR, B_DQ, B_DK, B_DV = 1540, 1796, 1924, 1956, 2724, 3492


def layout(parts):
    at, where = 0, {}
    for name, width in parts:
        where[name] = (at, at + width)
        at += width
    return where, at


CONST_A, WIDTH_CA = layout([
    ("ident", P), ("cumsum", P), ("chunk", P), ("later", P), ("strict", P), ("merge", 6 * P),
    ("rot_head", P), ("rot_index", P), ("cos_head", T), ("sin_head", T), ("cos_index", T), ("sin_index", T),
    ("count", len(WINDOWS) * T), ("causal", NT * T)])
CONST_B, WIDTH_CB = layout([
    ("ident", P), ("upto", P), ("after", P), ("pair", P), ("rot64", P), ("rot_mla", P),
    ("cos64", T), ("sin64", T), ("cos_mla", T), ("sin_mla", T), ("before", NT * T), ("causal", NT * T),
    ("dilated", 3 * NT * T), ("first_row", EXPERTS)])
PARAM_A, WIDTH_PA = layout([
    ("norm_g", KD), ("conv_w", 12 * CONV), ("gate_b", 24), ("o_norm", 1), ("pool_scale", 4),
    ("q_norm", 1), ("k_norm", 1), ("a_log", H), ("dt_bias", H), ("pool_w", 4 * P)])
PARAM_B, WIDTH_PB = layout([
    ("b_forget", H), ("g_cq", 2), ("g_ckv", 1), ("g_head", 8), ("b_router", 20), ("w_router", KD * 20),
    ("w_uq", 2 * 384), ("w_ukv", 512)])


def rotation(n, half, first=0, size=P):
    m = np.zeros((P, size), np.float32)
    for at in range(first, n, 2 * half):
        for i in range(half):
            m[at + half + i, at + i] = -1.0
            m[at + i, at + half + i] = 1.0
    return m


def rope(half, copies):
    freq = np.float32(10000.0) ** (-np.arange(half, dtype=np.float32) / np.float32(half))
    angle = (np.arange(T, dtype=np.float32)[:, None] * freq[None, :].astype(np.float32)).T
    return np.tile(np.cos(angle), (copies, 1)).astype(np.float32), np.tile(np.sin(angle), (copies, 1)).astype(np.float32)


def constants():
    a = np.zeros((P, WIDTH_CA), np.float32)
    b = np.zeros((P, WIDTH_CB), np.float32)

    def put(to, where, name, value):
        lo, hi = where[name]
        to[:value.shape[0], lo:hi] = value.reshape(value.shape[0], hi - lo)

    r, c = np.arange(P)[:, None], np.arange(P)[None, :]
    same = (r // CHUNK) == (c // CHUNK)
    q = np.arange(P)[:, None, None] + P * np.arange(NT)[None, :, None]
    k = np.arange(T)[None, None, :]
    causal = np.where(k <= q, 0.0, NEG)
    put(a, CONST_A, "ident", np.eye(P))
    put(a, CONST_A, "cumsum", (same & (r <= c)) * 1.0)
    put(a, CONST_A, "chunk", same * 1.0)
    put(a, CONST_A, "later", np.where(same & (r <= c), 0.0, NEG))
    put(a, CONST_A, "strict", (same & (r < c)) * 1.0)
    merge = [((r // (2 * s)) == (c // (2 * s))) & ((r // s) % 2 == 0) & ((c // s) % 2 == 1) for s in (1, 2, 4, 8, 16, 32)]
    put(a, CONST_A, "merge", np.stack(merge, 1) * 1.0)
    put(a, CONST_A, "rot_head", rotation(P, 64))
    put(a, CONST_A, "rot_index", rotation(64, 32))
    cos, sin = rope(64, 2)
    put(a, CONST_A, "cos_head", cos)
    put(a, CONST_A, "sin_head", sin)
    cos, sin = rope(32, 4)
    put(a, CONST_A, "cos_index", cos)
    put(a, CONST_A, "sin_index", sin)
    count = np.stack([1.0 / np.minimum(np.arange(1, T + 1), w).astype(np.float32) for w in WINDOWS])
    put(a, CONST_A, "count", np.tile(count.reshape(1, -1), (P, 1)))
    put(a, CONST_A, "causal", causal)
    put(b, CONST_B, "ident", np.eye(P))
    put(b, CONST_B, "upto", (r <= c) * 1.0)
    put(b, CONST_B, "after", (r > c) * 1.0)
    put(b, CONST_B, "pair", same * 1.0)
    put(b, CONST_B, "rot64", rotation(P, 32))
    put(b, CONST_B, "rot_mla", rotation(96, 16, 64))
    put(b, CONST_B, "cos64", cos)
    put(b, CONST_B, "sin64", sin)
    cos, sin = rope(16, 2)
    put(b, CONST_B, "cos_mla", np.concatenate([np.ones((64, T), np.float32), cos]))
    put(b, CONST_B, "sin_mla", np.concatenate([np.zeros((64, T), np.float32), sin]))
    key = np.arange(P)[:, None, None] + P * np.arange(NT)[None, :, None]
    put(b, CONST_B, "before", (key < k) * 1.0)
    put(b, CONST_B, "causal", causal)
    dilated = [np.where((k <= q) & (q - k <= window) & ((q - k) % dil == 0), 0.0, NEG)
               for window, dil in ((128, 1), (512, 4), (2048, 16))]
    put(b, CONST_B, "dilated", np.stack(dilated, 1))
    put(b, CONST_B, "first_row", np.tile(P * np.arange(EXPERTS), (P, 1)))
    return a, b


class Ring:

    def __init__(self, banks, full, empty):
        self.banks, self.full, self.empty = banks, full, empty
        self.filled = self.taken = 0

    def fill(self, pe):
        n = self.filled
        if n >= len(self.banks):
            pe.wait_ge(self.empty, n - len(self.banks) + 1)
        self.filled += 1
        return self.banks[n % len(self.banks)]

    def take(self, eng):
        self.taken += 1
        eng.wait_ge(self.full, self.taken)
        return self.banks[(self.taken - 1) % len(self.banks)]


class Count:

    def __init__(self):
        self.of = {}

    def __call__(self, sem):
        self.of[sem.name] = self.of.get(sem.name, 0) + 1
        return self.of[sem.name]


def branch_state(c, *rings):
    return dict(c.of), [(r.filled, r.taken) for r in rings]


def to_state(c, state, *rings):
    c.of = dict(state[0])
    for r, (filled, taken) in zip(rings, state[1]):
        r.filled, r.taken = filled, taken


class Arena:

    def __init__(self, tensor, at=0):
        self.tensor, self.at, self.most = tensor, at, at

    def take(self, *shape):
        n = int(np.prod(shape))
        v = self.tensor[:, self.at:self.at + n]
        self.at += n
        self.most = max(self.most, self.at)
        if len(shape) == 2:
            v = v.rearrange("p (a b) -> p a b", a=shape[0])
        if len(shape) == 3:
            v = v.rearrange("p (a b c) -> p a b c", a=shape[0], b=shape[1])
        return v


def over_last(ap, n):
    return ap.unsqueeze(len(ap.shape)).to_broadcast([*ap.shape, n])


def over_mid(ap, n):
    return ap.unsqueeze(1).to_broadcast([ap.shape[0], n, ap.shape[1]])


def build_program(nc, a):
    ctx = ExitStack()
    with ctx:
        def sem(name):
            return ctx.enter_context(nc.semaphore(name))

        def sb(name, n):
            return ctx.enter_context(nc.sbuf_tensor(name, [P, n], F32))

        slots = [sb(f"weights{i}", SLOT) for i in range(NSLOT)]
        x_t = sb("x", NT * D)
        xT_t = sb("xT", KD * T)
        const_t = sb("const", max(WIDTH_CA, WIDTH_CB))
        param_t = sb("param", max(WIDTH_PA, WIDTH_PB))
        ones_t = sb("ones", P)
        small_t = sb("small", 900)
        zeros_t = sb("zeros", 512)
        whole_t = ctx.enter_context(nc.sbuf_tensor("whole", [P, 8], mybir.dt.int32))
        rows_of = whole_t[:, 0:4]
        crowded = whole_t[0:1, 4:5]
        x_rows = nc.dram_tensor("x_rows", (EXPERTS * P, D), F32).ap()
        y_rows = nc.dram_tensor("y_rows", (EXPERTS * P, D), F32).ap()
        work_t = sb("work", 25100)
        x = x_t[:, :].rearrange("p (t d) -> p t d", t=NT)
        xT = xT_t[:, :].rearrange("p (k t) -> p k t", k=KD)
        ones = ones_t[:, :]

        vbanks = [ctx.enter_context(nc.psum_tensor(f"to_vector{i}", [P, 512], F32))[:, :] for i in range(4)]
        sbanks = [ctx.enter_context(nc.psum_tensor(f"to_scalar{i}", [P, 512], F32))[:, :] for i in range(4)]
        vring = Ring(vbanks, sem("vector_bank_full"), sem("vector_bank_empty"))
        sring = Ring(sbanks, sem("scalar_bank_full"), sem("scalar_bank_empty"))

        const_in, param_in, x_in = sem("const_in"), sem("param_in"), sem("x_in")
        norms_in, out_done = sem("ln_rows_in"), sem("out_done")
        weights_in = [sem(f"weights{i}_in") for i in range(NSLOT)]
        slot_used = sem("slot_used")
        x_rows_in = [sem(f"x_rows{i}_in") for i in range(3)]
        y_rows_out = [sem(f"y_rows{i}_out") for i in range(2)]
        rows_cleared, rows_sent, y_rows_in = sem("rows_cleared"), sem("rows_sent"), sem("y_rows_in")
        vector_step, scalar_step, gpsimd_step = sem("vector_step"), sem("scalar_step"), sem("gpsimd_step")
        sem_attention_inputs = sem("attention_inputs")
        sem_beta_exps = sem("beta_exps")
        sem_beta_inputs = sem("beta_inputs")
        sem_branches_ready = sem("branches_ready")
        sem_centred = sem("centred")
        sem_conv_in = sem("conv_in")
        sem_convolved = sem("convolved")
        sem_decay_logs = sem("decay_logs")
        sem_decays = sem("decays")
        sem_dens = sem("dens")
        sem_dil_raw = sem("dil_raw")
        sem_dn_normed1 = sem("dn_normed1")
        sem_dn_qk_normed = sem("dn_qk_normed")
        sem_dn_rstd = sem("dn_rstd")
        sem_dn_squares = sem("dn_squares")
        sem_exped = sem("exped")
        sem_forget_exps = sem("forget_exps")
        sem_forget_inputs = sem("forget_inputs")
        sem_forget_rows = sem("forget_rows")
        sem_g_ready = sem("g_ready")
        sem_g_rows = sem("g_rows")
        sem_gate_sigmoid = sem("gate_sigmoid")
        sem_gate_used = sem("gate_used")
        sem_gc_exps = sem("gc_exps")
        sem_gc_ready = sem("gc_ready")
        sem_group_exps = sem("group_exps")
        sem_group_shifted = sem("group_shifted")
        sem_head_normed = sem("head_normed")
        sem_head_rstd = sem("head_rstd")
        sem_head_squares = sem("head_squares")
        sem_head_turned = sem("head_turned")
        sem_chosen = sem("chosen")
        sem_crowded = sem("crowded")
        sem_rows_turned = sem("rows_turned")
        sem_rows_turned_s = sem("rows_turned_s")
        sem_h_rows = sem("h_rows")
        sem_h_turned = sem("h_turned")
        sem_y_out = sem("y_out")
        sem_hidden_ready = sem("hidden_ready")
        sem_hidden_silu = sem("hidden_silu")
        sem_hidden_used = sem("hidden_used")
        sem_index_dots = sem("index_dots")
        sem_index_raw = sem("index_raw")
        sem_index_ready = sem("index_ready")
        sem_inverse_ready = sem("inverse_ready")
        sem_inverse_started = sem("inverse_started")
        sem_layer_out = sem("layer_out")
        sem_ln_rstd = sem("ln_rstd")
        sem_log_dens = sem("log_dens")
        sem_log_keep = sem("log_keep")
        sem_logf_ready = sem("logf_ready")
        sem_logf_rows = sem("logf_rows")
        sem_lora_normed = sem("lora_normed")
        sem_lora_rstd = sem("lora_rstd")
        sem_lora_squares = sem("lora_squares")
        sem_merged_ready = sem("merged_ready")
        sem_mix_exps = sem("mix_exps")
        sem_mix_shifted = sem("mix_shifted")
        sem_mla_raw = sem("mla_raw")
        sem_o_all = sem("o_all")
        sem_o_ready_b = sem("o_ready_b")
        sem_o_rstd = sem("o_rstd")
        sem_o_rstd_b = sem("o_rstd_b")
        sem_o_scaled = sem("o_scaled")
        sem_o_squares = sem("o_squares")
        sem_o_squares_b = sem("o_squares_b")
        sem_off_block = sem("off_block")
        sem_off_times_T = sem("off_times_T")
        sem_ones_ready = sem("ones_ready")
        sem_pair_exps = sem("pair_exps")
        sem_pair_shifted = sem("pair_shifted")
        sem_pool_in = sem("pool_in")
        sem_pooled = sem("pooled")
        sem_prob_free = sem("prob_free")
        sem_probs_ready = sem("probs_ready")
        sem_probs_turned = sem("probs_turned")
        sem_qk_ready = sem("qk_ready")
        sem_scored = sem("scored")
        sem_shifted = sem("shifted")
        sem_state_ready = sem("state_ready")
        sem_stick_exp = sem("stick_exp")
        sem_stick_logs = sem("stick_logs")
        sem_stick_sum = sem("stick_sum")
        sem_stick_weights = sem("stick_weights")
        sem_u_w_ready = sem("u_w_ready")
        sem_v_new = sem("v_new")
        sem_xT_ready = sem("xT_ready")
        sem_x_normed = sem("x_normed")
        sem_x_scaled = sem("x_scaled")
        sem_y_pooled = sem("y_pooled")
        sem_z_ready = sem("z_ready")

        def cols(w, l, lo, n, at=0, rows=KD):
            src = w[l, :, lo:lo + n].rearrange("(k p) n -> p k n", p=P)
            return (at, rows, n, src)

        loads = []
        for l in range(DEPTH):
            wa = a["w_in"]
            loads.append([cols(wa, l, A_IQ, 324), cols(wa, l, A_BA, 8, 324)])
            for lo in (A_QC, A_KC, A_VC, A_ZC, A_UB, A_ZB, A_QKV, A_QKV + 512, A_QKV + 1024, A_ZA):
                loads.append([cols(wa, l, lo, 512)])
            for n in range(3):
                loads.append([cols(wa, l, A_GATE + n * D, 512)])
                loads.append([(0, 4, D, a["w_branch"][l, n].rearrange("(k p) d -> p k d", p=P))])
                loads.append([cols(wa, l, A_GATE + n * D + 512, 512)])
            for c in range(2):
                loads.append([cols(a["w_out"], l, c * 512, 512)])
        for l in range(DEPTH):
            wb = a["w_in_2"]
            for lo, n in ((B_SBQK, 512), (B_SBV, 512), (B_FOXK, 512), (B_F, 420), (B_DQ, 512), (B_DQ + 512, 512),
                          (B_DK + 256, 512), (B_DV, 512), (B_DV + 512, 256)):
                loads.append([cols(wb, l, lo, n)])
            for c in range(2):
                loads.append([cols(a["w_out_2"], l, c * 512, 512)])
            for e in range(EXPERTS + 1):
                if e < EXPERTS:
                    loads.append([(0, KD, 512, a["w1_2"][l, e].rearrange("(k p) n -> p k n", p=P))])
                    loads.append([(0, KD, 512, a["w3_2"][l, e].rearrange("(k p) n -> p k n", p=P))])
                if e:
                    loads.append([(0, 4, D, a["w2_2"][l, e - 1].rearrange("(k p) n -> p k n", p=P))])

        def width(parts):
            return sum(n for _, _, n, _ in parts)

        arrived, per_slot = [], [0] * NSLOT
        for i, parts in enumerate(loads):
            per_slot[i % NSLOT] += len(parts)
            arrived.append(per_slot[i % NSLOT])

        def slot_view(i):
            parts = loads[i]
            rows = parts[0][1]
            w = width(parts)
            return slots[i % NSLOT][:, 0:rows * w].rearrange("p (k n) -> p k n", k=rows)

        def ca(name, rows=P):
            lo, hi = CONST_A[name]
            return const_t[0:rows, lo:hi]

        def cb(name, rows=P):
            lo, hi = CONST_B[name]
            return const_t[0:rows, lo:hi]

        def pa(name):
            lo, hi = PARAM_A[name]
            return param_t[:, lo:hi]

        def pb(name):
            lo, hi = PARAM_B[name]
            return param_t[:, lo:hi]

        sm = Arena(small_t)
        eps = sm.take(1)
        eps5 = sm.take(1)
        stat = sm.take(NT)
        rstd = sm.take(NT)
        mean = sm.take(NT)
        ba = sm.take(NT, 12)
        beta = sm.take(NT * H)
        g = sm.take(NT * H)
        exp_a = sm.take(H)
        tmp8 = sm.take(4, NT * H)
        gc = sm.take(NT, 8)
        kb_scale = sm.take(NT * H)
        kd_scale = sm.take(NT * H)
        wi = sm.take(NT, H)
        best = sm.take(8)
        rowmax = sm.take(12)
        rowmax_t = [rowmax, sm.take(12)]
        rowsum = sm.take(12)
        lse = sm.take(12)
        mixw = sm.take(12)
        mix1 = sm.take(H)
        mix2 = sm.take(H)
        logf = sm.take(NT, H)
        cq_tok = sm.take(NT, H)
        router = sm.take(NT, 20)
        rt = sm.take(16, 16)
        gates = sm.take(NT, EXPERTS)
        chosen = sm.take(3, NT * EXPERTS)
        rank = sm.take(NT * EXPERTS)
        rows_f = sm.take(4)

        wk = Arena(work_t)
        y = wk.take(3, H, T)
        silu_z = wk.take(H, T)
        s12_at = wk.at
        s1, s2, s3, s4 = (wk.take(H, T) for _ in range(4))
        scaled_x = work_t[:, s12_at:s12_at + NT * D].rearrange("p (t d) -> p t d", t=NT)
        phase = wk.at
        qa_, ka_ = wk.take(H, T), wk.take(H, T)
        va_ = wk.take(NT, 512)
        idx_raw, idx = wk.take(5, T), wk.take(5, T)
        score, sel = wk.take(T), wk.take(NT, T)
        logit = wk.take(H, T)
        pT = wk.take(NT, 512)
        wk.at = phase + 12000
        pool_u, pool_1, pool_2 = (wk.take(4, PAD + T) for _ in range(3))
        wk.at = phase
        qkv = wk.take(12, T)
        conv_in = wk.take(12, T + CONV - 1)
        wk.at = phase + 12 * T
        kbe, kdec, vbeta, attnT, qe, expg, TT, Tm, X, U, DT = (wk.take(NT, 512) for _ in range(11))
        vnew, state = wk.take(H, P), wk.take(H, P)
        oT = wk.take(H, T)
        wk.at = phase
        merged = wk.take(KD, T)
        msig = wk.take(2, T)
        most_a = wk.most

        wb_ = Arena(work_t)
        ln_rows = wb_.take(4, D)
        oall = wb_.take(8, T)
        phase_b = wb_.at
        sbqk, sbv = wb_.take(4, T), wb_.take(NT, 256)
        dq, dk, dv = wb_.take(6, T), wb_.take(6, T), wb_.take(NT, 768)
        early = wb_.at
        foxq, foxk, mq, mk = wb_.take(2, T), wb_.take(2, T), wb_.take(4, T), wb_.take(4, T)
        foxv, mv = wb_.take(NT, 256), wb_.take(NT, 256)
        cdiff, b2 = wb_.take(H, T), wb_.take(4, T)
        big = wb_.at
        prob = wb_.take(12, T)
        prob_0 = wb_.take(12, P)
        pTb = wb_.take(NT, 512)
        b1 = wb_.take(4, T)
        most_b = wb_.at
        wb_.at = early
        sz, sp, slk = wb_.take(8, T), wb_.take(8, T), wb_.take(8, T)
        assert wb_.at <= big
        crs8, sq8 = sp, slk
        f_row = b1.rearrange("p h (t c) -> p (h t) c", t=2).rearrange("p (t h) c -> p t h c", t=NT)
        wb_.at = big
        cqkv = wb_.take(3, T)
        csq = wb_.take(3, T)
        crs = wb_.take(3, T)
        wb_.at = phase_b
        ymoe = wb_.take(NT, D)
        hh = [wb_.take(4, T) for _ in range(2)]
        xc = wb_.take(NT, D)
        sq_scr = wb_.take(D)
        rows_at = wb_.at
        x_in_rows = wb_.take(3, D)
        x_turned = wb_.take(2, KD * P)
        h_silu, h_rows, h_turned = wb_.take(2, 512), wb_.take(2, 512), wb_.take(2, 512)
        y_out = wb_.take(2, D)
        wb_.at = rows_at
        y_in = wb_.take(4, D)
        print("MOST", most_a, most_b, wb_.most, sm.most)
        assert max(most_a, wb_.most) <= 25100 and sm.most <= 900, (most_a, wb_.most, sm.most)

        fills = {vring: 8 * EXPERTS, sring: 4 * EXPERTS}
        per_layer = {sem_hidden_silu: 4 * EXPERTS, y_rows_in: 1, rows_sent: 1}
        for s_ in (sem_hidden_ready, sem_hidden_used, sem_rows_turned, sem_rows_turned_s, sem_h_rows, sem_h_turned, sem_y_out):
            per_layer[s_] = EXPERTS
        for i, s_ in enumerate(x_rows_in):
            per_layer[s_] = len(range(i, EXPERTS, 3))
        for s_ in y_rows_out:
            per_layer[s_] = EXPERTS // 2
        by_dma = {s_: 16 for s_ in (*x_rows_in, *y_rows_out)}
        by_dma[y_rows_in] = by_dma[rows_sent] = 64

        def make_up(eng, c, start, sent, filled=(), emptied=()):
            counts, rings = start
            for ring in filled:
                eng.wait_ge(ring.empty, ring.filled)
            for (n_filled, n_taken), ring in zip(rings, (vring, sring)):
                if ring in filled:
                    if ring.filled < n_filled + fills[ring]:
                        eng.sem_inc(ring.full, n_filled + fills[ring] - ring.filled)
                    ring.filled = n_filled + fills[ring]
                if ring in emptied:
                    if ring.taken < n_taken + fills[ring]:
                        eng.sem_inc(ring.empty, n_taken + fills[ring] - ring.taken)
                    ring.taken = n_taken + fills[ring]
                    c.of[ring.empty.name] = counts.get(ring.empty.name, 0) + fills[ring]
            for s_, n in per_layer.items():
                target = counts.get(s_.name, 0) + n
                behind = target - c.of.get(s_.name, 0)
                if s_ in sent and behind:
                    eng.sem_inc(s_, behind * by_dma.get(s_, 1))
                c.of[s_.name] = target

        block = ctx.enter_context(nc.Block())

        @block.sync
        def _(sp_):
            sp_.dma_start(x_t[:, :].rearrange("p (t d) -> p t d", t=NT),
                          a["x"][0].rearrange("(t p) d -> p t d", p=P)).then_inc(x_in, 16)
            at = 0
            for i, parts in enumerate(loads):
                if i >= NSLOT:
                    sp_.wait_ge(slot_used, i - NSLOT + 1)
                w = width(parts)
                for off, rows, n, src in parts:
                    dst = slots[i % NSLOT][:, 0:rows * w].rearrange("p (k n) -> p k n", k=rows)[:, :, off:off + n]
                    sp_.dma_start(dst, src).then_inc(weights_in[i % NSLOT], 16)
            sp_.wait_ge(sem_layer_out, 2 * DEPTH)
            sp_.dma_start(a["out"][0].rearrange("(t p) d -> p t d", p=P), x).then_inc(out_done, 16)
            sp_.wait_ge(out_done, 16)

        @block.gpsimd
        def _(pool):
            c = Count()
            for l in range(2 * DEPTH):
                if l:
                    pool.wait_ge(sem_layer_out, l)
                if l == 0:
                    pool.dma_start(const_t[:, 0:WIDTH_CA], a["const_a"]).then_inc(const_in, 16)
                if l == 1:
                    pool.memset(zeros_t[:, :], 0.0).then_inc(gpsimd_step, 1)
                    pool.wait_ge(gpsimd_step, c(gpsimd_step))
                    pool.dma_start(x_rows.rearrange("(p r) (c d) -> p (r c) d", p=P, d=512),
                                   over_mid(zeros_t[:, :], 2 * EXPERTS)).then_inc(rows_cleared, 16)
                if l == DEPTH:
                    pool.dma_start(const_t[:, 0:WIDTH_CB], a["const_b"]).then_inc(const_in, 16)
                if l < DEPTH:
                    pool.dma_start(param_t[:, 0:WIDTH_PA], a["param_a"][l]).then_inc(param_in, 16)
                    pool.memset(pool_1[:, :, 0:PAD], 0.0).then_inc(gpsimd_step, 1)
                    pool.wait_ge(gpsimd_step, c(gpsimd_step))
                    pool.memset(pool_2[:, :, 0:PAD], 0.0).then_inc(gpsimd_step, 1)
                    pool.wait_ge(gpsimd_step, c(gpsimd_step))
                    pool.wait_ge(const_in, 16)
                    pool.wait_ge(sem_pool_in, c(sem_pool_in))
                    src, dst = pool_u, pool_1
                    for i, w in enumerate(WINDOWS):
                        s = w // 2
                        pool.tensor_tensor(dst[:, i:4, PAD:PAD + T], src[:, i:4, PAD:PAD + T],
                                           src[:, i:4, PAD - s:PAD - s + T], ALU.add).then_inc(gpsimd_step, 1)
                        pool.wait_ge(gpsimd_step, c(gpsimd_step))
                        src, dst = dst, (pool_2 if dst is pool_1 else pool_1)
                    for i in range(4):
                        s = (pool_1, pool_2)[i % 2]
                        pool.tensor_tensor(s3[:, i, :], s[:, i, PAD:PAD + T],
                                           ca("count").rearrange("p (g t) -> p g t", g=4)[:, i, :], ALU.mult).then_inc(gpsimd_step, 1)
                        pool.wait_ge(gpsimd_step, c(gpsimd_step))
                    pool.tensor_tensor(s3, s3, pool_u[:, :, PAD:PAD + T], ALU.subtract).then_inc(sem_pooled, 1)
                    pool.wait_ge(sem_pooled, c(sem_pooled))
                else:
                    pool.dma_start(param_t[:, 0:WIDTH_PB], a["param_b"][l - DEPTH]).then_inc(param_in, 16)
                    for i, name in enumerate(("ln1_g_2", "ln1_b_2", "ln2_g_2", "ln2_b_2")):
                        pool.dma_start(ln_rows[:, i, :], a[name][l - DEPTH].partition_broadcast(P)).then_inc(norms_in, 16)
                    pool.wait_ge(sem_crowded, c(sem_crowded))
                    full = pool.value_load(crowded, min_val=0, max_val=1)
                    start = branch_state(c, vring, sring)
                    with pool.If(full != 0):
                        make_up(pool, c, start, (*x_rows_in, *y_rows_out, y_rows_in, rows_sent))
                    to_state(c, start, vring, sring)
                    with pool.Else():
                        pool.wait_ge(rows_cleared, 16)
                        for t in range(NT):
                            for j in range(2):
                                pool.indirect_dma_start(
                                    x_rows, bass.IndirectOffsetOnAxis(ap=rows_of[:, 2 * t + j:2 * t + j + 1], axis=0),
                                    x[:, t, :], None).then_inc(rows_sent, 16)
                        pool.wait_ge(rows_sent, 64 * c(rows_sent))
                        for e in range(EXPERTS + 3):
                            if e < EXPERTS:
                                if e >= 3:
                                    pool.wait_ge(sem_rows_turned, c(sem_rows_turned))
                                pool.dma_start(x_in_rows[:, e % 3, :], x_rows[e * P:(e + 1) * P, :])\
                                    .then_inc(x_rows_in[e % 3], 16)
                            if e >= 3:
                                pool.wait_ge(sem_y_out, c(sem_y_out))
                                pool.dma_start(y_rows[(e - 3) * P:(e - 2) * P, :], y_out[:, (e - 3) % 2, :])\
                                    .then_inc(y_rows_out[(e - 3) % 2], 16)
                        for _ in range(3):
                            pool.wait_ge(sem_rows_turned, c(sem_rows_turned))
                        for i in range(2):
                            for _ in range(EXPERTS // 2):
                                c(y_rows_out[i])
                            pool.wait_ge(y_rows_out[i], 16 * c.of[y_rows_out[i].name])
                        for t in range(NT):
                            for j in range(2):
                                pool.indirect_dma_start(
                                    y_in[:, 2 * t + j, :], None, y_rows,
                                    bass.IndirectOffsetOnAxis(ap=rows_of[:, 2 * t + j:2 * t + j + 1], axis=0))\
                                    .then_inc(y_rows_in, 16)
                        make_up(pool, c, start, ())

        @block.tensor
        def _(pe):
            c = Count()
            release = [0]
            nload = [0]

            def mm(out, lhsT, rhs, start=True, stop=True, inc=None):
                ins = nc.tensor.matmul(out, lhsT, rhs, start=start, stop=stop)
                if inc is not None:
                    ins.then_inc(inc, 1)
                elif release[0]:
                    ins.then_inc(slot_used, 1)
                    release[0] -= 1

            def tr(out, in_, ident, inc=None):
                ins = nc.tensor.transpose(out, in_, ident)
                if inc is not None:
                    ins.then_inc(inc, 1)

            def weights():
                i = nload[0]
                nload[0] += 1
                pe.wait_ge(weights_in[i % NSLOT], 16 * arrived[i])
                return slot_view(i)

            def used():
                release[0] += 1

            def channels(ring, w, tiles, m=P, rhs=None):
                for j in range(0, len(tiles), 2):
                    bank = ring.fill(pe)
                    pair = tiles[j:j + 2]
                    for i, lo in enumerate(pair):
                        for k in range(KD):
                            mm(bank[0:m, i * T:(i + 1) * T], w[:, k, lo:lo + m], xT[:, k, :], k == 0, k == KD - 1,
                               ring.full if i == len(pair) - 1 and k == KD - 1 else None)

            def tokens(ring, w, lo, n):
                per = 512 // n
                for t in range(NT):
                    if t % per == 0:
                        bank = ring.fill(pe)
                    for k in range(KD):
                        mm(bank[:, (t % per) * n:(t % per + 1) * n], xT[:, k, t * P:(t + 1) * P], w[:, k, lo:lo + n],
                           k == 0, k == KD - 1, ring.full if (t % per == per - 1 or t == NT - 1) and k == KD - 1 else None)

            def heads(ring, fn, n=H, size=P, rows=P):
                bank = ring.fill(pe)
                for h in range(n):
                    pairs = fn(h)
                    for i, (lhsT, rhs) in enumerate(pairs):
                        mm(bank[0:rows, h * size:h * size + rhs.shape[-1]], lhsT, rhs, i == 0, i == len(pairs) - 1,
                           ring.full if h == n - 1 and i == len(pairs) - 1 else None)

            def column_sums(ring, sq, matrix=None, parts=2):
                for j in range(parts):
                    bank = ring.fill(pe)
                    mm(bank, ones if matrix is None else matrix, sq[:, 2 * j:2 * j + 2, :].rearrange("p a b -> p (a b)"),
                       inc=ring.full)

            def transposed(src, ident):
                for t in range(NT):
                    for j in range(2):
                        bank = vring.fill(pe)
                        for i in range(4):
                            k = 4 * j + i
                            tr(bank[:, i * P:(i + 1) * P], src[:, t, k * P:(k + 1) * P], ident,
                               vring.full if i == 3 else None)

            def attention_scores(t, q_of, k_of):
                nk = (t + 1) * P
                for r in range(2):
                    bank = vring.fill(pe)
                    for h in (r, r + 2):
                        mm(bank[:, (h - r) * P:(h - r) * P + nk], q_of(h)[:, t * P:(t + 1) * P], k_of(h)[:, 0:nk],
                           inc=vring.full if h == r + 2 else None)

            def attention_turn(t, p_of, ident):
                for kt in range(t + 1):
                    bank = sring.fill(pe)
                    for h in range(H):
                        tr(bank[:, h * P:(h + 1) * P], p_of(h)[:, kt * P:(kt + 1) * P], ident,
                           sring.full if h == H - 1 else None)

            pe.wait_ge(sem_ones_ready, 1)
            for l in range(DEPTH):
                ident = ca("ident")
                if l == 0:
                    pe.wait_ge(const_in, 16)
                pe.wait_ge(param_in, 16 * (l + 1))
                pe.wait_ge(sem_x_scaled, c(sem_x_scaled))
                transposed(scaled_x, ident)
                pe.wait_ge(sem_xT_ready, c(sem_xT_ready))
                w = weights()
                channels(sring, w, [0, 64, 128, 192, 256], 64)
                tokens(vring, w, 320, 12)
                used()
                pe.wait_ge(sem_index_raw, c(sem_index_raw))
                for j in (0, 2, 4):
                    bank = vring.fill(pe)
                    n = min(2, 5 - j)
                    mm(bank[0:64, 0:n * T], ca("rot_index", 64)[:, 0:64],
                       idx_raw[0:64, j:j + n, :].rearrange("p a b -> p (a b)"), inc=vring.full)
                for i in range(2):
                    w = weights()
                    channels(sring, w, [0, 128, 256, 384])
                    used()
                    pe.wait_ge(sem_head_squares, c(sem_head_squares))
                    column_sums(sring, s1)
                    pe.wait_ge(sem_head_normed, c(sem_head_normed))
                    for j in (0, 2):
                        bank = vring.fill(pe)
                        mm(bank, ca("rot_head"), s3[:, j:j + 2, :].rearrange("p a b -> p (a b)"), inc=vring.full)
                w = weights()
                tokens(sring, w, 0, 512)
                used()
                w = weights()
                channels(sring, w, [0, 128, 256, 384])
                used()
                pe.wait_ge(sem_index_ready, c(sem_index_ready))
                for t in range(NT):
                    for h0 in (0, 2):
                        bank = sring.fill(pe)
                        for h in (h0, h0 + 1):
                            mm(bank[:, (h - h0) * T:(h - h0) * T + (t + 1) * P], idx[0:64, h, t * P:(t + 1) * P],
                               idx[0:64, 4, 0:(t + 1) * P], inc=sring.full if h == h0 + 1 else None)
                pe.wait_ge(sem_qk_ready, c(sem_qk_ready))
                for t in range(NT):
                    attention_scores(t, lambda h: qa_[:, h, :], lambda h: ka_[:, h, :])
                    pe.wait_ge(sem_probs_ready, c(sem_probs_ready))
                    attention_turn(t, lambda h: logit[:, h, :], ident)
                    pe.wait_ge(sem_probs_turned, c(sem_probs_turned))
                    heads(vring, lambda h: [(va_[:, kt, h * P:(h + 1) * P], pT[:, kt, h * P:(h + 1) * P])
                                            for kt in range(t + 1)])
                w = weights()
                channels(sring, w, [0, 128, 256, 384])
                used()
                w = weights()
                channels(sring, w, [0, 128, 256, 384])
                used()
                pe.wait_ge(sem_pooled, c(sem_pooled))
                for j in (0, 2):
                    bank = vring.fill(pe)
                    for i in (j, j + 1):
                        mm(bank[:, (i - j) * T:(i - j + 1) * T], pa("pool_w")[:, i * P:(i + 1) * P], s3[:, i, :],
                           inc=vring.full if i == j + 1 else None)
                for i in range(3):
                    w = weights()
                    channels(sring, w, [0, 128, 256, 384])
                    used()
                for i in range(2):
                    pe.wait_ge(sem_dn_squares, c(sem_dn_squares))
                    column_sums(sring, s1)
                w = weights()
                channels(sring, w, [0, 128, 256, 384])
                used()
                pe.wait_ge(sem_g_ready, c(sem_g_ready))
                bank = vring.fill(pe)
                for t in range(NT):
                    for j, m in enumerate(("cumsum", "chunk")):
                        mm(bank[:, t * 8 + j * 4:t * 8 + j * 4 + 4], ca(m), g[:, t * H:(t + 1) * H],
                           inc=vring.full if t == NT - 1 and j == 1 else None)
                pe.wait_ge(sem_g_rows, c(sem_g_rows))
                g_row = s3.rearrange("p a b -> p (a b)")
                beta_row = s4.rearrange("p a b -> p (a b)")

                def tile_of(v, t, h):
                    return v[:, h, t * P:(t + 1) * P]
                for t in range(NT):
                    heads(vring, lambda h: [(g_row[:, (t * H + h) * P:(t * H + h + 1) * P], ca("cumsum"))])
                pe.wait_ge(sem_dn_qk_normed, c(sem_dn_qk_normed))
                for t in range(NT):
                    for v in (4, 8):
                        bank = vring.fill(pe)
                        for h in range(H):
                            tr(bank[:, h * P:(h + 1) * P], qkv[:, v + h, t * P:(t + 1) * P], ident,
                               vring.full if h == H - 1 else None)
                for t in range(NT):
                    heads(vring, lambda h: [(qkv[:, 4 + h, t * P:(t + 1) * P], qkv[:, 4 + h, t * P:(t + 1) * P])])
                    heads(vring, lambda h: [(beta_row[:, (t * H + h) * P:(t * H + h + 1) * P], ident)])
                    heads(vring, lambda h: [(qkv[:, 4 + h, t * P:(t + 1) * P], qkv[:, h, t * P:(t + 1) * P])])
                pe.wait_ge(sem_inverse_started, c(sem_inverse_started))
                for t in range(NT):
                    bank = vring.fill(pe)
                    for h in range(H):
                        tr(bank[:, h * P:(h + 1) * P], TT[:, t, h * P:(h + 1) * P], ident, vring.full if h == H - 1 else None)
                for s in range(1, 6):
                    pe.wait_ge(sem_off_block, c(sem_off_block))
                    for t in range(NT):
                        heads(sring, lambda h: [(DT[:, t, h * P:(h + 1) * P], Tm[:, t, h * P:(h + 1) * P])])
                    for t in range(NT):
                        pe.wait_ge(sem_off_times_T, c(sem_off_times_T))
                        heads(vring, lambda h: [(TT[:, t, h * P:(h + 1) * P], X[:, t, h * P:(h + 1) * P])])
                        heads(vring, lambda h: [(X[:, t, h * P:(h + 1) * P], TT[:, t, h * P:(h + 1) * P])])
                pe.wait_ge(sem_inverse_ready, c(sem_inverse_ready))
                for t in range(NT):
                    heads(sring, lambda h: [(TT[:, t, h * P:(h + 1) * P], vbeta[:, t, h * P:(h + 1) * P])])
                    heads(sring, lambda h: [(kbe[:, t, h * P:(h + 1) * P], TT[:, t, h * P:(h + 1) * P])])
                pe.wait_ge(sem_u_w_ready, c(sem_u_w_ready))
                for n in range(T // CHUNK):
                    t, r = n // 2, CHUNK * (n % 2)
                    if n:
                        pe.wait_ge(sem_state_ready, c(sem_state_ready))
                        heads(vring, lambda h: [(X[:, t, h * P:(h + 1) * P], state[:, h, :])])
                    pe.wait_ge(sem_v_new, c(sem_v_new))
                    rows = slice(r, r + CHUNK)

                    def o_parts(h):
                        first = [(state[:, h, :], qe[:, t, h * P + r:h * P + r + CHUNK])] if n else []
                        return first + [(vnew[rows, h, :], attnT[rows, t, h * P + r:h * P + r + CHUNK])]
                    heads(sring, o_parts, size=CHUNK)
                    if n < T // CHUNK - 1:
                        heads(vring, lambda h: [(kdec[rows, t, h * P:(h + 1) * P], vnew[rows, h, :])])
                pe.wait_ge(sem_o_squares, c(sem_o_squares))
                column_sums(sring, s1)
                pe.wait_ge(sem_branches_ready, c(sem_branches_ready))
                for n in range(3):
                    for m in range(KD):
                        if m % 4 == 0:
                            wg = weights()
                        bank = sring.fill(pe)
                        for k in range(KD):
                            mm(bank[:, 0:T], wg[:, k, (m % 4) * P:(m % 4 + 1) * P], xT[:, k, :], k == 0, k == KD - 1,
                               sring.full if k == KD - 1 else None)
                        if m == 0:
                            wbr = weights()
                        if m == 3:
                            used()
                        bank = vring.fill(pe)
                        for k in range(4):
                            mm(bank[:, 0:T], wbr[:, k, m * P:(m + 1) * P], y[:, n, k, :], k == 0, k == 3,
                               vring.full if k == 3 else None)
                    used()
                    used()
                pe.wait_ge(sem_merged_ready, c(sem_merged_ready))
                for cc in range(2):
                    w = weights()
                    for t in range(NT):
                        bank = vring.fill(pe)
                        for k in range(KD):
                            mm(bank, merged[:, k, t * P:(t + 1) * P], w[:, k, :], k == 0, k == KD - 1,
                               vring.full if k == KD - 1 else None)
                    used()

            for l in range(DEPTH):
                ident = cb("ident")
                if l == 0:
                    pe.wait_ge(const_in, 32)
                pe.wait_ge(param_in, 16 * (DEPTH + l + 1))
                pe.wait_ge(sem_layer_out, DEPTH + l)
                transposed(x, ident)
                pe.wait_ge(sem_xT_ready, c(sem_xT_ready))
                w = weights()
                channels(sring, w, [0, 128, 256, 384])
                used()
                w = weights()
                tokens(sring, w, 0, 256)
                channels(sring, w, [256, 384])
                used()
                w = weights()
                channels(sring, w, [0, 128])
                tokens(sring, w, 256, 256)
                used()
                w = weights()
                tokens(vring, w, 0, 4)
                channels(sring, w, [4, 132, 260])
                channels(sring, w, [420 - 96], 96)
                used()
                pe.wait_ge(sem_lora_squares, c(sem_lora_squares))
                bank = sring.fill(pe)
                for i in range(2):
                    mm(bank[:, 0:T], ones, csq[:, i, :], i == 0, i == 1)
                mm(bank[:, T:2 * T], ones, csq[:, 2, :], inc=sring.full)

                def turned_halves(ring, lo=(0, 128, 256, 384)):
                    w = weights()
                    channels(ring, w, lo)
                    used()

                turned_halves(sring)
                pe.wait_ge(sem_logf_ready, c(sem_logf_ready))
                bank = vring.fill(pe)
                mm(bank[:, 0:H], cb("upto"), logf[:, 0, :])
                mm(bank[:, H:2 * H], ones, logf[:, 0, :], True, False)
                mm(bank[:, H:2 * H], cb("upto"), logf[:, 1, :], False, True, vring.full)

                def halves(v, at=0):
                    return lambda h: v[64 * (h % 2):64 * (h % 2) + 64, at + h // 2, :]

                def scores(unit):
                    group, t = divmod(unit, NT)
                    if group == 0:
                        attention_scores(t, halves(foxq), halves(foxk))
                    else:
                        attention_scores(t, lambda h: mq[0:96, h, :], lambda h: mk[0:96, h, :])

                def values(unit):
                    group, t = divmod(unit, NT)
                    pe.wait_ge(sem_probs_ready, c(sem_probs_ready))
                    attention_turn(t, lambda h: prob[:, 4 * (unit % 3) + h, :], ident)
                    pe.wait_ge(sem_probs_turned, c(sem_probs_turned))
                    v = foxv if group == 0 else mv
                    heads(vring, lambda h: [(v[:, kt, (h // 2) * P:(h // 2 + 1) * P], pTb[:, kt, h * P:(h + 1) * P])
                                            for kt in range(t + 1)])

                scores(0)
                pe.wait_ge(sem_lora_normed, c(sem_lora_normed))
                wuq = pb("w_uq").rearrange("p (k n) -> p k n", k=2)
                wukv = pb("w_ukv").rearrange("p (h n) -> p h n", h=H)
                for h0 in (0, 2):
                    heads(sring, lambda h: [(wuq[:, k, (h0 + h) * 96:(h0 + h + 1) * 96], cqkv[:, k, :]) for k in range(2)],
                          2, T, 96)
                for h0 in (0, 2):
                    heads(sring, lambda h: [(wukv[:, h0 + h, 0:64], cqkv[:, 2, :])], 2, T, 64)
                bank = sring.fill(pe)
                for t in range(NT):
                    for h in range(H):
                        mm(bank[:, t * 256 + h * 64:t * 256 + h * 64 + 64], cqkv[:, 2, t * P:(t + 1) * P], wukv[:, h, 64:128],
                           inc=sring.full if t == NT - 1 and h == H - 1 else None)
                pe.wait_ge(sem_logf_rows, c(sem_logf_rows))
                for h0 in (0, 2):
                    bank = sring.fill(pe)
                    for h in (h0, h0 + 1):
                        o = (h - h0) * T
                        mm(bank[:, o:o + P], f_row[:, 0, h, :], cb("upto"))
                        mm(bank[:, o + P:o + T], f_row[:, 0, h, :], ones, True, False)
                        mm(bank[:, o + P:o + T], f_row[:, 1, h, :], cb("upto"), False, True,
                           sring.full if h == h0 + 1 else None)
                for v in (mq, mk):
                    pe.wait_ge(sem_mla_raw, c(sem_mla_raw))
                    for j in (0, 2):
                        bank = vring.fill(pe)
                        mm(bank[0:96, :], cb("rot_mla", 96)[:, 0:96],
                           v[0:96, j:j + 2, :].rearrange("p a b -> p (a b)"), inc=vring.full)
                scores(1)
                turned_halves(sring)
                pe.wait_ge(sem_attention_inputs, c(sem_attention_inputs))
                scores(2)
                values(0)
                turned_halves(sring)
                scores(3)
                values(1)
                w = weights()
                tokens(sring, w, 0, 512)
                used()
                pe.wait_ge(sem_dil_raw, c(sem_dil_raw))
                for v, unit in ((dq, 2), (dk, 3)):
                    if unit == 3:
                        w = weights()
                        tokens(sring, w, 0, 256)
                        used()
                    for j in (0, 2, 4):
                        bank = vring.fill(pe)
                        mm(bank, cb("rot64"), v[:, j:j + 2, :].rearrange("p a b -> p (a b)"), inc=vring.full)
                    values(unit)
                pe.wait_ge(sem_attention_inputs, c(sem_attention_inputs))
                for t in range(NT):
                    for br in range(3):
                        attention_scores(t, halves(dq, 2 * br), halves(dk, 2 * br))
                    if t == 0:
                        for kt in range(NT):
                            for r in range(2):
                                heads(sring, lambda h: [(halves(sbqk, 2)(r + 2 * h)[:, kt * P:(kt + 1) * P],
                                                         halves(sbqk)(r + 2 * h))], 2, T)
                for t in range(NT):
                    p12 = prob if t else prob_0
                    pe.wait_ge(sem_probs_ready, c(sem_probs_ready))
                    for br in range(3):
                        attention_turn(t, lambda h: p12[:, 4 * br + h, :], ident)
                        pe.wait_ge(sem_probs_turned, c(sem_probs_turned))
                        heads(vring, lambda h: [(dv[:, kt, br * 256 + (h // 2) * P:br * 256 + (h // 2 + 1) * P],
                                                 pTb[:, kt, h * P:(h + 1) * P]) for kt in range(t + 1)])
                    if t == 0:
                        pe.wait_ge(sem_log_keep, c(sem_log_keep))
                        for kt in range(NT):
                            for h0 in (0, 2):
                                heads(vring, lambda h: [(cb("after"), slk[:, kt * 4 + h0 + h, :])]
                                      + ([(ones, slk[:, 4 + h0 + h, :])] if kt == 0 else []), 2, T)
                pe.wait_ge(sem_stick_weights, c(sem_stick_weights))
                for h0 in (0, 2):
                    heads(vring, lambda h: [(sbv[:, kt, (h0 // 2) * P:(h0 // 2 + 1) * P], sz[:, kt * 4 + h0 + h, :])
                                            for kt in range(NT)], 2, T)
                pe.wait_ge(sem_o_squares_b, c(sem_o_squares_b))
                column_sums(sring, sq8, cb("pair"), 4)
                pe.wait_ge(sem_o_ready_b, c(sem_o_ready_b))
                for cc in range(2):
                    w = weights()
                    for t in range(NT):
                        bank = vring.fill(pe)
                        for k in range(KD):
                            mm(bank, oall[:, k, t * P:(t + 1) * P], w[:, k, :], k == 0, k == KD - 1,
                               vring.full if k == KD - 1 else None)
                    used()
                pe.wait_ge(sem_x_normed, c(sem_x_normed))
                transposed(x, ident)
                pe.wait_ge(sem_xT_ready, c(sem_xT_ready))
                bank = vring.fill(pe)
                wr = pb("w_router").rearrange("p (k n) -> p k n", k=KD)
                for t in range(NT):
                    for k in range(KD):
                        mm(bank[:, t * 20:(t + 1) * 20], xT[:, k, t * P:(t + 1) * P], wr[:, k, :], k == 0, k == KD - 1,
                           vring.full if t == NT - 1 and k == KD - 1 else None)
                pe.wait_ge(sem_chosen, c(sem_chosen))
                bank = vring.fill(pe)
                both = chosen[:, 2, :]
                mm(bank[:, 0:16], cb("upto"), both[:, 0:16])
                mm(bank[:, 16:32], ones, both[:, 0:16], True, False)
                mm(bank[:, 16:32], cb("upto"), both[:, 16:32], False, True)
                mm(bank[:, 32:48], ones, both[:, 0:16], True, False)
                mm(bank[:, 32:48], ones, both[:, 16:32], False, True, vring.full)
                pe.wait_ge(sem_crowded, c(sem_crowded))
                full = pe.value_load(crowded, min_val=0, max_val=1)
                start, loads_before, pending = branch_state(c, vring, sring), nload[0], release[0]
                with pe.If(full != 0):
                    for e in range(EXPERTS + 1):
                        if e < EXPERTS:
                            w1 = weights()
                            for m in range(4):
                                for ring in (sring, vring):
                                    if m == 0 and ring is vring:
                                        w3 = weights()
                                    w = w1 if ring is sring else w3
                                    bank = ring.fill(pe)
                                    for k in range(KD):
                                        mm(bank[:, 0:T], w[:, k, m * P:(m + 1) * P], xT[:, k, :], k == 0, k == KD - 1,
                                           ring.full if k == KD - 1 else None)
                            used()
                            used()
                        if e:
                            w2 = weights()
                            pe.wait_ge(sem_hidden_ready, c(sem_hidden_ready))
                            for t in range(NT):
                                for cc in range(2):
                                    bank = vring.fill(pe)
                                    for k in range(4):
                                        mm(bank, hh[(e - 1) % 2][:, k, t * P:(t + 1) * P], w2[:, k, cc * 512:(cc + 1) * 512],
                                           k == 0, k == 3, vring.full if k == 3 else None)
                            used()
                    make_up(pe, c, start, (), filled=(vring, sring))
                to_state(c, start, vring, sring)
                nload[0], release[0] = loads_before, pending
                with pe.Else():
                    def turn_rows(e):
                        pe.wait_ge(x_rows_in[e % 3], 16 * c(x_rows_in[e % 3]))
                        for ring in (sring, vring):
                            bank = ring.fill(pe)
                            for i in range(4):
                                k = i + (4 if ring is vring else 0)
                                tr(bank[:, i * P:(i + 1) * P], x_in_rows[:, e % 3, k * P:(k + 1) * P], ident,
                                   ring.full if i == 3 else None)

                    turn_rows(0)
                    for e in range(EXPERTS + 1):
                        if e < EXPERTS:
                            pe.wait_ge(sem_rows_turned_s, c(sem_rows_turned_s))
                            pe.wait_ge(sem_rows_turned, c(sem_rows_turned))
                            for ring in (sring, vring):
                                w = weights()
                                bank = ring.fill(pe)
                                for k in range(KD):
                                    mm(bank, x_turned[:, e % 2, k * P:(k + 1) * P], w[:, k, :], k == 0, k == KD - 1,
                                       ring.full if k == KD - 1 else None)
                                used()
                        if e:
                            pe.wait_ge(sem_h_rows, c(sem_h_rows))
                            bank = sring.fill(pe)
                            for i in range(4):
                                tr(bank[:, i * P:(i + 1) * P], h_rows[:, (e - 1) % 2, i * P:(i + 1) * P], ident,
                                   sring.full if i == 3 else None)
                        if e + 1 < EXPERTS:
                            turn_rows(e + 1)
                        if e:
                            w2 = weights()
                            pe.wait_ge(sem_h_turned, c(sem_h_turned))
                            for cc in range(2):
                                bank = vring.fill(pe)
                                for k in range(4):
                                    mm(bank, h_turned[:, (e - 1) % 2, k * P:(k + 1) * P], w2[:, k, cc * 512:(cc + 1) * 512],
                                       k == 0, k == 3, vring.full if k == 3 else None)
                            used()
                    make_up(pe, c, start, (), filled=(vring, sring))

        @block.scalar
        def _(act):
            c = Count()
            A = nc.scalar.activation

            def move(dst, n=512, rows=P, scale=1.0, event=None):
                bank = sring.take(act)
                A(dst, bank[0:rows, 0:n].rearrange("p (a b) -> p a b", a=dst.shape[1]) if len(dst.shape) == 3
                  else bank[0:rows, 0:n], ACT.Copy, scale=scale).then_inc(sring.empty, 1)
                act.wait_ge(sring.empty, c(sring.empty))
                if event is not None:
                    act.sem_inc(event, 1)
                    c(event)

            def rsqrt_bank(dst, n=512, scale=1.0, bias=None, rows=P):
                bank = sring.take(act)
                A(dst, bank[0:rows, 0:n], ACT.Ln, scale=scale, bias=(eps if bias is None else bias)[0:rows]).then_inc(sring.empty, 1)
                act.wait_ge(sring.empty, c(sring.empty))
                A(dst, dst, ACT.Exp, scale=-0.5).then_inc(scalar_step, 1)
                act.wait_ge(scalar_step, c(scalar_step))

            def flat(v):
                return v.rearrange("p a b -> p (a b)")

            def tables(name):
                act.preload_act_table_set(name)

            def silu_z_in(dst):
                for j in (0, 2):
                    bank = sring.take(act)
                    A(flat(dst[:, j:j + 2, :]), bank, ACT.Silu).then_inc(sring.empty, 1)
                    act.wait_ge(sring.empty, c(sring.empty))
                act.sem_inc(sem_z_ready, 1)
                c(sem_z_ready)

            act.wait_ge(sem_ones_ready, 1)
            act.wait_ge(x_in, 16)
            for l in range(DEPTH):
                tables("natural_log_exp_and_others")
                for t in range(NT):
                    A(flat(s3), x[:, t, :], ACT.Square, accum_out=stat[:, t:t + 1]).then_inc(scalar_step, 1)
                    act.wait_ge(scalar_step, c(scalar_step))
                A(rstd, stat, ACT.Ln, scale=1.0 / D, bias=eps).then_inc(scalar_step, 1)
                act.wait_ge(scalar_step, c(scalar_step))
                A(rstd, rstd, ACT.Exp, scale=-0.5).then_inc(scalar_step, 1)
                act.wait_ge(scalar_step, c(scalar_step))
                sx = scaled_x
                A(sx[:, 0, :], x[:, 0, :], ACT.Copy, scale=rstd[:, 0:1]).then_inc(scalar_step, 1)
                act.wait_ge(scalar_step, c(scalar_step))
                A(sx[:, 1, :], x[:, 1, :], ACT.Copy, scale=rstd[:, 1:2]).then_inc(sem_x_scaled, 1)
                act.wait_ge(sem_x_scaled, c(sem_x_scaled))
                act.wait_ge(param_in, 16 * (l + 1))
                A(exp_a, pa("a_log"), ACT.Exp).then_inc(scalar_step, 1)
                act.wait_ge(scalar_step, c(scalar_step))
                for j in (0, 2, 4):
                    n = min(2, 5 - j)
                    bank = sring.take(act)
                    A(flat(idx_raw[0:64, j:j + n, :]), bank[0:64, 0:n * T], ACT.Copy).then_inc(sring.empty, 1)
                    act.wait_ge(sring.empty, c(sring.empty))
                act.sem_inc(sem_index_raw, 1)
                c(sem_index_raw)
                for i in range(2):
                    if i:
                        act.wait_ge(sem_head_turned, c(sem_head_turned))
                    for j in (0, 2):
                        move(s2[:, j:j + 2, :])
                    A(s1, s2, ACT.Square).then_inc(sem_head_squares, 1)
                    act.wait_ge(sem_head_squares, c(sem_head_squares))
                    for j in (0, 2):
                        rsqrt_bank(flat(s4[:, j:j + 2, :]), scale=1.0 / P)
                    act.sem_inc(sem_head_rstd, 1)
                    c(sem_head_rstd)
                for t in range(NT):
                    move(va_[:, t, :])
                act.wait_ge(sem_head_turned, c(sem_head_turned))
                tables("silu_and_others")
                silu_z_in(silu_z)
                tables("natural_log_exp_and_others")
                for t in range(NT):
                    if t:
                        act.wait_ge(sem_scored, c(sem_scored))
                    for j in (0, 2):
                        bank = sring.take(act)
                        nk = (t + 1) * P
                        A(s1[:, j:j + 2, 0:nk], bank.rearrange("p (a b) -> p a b", a=2)[:, :, 0:nk], ACT.Relu).then_inc(sring.empty, 1)
                        act.wait_ge(sring.empty, c(sring.empty))
                    act.sem_inc(sem_index_dots, 1)
                    c(sem_index_dots)
                for t in range(NT):
                    act.wait_ge(sem_shifted, c(sem_shifted))
                    A(logit[:, :, 0:(t + 1) * P], logit[:, :, 0:(t + 1) * P], ACT.Exp).then_inc(sem_exped, 1)
                    act.wait_ge(sem_exped, c(sem_exped))
                    for kt in range(t + 1):
                        move(pT[:, kt, :])
                    act.sem_inc(sem_probs_turned, 1)
                    c(sem_probs_turned)
                A(pool_u[:, :, 0:PAD], over_mid(ones[:, 0:PAD], 4), ACT.Copy, scale=0.0).then_inc(scalar_step, 1)
                act.wait_ge(scalar_step, c(scalar_step))
                for j in (0, 2):
                    move(pool_u[:, j:j + 2, PAD:PAD + T])
                act.sem_inc(sem_pool_in, 1)
                c(sem_pool_in)
                tables("silu_and_others")
                silu_z_in(s4)
                act.wait_ge(sem_y_pooled, c(sem_y_pooled))
                A(conv_in[:, :, 0:CONV - 1], over_mid(ones[:, 0:CONV - 1], 12), ACT.Copy, scale=0.0).then_inc(scalar_step, 1)
                act.wait_ge(scalar_step, c(scalar_step))
                for i in range(3):
                    for j in (0, 2):
                        move(conv_in[:, 4 * i + j:4 * i + j + 2, CONV - 1:CONV - 1 + T])
                    act.sem_inc(sem_conv_in, 1)
                    c(sem_conv_in)
                for i in range(3):
                    act.wait_ge(sem_convolved, c(sem_convolved))
                    A(qkv[:, 4 * i:4 * i + 4, :], qkv[:, 4 * i:4 * i + 4, :], ACT.Silu).then_inc(scalar_step, 1)
                    act.wait_ge(scalar_step, c(scalar_step))
                tables("natural_log_exp_and_others")
                for i in range(2):
                    A(s1, qkv[:, 4 * i:4 * i + 4, :], ACT.Square).then_inc(sem_dn_squares, 1)
                    act.wait_ge(sem_dn_squares, c(sem_dn_squares))
                    for j in (0, 2):
                        rsqrt_bank(flat(s2[:, j:j + 2, :]))
                    act.sem_inc(sem_dn_rstd, 1)
                    c(sem_dn_rstd)
                    act.wait_ge(sem_dn_normed1, c(sem_dn_normed1))
                tables("silu_and_others")
                silu_z_in(silu_z)
                tables("natural_log_exp_and_others")
                act.wait_ge(sem_beta_inputs, c(sem_beta_inputs))
                z8 = [tmp8[:, i, :] for i in range(4)]
                A(z8[0], z8[0], ACT.Exp, scale=-1.0).then_inc(scalar_step, 1)
                act.wait_ge(scalar_step, c(scalar_step))
                A(z8[2], z8[1], ACT.Abs).then_inc(scalar_step, 1)
                act.wait_ge(scalar_step, c(scalar_step))
                A(z8[2], z8[2], ACT.Exp, scale=-1.0).then_inc(scalar_step, 1)
                act.wait_ge(scalar_step, c(scalar_step))
                A(z8[2], z8[2], ACT.Ln, bias=ones[:, 0:1]).then_inc(sem_beta_exps, 1)
                act.wait_ge(sem_beta_exps, c(sem_beta_exps))
                act.wait_ge(sem_gc_ready, c(sem_gc_ready))
                A(kb_scale, kb_scale, ACT.Exp).then_inc(scalar_step, 1)
                act.wait_ge(scalar_step, c(scalar_step))
                A(kd_scale, kd_scale, ACT.Exp).then_inc(sem_gc_exps, 1)
                act.wait_ge(sem_gc_exps, c(sem_gc_exps))
                for t in range(NT):
                    act.wait_ge(sem_decay_logs, c(sem_decay_logs))
                    A(DT[:, t, :], DT[:, t, :], ACT.Exp).then_inc(scalar_step, 1)
                    act.wait_ge(scalar_step, c(scalar_step))
                    A(expg[:, t, :], expg[:, t, :], ACT.Exp).then_inc(sem_decays, 1)
                    act.wait_ge(sem_decays, c(sem_decays))
                for s in range(1, 6):
                    for t in range(NT):
                        move(X[:, t, :], event=sem_off_times_T)
                for t in range(NT):
                    move(Tm[:, t, :])
                    move(X[:, t, :])
                act.sem_inc(sem_u_w_ready, 1)
                c(sem_u_w_ready)
                for n in range(T // CHUNK):
                    bank = sring.take(act)
                    A(oT[:, :, n * CHUNK:(n + 1) * CHUNK], bank[:, 0:H * CHUNK].rearrange("p (a b) -> p a b", a=H),
                      ACT.Copy).then_inc(sring.empty, 1)
                    act.wait_ge(sring.empty, c(sring.empty))
                A(s1, oT, ACT.Square).then_inc(sem_o_squares, 1)
                act.wait_ge(sem_o_squares, c(sem_o_squares))
                for j in (0, 2):
                    rsqrt_bank(flat(s2[:, j:j + 2, :]), scale=1.0 / P)
                act.sem_inc(sem_o_rstd, 1)
                c(sem_o_rstd)
                tables("sigmoid_and_others")
                for n in range(3):
                    for m in range(KD):
                        i = n * KD + m
                        if i == 0:
                            act.wait_ge(sem_o_scaled, c(sem_o_scaled))
                        if i >= 2:
                            act.wait_ge(sem_gate_used, c(sem_gate_used))
                        bank = sring.take(act)
                        A(msig[:, i % 2, :], bank[:, 0:T], ACT.Sigmoid, bias=pa("gate_b")[:, i:i + 1]).then_inc(sring.empty, 1)
                        act.wait_ge(sring.empty, c(sring.empty))
                        act.sem_inc(sem_gate_sigmoid, 1)
                        c(sem_gate_sigmoid)
                for _ in range(2):
                    act.wait_ge(sem_gate_used, c(sem_gate_used))
                act.wait_ge(sem_layer_out, c(sem_layer_out))

            for l in range(DEPTH):
                tables("natural_log_exp_and_others")
                for j in (0, 2):
                    move(sbqk[:, j:j + 2, :])
                move(sbv)
                move(foxq)
                move(foxk)
                move(foxv)
                move(cqkv[:, 0:2, :])
                bank = sring.take(act)
                A(cqkv[:, 2, :], bank[:, 0:T], ACT.Copy).then_inc(sring.empty, 1)
                act.wait_ge(sring.empty, c(sring.empty))
                bank = sring.take(act)
                A(mk[64:96, :, :], bank[64:96, 0:T].unsqueeze(1).to_broadcast([32, H, T]), ACT.Copy).then_inc(sring.empty, 1)
                act.wait_ge(sring.empty, c(sring.empty))
                A(csq[:, 0:3, :], cqkv, ACT.Square).then_inc(sem_lora_squares, 1)
                act.wait_ge(sem_lora_squares, c(sem_lora_squares))
                act.wait_ge(sem_forget_inputs, c(sem_forget_inputs))
                z8 = [tmp8[:, i, :] for i in range(4)]
                A(z8[1], z8[0], ACT.Abs).then_inc(scalar_step, 1)
                act.wait_ge(scalar_step, c(scalar_step))
                A(z8[1], z8[1], ACT.Exp, scale=-1.0).then_inc(scalar_step, 1)
                act.wait_ge(scalar_step, c(scalar_step))
                A(z8[1], z8[1], ACT.Ln, bias=ones[:, 0:1]).then_inc(sem_forget_exps, 1)
                act.wait_ge(sem_forget_exps, c(sem_forget_exps))
                bank = sring.take(act)
                A(crs[:, 0, :], bank[:, 0:T], ACT.Ln, scale=1.0 / 256, bias=eps).then_inc(scalar_step, 1)
                act.wait_ge(scalar_step, c(scalar_step))
                A(crs[:, 1, :], bank[:, T:2 * T], ACT.Ln, scale=1.0 / 128, bias=eps).then_inc(sring.empty, 1)
                act.wait_ge(sring.empty, c(sring.empty))
                A(crs[:, 0:2, :], crs[:, 0:2, :], ACT.Exp, scale=-0.5).then_inc(sem_lora_rstd, 1)
                act.wait_ge(sem_lora_rstd, c(sem_lora_rstd))
                for j in (0, 2):
                    move(dq[:, j:j + 2, :])
                for j in (0, 2):
                    move(mq[0:96, j:j + 2, :], rows=96)
                act.sem_inc(sem_mla_raw, 1)
                c(sem_mla_raw)
                for j in (0, 2):
                    move(mk[0:64, j:j + 2, :], rows=64)
                act.sem_inc(sem_mla_raw, 1)
                c(sem_mla_raw)
                move(mv)
                for j in (0, 2):
                    move(cdiff[:, j:j + 2, :])
                act.sem_inc(sem_forget_rows, 1)
                c(sem_forget_rows)

                def exps(p):
                    act.wait_ge(sem_shifted, c(sem_shifted))
                    A(p, p, ACT.Exp).then_inc(sem_exped, 1)
                    act.wait_ge(sem_exped, c(sem_exped))

                def probs_turned(t):
                    for kt in range(t + 1):
                        move(pTb[:, kt, :])
                    act.sem_inc(sem_probs_turned, 1)
                    c(sem_probs_turned)

                def unit_exps(unit):
                    exps(prob[:, 4 * (unit % 3):4 * (unit % 3) + 4, 0:(unit % NT + 1) * P])

                unit_exps(0)
                unit_exps(1)
                move(dq[:, 4:6, :])
                move(dk[:, 0:2, :])
                probs_turned(0)
                unit_exps(2)
                move(dk[:, 2:4, :])
                move(dk[:, 4:6, :])
                act.sem_inc(sem_dil_raw, 1)
                c(sem_dil_raw)
                probs_turned(1)
                unit_exps(3)
                for t in range(NT):
                    move(dv[:, t, 0:512])
                probs_turned(0)
                move(dv[:, :, 512:768])
                probs_turned(1)
                for t in range(NT):
                    for br in range(3):
                        exps((prob if t else prob_0)[:, 4 * br:4 * br + 4, 0:(t + 1) * P])
                    if t == 0:
                        act.wait_ge(sem_prob_free, c(sem_prob_free))
                        for i in range(4):
                            kt, r = i // 2, i % 2
                            move(sz[:, 4 * kt + r:4 * kt + 4:2, :], scale=0.125)
                        A(sp, sz, ACT.Abs).then_inc(scalar_step, 1)
                        act.wait_ge(scalar_step, c(scalar_step))
                        A(sp, sp, ACT.Exp, scale=-1.0).then_inc(scalar_step, 1)
                        act.wait_ge(scalar_step, c(scalar_step))
                        A(sp, sp, ACT.Ln, bias=ones[:, 0:1]).then_inc(sem_stick_logs, 1)
                        act.wait_ge(sem_stick_logs, c(sem_stick_logs))
                for t in range(NT):
                    act.wait_ge(sem_dens, c(sem_dens))
                    A(lse, rowsum, ACT.Ln).then_inc(sem_log_dens, 1)
                    act.wait_ge(sem_log_dens, c(sem_log_dens))
                    act.wait_ge(sem_mix_shifted, c(sem_mix_shifted))
                    A(mixw, mixw, ACT.Exp).then_inc(sem_mix_exps, 1)
                    act.wait_ge(sem_mix_exps, c(sem_mix_exps))
                    for br in range(3):
                        probs_turned(t)
                act.wait_ge(sem_stick_sum, c(sem_stick_sum))
                A(sz, sz, ACT.Exp).then_inc(sem_stick_exp, 1)
                act.wait_ge(sem_stick_exp, c(sem_stick_exp))
                act.wait_ge(sem_o_all, c(sem_o_all))
                A(sq8, oall, ACT.Square).then_inc(sem_o_squares_b, 1)
                act.wait_ge(sem_o_squares_b, c(sem_o_squares_b))
                for j in range(4):
                    rsqrt_bank(flat(crs8[:, 2 * j:2 * j + 2, :]), scale=1.0 / 64)
                act.sem_inc(sem_o_rstd_b, 1)
                c(sem_o_rstd_b)
                for part in range(2):
                    act.wait_ge(sem_centred, c(sem_centred))
                    for t in range(NT):
                        A(sq_scr, xc[:, t, :], ACT.Square, accum_out=stat[:, t:t + 1]).then_inc(scalar_step, 1)
                        act.wait_ge(scalar_step, c(scalar_step))
                    A(rstd, stat, ACT.Ln, scale=1.0 / D, bias=eps5).then_inc(scalar_step, 1)
                    act.wait_ge(scalar_step, c(scalar_step))
                    A(rstd, rstd, ACT.Exp, scale=-0.5).then_inc(sem_ln_rstd, 1)
                    act.wait_ge(sem_ln_rstd, c(sem_ln_rstd))
                    if part:
                        break
                    act.wait_ge(sem_group_shifted, c(sem_group_shifted))
                    A(rt[:, 1, 0:8], rt[:, 1, 0:8], ACT.Exp).then_inc(sem_group_exps, 1)
                    act.wait_ge(sem_group_exps, c(sem_group_exps))
                    act.wait_ge(sem_pair_shifted, c(sem_pair_shifted))
                    A(rt[:, 9, 0:2], rt[:, 9, 0:2], ACT.Exp).then_inc(sem_pair_exps, 1)
                    act.wait_ge(sem_pair_exps, c(sem_pair_exps))
                    tables("silu_and_others")
                    act.wait_ge(sem_crowded, c(sem_crowded))
                    full = act.value_load(crowded, min_val=0, max_val=1)
                    start = branch_state(c, vring, sring)
                    with act.If(full != 0):
                        for e in range(EXPERTS):
                            if e >= 2:
                                act.wait_ge(sem_hidden_used, c(sem_hidden_used))
                            for m in range(4):
                                bank = sring.take(act)
                                A(hh[e % 2][:, m, :], bank[:, 0:T], ACT.Silu).then_inc(sring.empty, 1)
                                act.wait_ge(sring.empty, c(sring.empty))
                                act.sem_inc(sem_hidden_silu, 1)
                                c(sem_hidden_silu)
                        for _ in range(2):
                            act.wait_ge(sem_hidden_used, c(sem_hidden_used))
                        make_up(act, c, start, (sem_hidden_silu, sem_rows_turned_s, sem_h_turned), emptied=(sring,))
                    to_state(c, start, vring, sring)
                    with act.Else():
                        def turned_in(e):
                            bank = sring.take(act)
                            A(x_turned[:, e % 2, 0:512], bank, ACT.Copy).then_inc(sring.empty, 1)
                            act.wait_ge(sring.empty, c(sring.empty))
                            act.sem_inc(sem_rows_turned_s, 1)
                            c(sem_rows_turned_s)

                        turned_in(0)
                        for e in range(EXPERTS + 1):
                            if e < EXPERTS:
                                bank = sring.take(act)
                                if e >= 2:
                                    act.wait_ge(sem_h_rows, c(sem_h_rows))
                                A(h_silu[:, e % 2, :], bank, ACT.Silu).then_inc(sring.empty, 1)
                                act.wait_ge(sring.empty, c(sring.empty))
                                act.sem_inc(sem_hidden_silu, 1)
                                c(sem_hidden_silu)
                            if e:
                                bank = sring.take(act)
                                A(h_turned[:, (e - 1) % 2, :], bank, ACT.Copy).then_inc(sring.empty, 1)
                                act.wait_ge(sring.empty, c(sring.empty))
                                act.sem_inc(sem_h_turned, 1)
                                c(sem_h_turned)
                            if e + 1 < EXPERTS:
                                turned_in(e + 1)
                        for _ in range(2):
                            act.wait_ge(sem_h_rows, c(sem_h_rows))
                        make_up(act, c, start, (sem_hidden_silu, sem_rows_turned_s, sem_h_turned), emptied=(sring,))
                    tables("natural_log_exp_and_others")
                act.wait_ge(sem_layer_out, c(sem_layer_out))

        @block.vector
        def _(dve):
            c = Count()
            V = nc.vector
            V.memset(ones, 1.0).then_inc(vector_step, 1)
            dve.wait_ge(vector_step, c(vector_step))
            V.memset(eps, 1e-6).then_inc(vector_step, 1)
            dve.wait_ge(vector_step, c(vector_step))
            V.memset(eps5, 1e-5).then_inc(sem_ones_ready, 1)
            dve.wait_ge(sem_ones_ready, c(sem_ones_ready))

            def take2(fn, rows=P, n=512):
                bank = vring.take(dve)
                fn(bank[0:rows, 0:n]).then_inc(vring.empty, 1)
                dve.wait_ge(vring.empty, c(vring.empty))

            def split(bank, n=2):
                return bank.rearrange("p (a b) -> p a b", a=n)

            def turn(dst, src, cos, sin, tiles, rows=P, group=2):
                V.tensor_tensor(dst[0:rows], src[0:rows], over_mid(cos, tiles), ALU.mult).then_inc(vector_step, 1)
                dve.wait_ge(vector_step, c(vector_step))
                for j in range(0, tiles, 2):
                    n = min(2, tiles - j)
                    bank = vring.take(dve)
                    tmp = turn_tmp[0:rows, 0:n, :]
                    V.tensor_tensor(tmp, split(bank[0:rows, 0:n * T], n), over_mid(sin, n), ALU.mult).then_inc(vring.empty, 1)
                    dve.wait_ge(vring.empty, c(vring.empty))
                    V.tensor_tensor(dst[0:rows, j:j + n, :], dst[0:rows, j:j + n, :], tmp, ALU.add).then_inc(vector_step, 1)
                    dve.wait_ge(vector_step, c(vector_step))

            def softmax_logits(dst, t, scale, mask, more=None):
                nk = (t + 1) * P
                for j in range(2):
                    bank = vring.take(dve)
                    V.scalar_tensor_tensor(out=dst[:, j:4:2, 0:nk], in0=split(bank)[:, :, 0:nk], scalar=scale,
                                           in1=over_mid(mask[:, 0:nk], 2) if more is None else more[:, j:4:2, 0:nk],
                                           op0=ALU.mult, op1=ALU.add).then_inc(vring.empty, 1)
                    dve.wait_ge(vring.empty, c(vring.empty))
                if more is not None:
                    V.tensor_tensor(dst[:, 0:4, 0:nk], dst[:, 0:4, 0:nk], over_mid(mask[:, 0:nk], 4), ALU.add).then_inc(vector_step, 1)
                    dve.wait_ge(vector_step, c(vector_step))

            def shift(dst, nk, m):
                V.tensor_reduce(m, dst[:, 0:4, 0:nk], AX.X, ALU.max).then_inc(vector_step, 1)
                dve.wait_ge(vector_step, c(vector_step))
                V.tensor_tensor(dst[:, 0:4, 0:nk], dst[:, 0:4, 0:nk], over_last(m, nk), ALU.subtract).then_inc(sem_shifted, 1)
                dve.wait_ge(sem_shifted, c(sem_shifted))

            def normalise(dst, nk, s):
                dve.wait_ge(sem_exped, c(sem_exped))
                V.tensor_reduce(s, dst[:, 0:4, 0:nk], AX.X, ALU.add).then_inc(vector_step, 1)
                dve.wait_ge(vector_step, c(vector_step))
                V.reciprocal(s, s).then_inc(vector_step, 1)
                dve.wait_ge(vector_step, c(vector_step))
                V.tensor_tensor(dst[:, 0:4, 0:nk], dst[:, 0:4, 0:nk], over_last(s, nk), ALU.mult).then_inc(sem_probs_ready, 1)
                dve.wait_ge(sem_probs_ready, c(sem_probs_ready))

            dve.wait_ge(const_in, 16)
            for l in range(DEPTH):
                dve.wait_ge(param_in, 16 * (l + 1))
                for t in range(NT):
                    for j in range(2):
                        bank = vring.take(dve)
                        V.tensor_tensor(xT[:, 4 * j:4 * j + 4, t * P:(t + 1) * P], split(bank, 4),
                                        over_last(pa("norm_g")[:, 4 * j:4 * j + 4], P), ALU.mult).then_inc(vring.empty, 1)
                        dve.wait_ge(vring.empty, c(vring.empty))
                dve.sem_inc(sem_xT_ready, 1)
                c(sem_xT_ready)
                bank = vring.take(dve)
                V.tensor_copy(ba, split(bank[:, 0:24])).then_inc(vring.empty, 1)
                dve.wait_ge(vring.empty, c(vring.empty))
                V.tensor_scalar(wi, ba[:, :, 0:H], 1.0 / 16.0, None, ALU.mult).then_inc(vector_step, 1)
                dve.wait_ge(vector_step, c(vector_step))
                turn_tmp = s3
                dve.wait_ge(sem_index_raw, c(sem_index_raw))
                turn(idx, idx_raw, ca("cos_index", 64), ca("sin_index", 64), 5, 64)
                dve.sem_inc(sem_index_ready, 1)
                c(sem_index_ready)
                for i, (dst, gain) in enumerate(((qa_, "q_norm"), (ka_, "k_norm"))):
                    dve.wait_ge(sem_head_rstd, c(sem_head_rstd))
                    V.scalar_tensor_tensor(out=s3, in0=s2, scalar=pa(gain), in1=s4, op0=ALU.mult, op1=ALU.mult).then_inc(sem_head_normed, 1)
                    dve.wait_ge(sem_head_normed, c(sem_head_normed))
                    turn_tmp = logit
                    turn(dst, s3, ca("cos_head"), ca("sin_head"), 4)
                    dve.sem_inc(sem_head_turned, 1)
                    c(sem_head_turned)
                    if i:
                        dve.sem_inc(sem_qk_ready, 1)
                        c(sem_qk_ready)
                causal = ca("causal").rearrange("p (t k) -> p t k", t=NT)
                for t in range(NT):
                    nk = (t + 1) * P
                    dve.wait_ge(sem_index_dots, c(sem_index_dots))
                    V.tensor_scalar(score[:, 0:nk], s1[:, 0, 0:nk], wi[:, t, 0:1], None, ALU.mult).then_inc(vector_step, 1)
                    dve.wait_ge(vector_step, c(vector_step))
                    for h in range(1, H):
                        V.scalar_tensor_tensor(out=score[:, 0:nk], in0=s1[:, h, 0:nk], scalar=wi[:, t, h:h + 1],
                                               in1=score[:, 0:nk], op0=ALU.mult, op1=ALU.add).then_inc(vector_step, 1)
                        dve.wait_ge(vector_step, c(vector_step))
                    V.tensor_tensor(score[:, 0:nk], score[:, 0:nk], causal[:, t, 0:nk], ALU.add).then_inc(vector_step, 1)
                    dve.wait_ge(vector_step, c(vector_step))
                    if t == 0:
                        dve.sem_inc(sem_scored, 1)
                        c(sem_scored)
                    for r in range(TOPK // 8):
                        V.max(best, score[:, 0:nk]).then_inc(vector_step, 1)
                        dve.wait_ge(vector_step, c(vector_step))
                        V.match_replace(out=score[:, 0:nk], in_to_replace=best, in_values=score[:, 0:nk],
                                        imm_value=TAKEN).then_inc(vector_step, 1)
                        dve.wait_ge(vector_step, c(vector_step))
                    V.tensor_scalar(sel[:, t, 0:nk], score[:, 0:nk], -2.0e38, NEG, ALU.is_ge, ALU.mult).then_inc(vector_step, 1)
                    dve.wait_ge(vector_step, c(vector_step))
                    V.tensor_tensor(sel[:, t, 0:nk], sel[:, t, 0:nk], causal[:, t, 0:nk], ALU.add).then_inc(vector_step, 1)
                    dve.wait_ge(vector_step, c(vector_step))
                dve.wait_ge(sem_z_ready, c(sem_z_ready))
                for t in range(NT):
                    nk = (t + 1) * P
                    softmax_logits(logit, t, float(P) ** -0.5, sel[:, t, :])
                    shift(logit, nk, rowmax[:, 0:4])
                    normalise(logit, nk, rowsum[:, 0:4])
                    bank = vring.take(dve)
                    V.tensor_tensor(y[:, 2, :, t * P:(t + 1) * P], split(bank, 4), silu_z[:, :, t * P:(t + 1) * P],
                                    ALU.mult).then_inc(vring.empty, 1)
                    dve.wait_ge(vring.empty, c(vring.empty))
                dve.wait_ge(sem_z_ready, c(sem_z_ready))
                for j in (0, 2):
                    bank = vring.take(dve)
                    V.tensor_tensor(y[:, 1, j:j + 2, :], split(bank), s4[:, j:j + 2, :], ALU.mult).then_inc(vring.empty, 1)
                    dve.wait_ge(vring.empty, c(vring.empty))
                V.tensor_tensor(y[:, 1, :, :], y[:, 1, :, :], over_last(pa("pool_scale"), T), ALU.mult).then_inc(sem_y_pooled, 1)
                dve.wait_ge(sem_y_pooled, c(sem_y_pooled))
                for i in range(3):
                    dve.wait_ge(sem_conv_in, c(sem_conv_in))
                    for m in range(4 * i, 4 * i + 4):
                        cw = pa("conv_w")[:, CONV * m:CONV * m + CONV]
                        V.tensor_scalar(qkv[:, m, :], conv_in[:, m, 0:T], cw[:, 0:1], None, ALU.mult).then_inc(vector_step, 1)
                        dve.wait_ge(vector_step, c(vector_step))
                        for j in range(1, CONV):
                            V.scalar_tensor_tensor(out=qkv[:, m, :], in0=conv_in[:, m, j:j + T],
                                                   scalar=cw[:, j:j + 1], in1=qkv[:, m, :],
                                                   op0=ALU.mult, op1=ALU.add).then_inc(vector_step, 1)
                            dve.wait_ge(vector_step, c(vector_step))
                    dve.sem_inc(sem_convolved, 1)
                    c(sem_convolved)
                for i in range(2):
                    dve.wait_ge(sem_dn_rstd, c(sem_dn_rstd))
                    v = qkv[:, 4 * i:4 * i + 4, :]
                    V.scalar_tensor_tensor(out=v, in0=v, scalar=float(P) ** -0.5 if i == 0 else 1.0, in1=s2,
                                           op0=ALU.mult, op1=ALU.mult).then_inc(sem_dn_normed1, 1)
                    dve.wait_ge(sem_dn_normed1, c(sem_dn_normed1))
                dve.sem_inc(sem_dn_qk_normed, 1)
                c(sem_dn_qk_normed)
                z8 = [tmp8[:, i, :] for i in range(4)]
                V.tensor_copy(split(z8[0]), ba[:, :, 4:8]).then_inc(vector_step, 1)
                dve.wait_ge(vector_step, c(vector_step))
                V.tensor_tensor(split(z8[1]), ba[:, :, 8:12], over_mid(pa("dt_bias"), NT), ALU.add).then_inc(sem_beta_inputs, 1)
                dve.wait_ge(sem_beta_inputs, c(sem_beta_inputs))
                dve.wait_ge(sem_beta_exps, c(sem_beta_exps))
                V.tensor_scalar(z8[0], z8[0], 1.0, None, ALU.add).then_inc(vector_step, 1)
                dve.wait_ge(vector_step, c(vector_step))
                V.reciprocal(beta, z8[0]).then_inc(vector_step, 1)
                dve.wait_ge(vector_step, c(vector_step))
                V.scalar_tensor_tensor(out=z8[1], in0=z8[1], scalar=0.0, in1=z8[2], op0=ALU.max, op1=ALU.add).then_inc(vector_step, 1)
                dve.wait_ge(vector_step, c(vector_step))
                V.scalar_tensor_tensor(out=split(g), in0=split(z8[1]), scalar=-1.0, in1=over_mid(exp_a, NT),
                                       op0=ALU.mult, op1=ALU.mult).then_inc(sem_g_ready, 1)
                dve.wait_ge(sem_g_ready, c(sem_g_ready))
                bank = vring.take(dve)
                V.tensor_copy(gc, split(bank[:, 0:16])).then_inc(vring.empty, 1)
                dve.wait_ge(vring.empty, c(vring.empty))
                V.tensor_copy(s3.rearrange("p a (b c) -> p (a b) c", c=P), over_last(g, P)).then_inc(vector_step, 1)
                dve.wait_ge(vector_step, c(vector_step))
                V.tensor_copy(s4.rearrange("p a (b c) -> p (a b) c", c=P), over_last(beta, P)).then_inc(sem_g_rows, 1)
                dve.wait_ge(sem_g_rows, c(sem_g_rows))
                V.tensor_copy(split(kb_scale), gc[:, :, 0:4]).then_inc(vector_step, 1)
                dve.wait_ge(vector_step, c(vector_step))
                V.tensor_tensor(split(kd_scale), gc[:, :, 4:8], gc[:, :, 0:4], ALU.subtract).then_inc(sem_gc_ready, 1)
                dve.wait_ge(sem_gc_ready, c(sem_gc_ready))
                dve.wait_ge(sem_gc_exps, c(sem_gc_exps))
                V.tensor_tensor(kb_scale, kb_scale, beta, ALU.mult).then_inc(vector_step, 1)
                dve.wait_ge(vector_step, c(vector_step))
                for t in range(NT):
                    bank = vring.take(dve)
                    V.tensor_copy(expg[:, t, :], bank).then_inc(vring.empty, 1)
                    dve.wait_ge(vring.empty, c(vring.empty))
                    dt4, eg4 = split(DT[:, t, :], 4), split(expg[:, t, :], 4)
                    V.tensor_tensor(dt4, eg4, over_last(gc[:, t, 0:4], P), ALU.subtract).then_inc(vector_step, 1)
                    dve.wait_ge(vector_step, c(vector_step))
                    V.tensor_tensor(dt4, dt4, over_mid(ca("later"), 4), ALU.add).then_inc(sem_decay_logs, 1)
                    dve.wait_ge(sem_decay_logs, c(sem_decay_logs))
                for t in range(NT):
                    h4 = slice(t * H, (t + 1) * H)
                    bank = vring.take(dve)
                    V.tensor_tensor(split(kbe[:, t, :], 4), split(bank, 4), over_last(kb_scale[:, h4], P), ALU.mult).then_inc(vector_step, 1)
                    dve.wait_ge(vector_step, c(vector_step))
                    V.tensor_tensor(split(kdec[:, t, :], 4), split(bank, 4), over_last(kd_scale[:, h4], P), ALU.mult).then_inc(vring.empty, 1)
                    dve.wait_ge(vring.empty, c(vring.empty))
                    bank = vring.take(dve)
                    V.tensor_tensor(split(vbeta[:, t, :], 4), split(bank, 4), over_last(beta[:, h4], P), ALU.mult).then_inc(vring.empty, 1)
                    dve.wait_ge(vring.empty, c(vring.empty))
                for t in range(NT):
                    dve.wait_ge(sem_decays, c(sem_decays))
                    V.tensor_tensor(split(qe[:, t, :], 4), qkv[:, 0:4, t * P:(t + 1) * P], split(expg[:, t, :], 4), ALU.mult).then_inc(vector_step, 1)
                    dve.wait_ge(vector_step, c(vector_step))
                    bank = vring.take(dve)
                    V.tensor_tensor(U[:, t, :], bank, DT[:, t, :], ALU.mult).then_inc(vring.empty, 1)
                    dve.wait_ge(vring.empty, c(vring.empty))
                    V.tensor_tensor(split(U[:, t, :], 4), split(U[:, t, :], 4), over_mid(ca("strict"), 4), ALU.mult).then_inc(vector_step, 1)
                    dve.wait_ge(vector_step, c(vector_step))
                    bank = vring.take(dve)
                    V.tensor_tensor(U[:, t, :], bank, U[:, t, :], ALU.mult).then_inc(vring.empty, 1)
                    dve.wait_ge(vring.empty, c(vring.empty))
                    bank = vring.take(dve)
                    V.tensor_tensor(attnT[:, t, :], bank, DT[:, t, :], ALU.mult).then_inc(vring.empty, 1)
                    dve.wait_ge(vring.empty, c(vring.empty))
                merge = ca("merge").rearrange("p (s c) -> p s c", s=6)
                for t in range(NT):
                    tt = split(TT[:, t, :], 4)
                    V.tensor_tensor(tt, split(U[:, t, :], 4), over_mid(merge[:, 0, :], 4), ALU.mult).then_inc(vector_step, 1)
                    dve.wait_ge(vector_step, c(vector_step))
                    V.tensor_tensor(tt, over_mid(ca("ident"), 4), tt, ALU.subtract).then_inc(vector_step, 1)
                    dve.wait_ge(vector_step, c(vector_step))
                dve.sem_inc(sem_inverse_started, 1)
                c(sem_inverse_started)
                for t in range(NT):
                    bank = vring.take(dve)
                    V.tensor_copy(Tm[:, t, :], bank).then_inc(vring.empty, 1)
                    dve.wait_ge(vring.empty, c(vring.empty))
                for s in range(1, 6):
                    for t in range(NT):
                        V.tensor_tensor(split(DT[:, t, :], 4), split(U[:, t, :], 4), over_mid(merge[:, s, :], 4), ALU.mult).then_inc(vector_step, 1)
                        dve.wait_ge(vector_step, c(vector_step))
                    dve.sem_inc(sem_off_block, 1)
                    c(sem_off_block)
                    for t in range(NT):
                        bank = vring.take(dve)
                        V.tensor_tensor(Tm[:, t, :], Tm[:, t, :], bank, ALU.subtract).then_inc(vring.empty, 1)
                        dve.wait_ge(vring.empty, c(vring.empty))
                        bank = vring.take(dve)
                        V.tensor_tensor(TT[:, t, :], TT[:, t, :], bank, ALU.subtract).then_inc(vring.empty, 1)
                        dve.wait_ge(vring.empty, c(vring.empty))
                dve.sem_inc(sem_inverse_ready, 1)
                c(sem_inverse_ready)
                for n in range(T // CHUNK):
                    t, r = n // 2, CHUNK * (n % 2)
                    rows = slice(r, r + CHUNK)
                    if n == 0:
                        dve.wait_ge(sem_u_w_ready, c(sem_u_w_ready))
                        V.tensor_copy(vnew[rows], split(Tm[rows, t, :], 4)).then_inc(sem_v_new, 1)
                        dve.wait_ge(sem_v_new, c(sem_v_new))
                    else:
                        bank = vring.take(dve)
                        V.tensor_tensor(vnew[rows], split(Tm[rows, t, :], 4), split(bank[rows], 4), ALU.subtract).then_inc(vring.empty, 1)
                        dve.wait_ge(vring.empty, c(vring.empty))
                        dve.sem_inc(sem_v_new, 1)
                        c(sem_v_new)
                        if n == T // CHUNK - 1:
                            break
                        last = split(expg[:, t, :], 4)[:, :, r + CHUNK - 1]
                        bank = vring.take(dve)
                        V.tensor_tensor(state, state, over_last(last, P), ALU.mult).then_inc(vector_step, 1)
                        dve.wait_ge(vector_step, c(vector_step))
                        V.tensor_tensor(state, state, split(bank, 4), ALU.add).then_inc(vring.empty, 1)
                        dve.wait_ge(vring.empty, c(vring.empty))
                        dve.sem_inc(sem_state_ready, 1)
                        c(sem_state_ready)
                        continue
                    bank = vring.take(dve)
                    V.tensor_copy(state, split(bank, 4)).then_inc(vring.empty, 1)
                    dve.wait_ge(vring.empty, c(vring.empty))
                    dve.sem_inc(sem_state_ready, 1)
                    c(sem_state_ready)
                dve.wait_ge(sem_z_ready, c(sem_z_ready))
                dve.wait_ge(sem_o_rstd, c(sem_o_rstd))
                V.scalar_tensor_tensor(out=oT, in0=oT, scalar=pa("o_norm"), in1=s2, op0=ALU.mult, op1=ALU.mult).then_inc(vector_step, 1)
                dve.wait_ge(vector_step, c(vector_step))
                V.tensor_tensor(y[:, 0, :, :], oT, silu_z, ALU.mult).then_inc(sem_branches_ready, 1)
                dve.wait_ge(sem_branches_ready, c(sem_branches_ready))
                dve.sem_inc(sem_o_scaled, 1)
                c(sem_o_scaled)
                for n in range(3):
                    for m in range(KD):
                        i = n * KD + m
                        dve.wait_ge(sem_gate_sigmoid, c(sem_gate_sigmoid))
                        bank = vring.take(dve)
                        sig = msig[:, i % 2, :]
                        if n == 0:
                            V.tensor_tensor(merged[:, m, :], bank[:, 0:T], sig, ALU.mult).then_inc(vring.empty, 1)
                            dve.wait_ge(vring.empty, c(vring.empty))
                        else:
                            V.tensor_tensor(sig, bank[:, 0:T], sig, ALU.mult).then_inc(vring.empty, 1)
                            dve.wait_ge(vring.empty, c(vring.empty))
                            V.tensor_tensor(merged[:, m, :], merged[:, m, :], sig, ALU.add).then_inc(vector_step, 1)
                            dve.wait_ge(vector_step, c(vector_step))
                        dve.sem_inc(sem_gate_used, 1)
                        c(sem_gate_used)
                dve.sem_inc(sem_merged_ready, 1)
                c(sem_merged_ready)
                for cc in range(2):
                    for t in range(NT):
                        bank = vring.take(dve)
                        xs = x[:, t, cc * 512:(cc + 1) * 512]
                        V.tensor_tensor(xs, xs, bank, ALU.add).then_inc(vring.empty, 1)
                        dve.wait_ge(vring.empty, c(vring.empty))
                dve.sem_inc(sem_layer_out, 1)
                c(sem_layer_out)

            dve.wait_ge(const_in, 32)
            for l in range(DEPTH):
                dve.wait_ge(param_in, 16 * (DEPTH + l + 1))
                for t in range(NT):
                    for j in range(2):
                        bank = vring.take(dve)
                        V.tensor_copy(xT[:, 4 * j:4 * j + 4, t * P:(t + 1) * P], split(bank, 4)).then_inc(vring.empty, 1)
                        dve.wait_ge(vring.empty, c(vring.empty))
                dve.sem_inc(sem_xT_ready, 1)
                c(sem_xT_ready)
                z8 = [tmp8[:, i, :] for i in range(4)]
                bank = vring.take(dve)
                V.tensor_tensor(split(z8[0]), split(bank[:, 0:8]), over_mid(pb("b_forget"), NT), ALU.add).then_inc(vring.empty, 1)
                dve.wait_ge(vring.empty, c(vring.empty))
                V.tensor_scalar(z8[0], z8[0], -1.0, None, ALU.mult).then_inc(sem_forget_inputs, 1)
                dve.wait_ge(sem_forget_inputs, c(sem_forget_inputs))
                dve.wait_ge(sem_forget_exps, c(sem_forget_exps))
                V.scalar_tensor_tensor(out=z8[2], in0=z8[0], scalar=0.0, in1=z8[1], op0=ALU.max, op1=ALU.add).then_inc(vector_step, 1)
                dve.wait_ge(vector_step, c(vector_step))
                V.tensor_scalar(logf, split(z8[2]), -1.0, None, ALU.mult).then_inc(sem_logf_ready, 1)
                dve.wait_ge(sem_logf_ready, c(sem_logf_ready))
                bank = vring.take(dve)
                V.tensor_copy(cq_tok, split(bank[:, 0:8])).then_inc(vring.empty, 1)
                dve.wait_ge(vring.empty, c(vring.empty))
                V.tensor_copy(f_row[:, 0], over_last(logf[:, 0, :], P)).then_inc(vector_step, 1)
                dve.wait_ge(vector_step, c(vector_step))
                V.tensor_copy(f_row[:, 1], over_last(logf[:, 1, :], P)).then_inc(sem_logf_rows, 1)
                dve.wait_ge(sem_logf_rows, c(sem_logf_rows))
                dve.wait_ge(sem_lora_rstd, c(sem_lora_rstd))
                for i in range(3):
                    gain = pb("g_cq")[:, i:i + 1] if i < 2 else pb("g_ckv")
                    V.scalar_tensor_tensor(out=cqkv[:, i, :], in0=cqkv[:, i, :], scalar=gain, in1=crs[:, i // 2, :],
                                           op0=ALU.mult, op1=ALU.mult).then_inc(vector_step, 1)
                    dve.wait_ge(vector_step, c(vector_step))
                dve.sem_inc(sem_lora_normed, 1)
                c(sem_lora_normed)
                causal = cb("causal").rearrange("p (t k) -> p t k", t=NT)

                def gather(group, t, add=False):
                    bank = vring.take(dve)
                    for r in range(2):
                        rows = slice(64 * r, 64 * r + 64)
                        src = split(bank[rows], 4)[:, r:4:2, :]
                        dst = oall[rows, 2 * group:2 * group + 2, t * P:(t + 1) * P]
                        op = V.tensor_tensor(dst, dst, src, ALU.add) if add else V.tensor_copy(dst, src)
                        last = vring.empty if r else vector_step
                        op.then_inc(last, 1)
                        dve.wait_ge(last, c(last))

                def unit_logits(unit):
                    group, t = divmod(unit, NT)
                    v = prob[:, 4 * (unit % 3):4 * (unit % 3) + 4, :]
                    nk = (t + 1) * P
                    if group == 0:
                        V.tensor_tensor(b2[:, :, 0:nk], over_last(cq_tok[:, t, :], nk), cdiff[:, :, 0:nk], ALU.subtract).then_inc(vector_step, 1)
                        dve.wait_ge(vector_step, c(vector_step))
                        softmax_logits(v, t, 0.125, causal[:, t, :], b2)
                    else:
                        softmax_logits(v, t, 96.0 ** -0.5, causal[:, t, :])
                    shift(v, nk, rowmax[:, 0:4])

                def unit_normalise(unit):
                    v = prob[:, 4 * (unit % 3):4 * (unit % 3) + 4, :]
                    normalise(v, (unit % NT + 1) * P, rowsum[:, 0:4])

                def unit_gather(unit):
                    gather(unit // NT + 1, unit % NT)

                def turn_dilated(v):
                    banks = [vring.take(dve) for _ in range(3)]
                    V.tensor_tensor(v, v, over_mid(cb("cos64"), 6), ALU.mult).then_inc(vector_step, 1)
                    dve.wait_ge(vector_step, c(vector_step))
                    for j, bank in enumerate(banks):
                        V.tensor_tensor(b1[:, 0:2, :], split(bank), over_mid(cb("sin64"), 2), ALU.mult).then_inc(vring.empty, 1)
                        dve.wait_ge(vring.empty, c(vring.empty))
                        V.tensor_tensor(v[:, 2 * j:2 * j + 2, :], v[:, 2 * j:2 * j + 2, :], b1[:, 0:2, :], ALU.add).then_inc(vector_step, 1)
                        dve.wait_ge(vector_step, c(vector_step))

                dve.wait_ge(sem_forget_rows, c(sem_forget_rows))
                unit_logits(0)
                for v in (mq, mk):
                    dve.wait_ge(sem_mla_raw, c(sem_mla_raw))
                    bank0 = vring.take(dve)
                    bank1 = vring.take(dve)
                    V.tensor_tensor(v[0:96], v[0:96], over_mid(cb("cos_mla", 96), 4), ALU.mult).then_inc(vector_step, 1)
                    dve.wait_ge(vector_step, c(vector_step))
                    for j, bank in ((0, bank0), (2, bank1)):
                        V.tensor_tensor(b1[0:96, 0:2, :], split(bank[0:96]), over_mid(cb("sin_mla", 96), 2), ALU.mult).then_inc(vring.empty, 1)
                        dve.wait_ge(vring.empty, c(vring.empty))
                        V.tensor_tensor(v[0:96, j:j + 2, :], v[0:96, j:j + 2, :], b1[0:96, 0:2, :], ALU.add).then_inc(vector_step, 1)
                        dve.wait_ge(vector_step, c(vector_step))
                dve.sem_inc(sem_attention_inputs, 1)
                c(sem_attention_inputs)
                unit_logits(1)
                unit_normalise(0)
                unit_logits(2)
                unit_gather(0)
                unit_normalise(1)
                unit_logits(3)
                unit_gather(1)
                unit_normalise(2)
                dve.wait_ge(sem_dil_raw, c(sem_dil_raw))
                turn_dilated(dq)
                unit_gather(2)
                unit_normalise(3)
                turn_dilated(dk)
                dve.sem_inc(sem_attention_inputs, 1)
                c(sem_attention_inputs)
                unit_gather(3)
                dve.sem_inc(sem_prob_free, 1)
                c(sem_prob_free)
                dil = cb("dilated").rearrange("p (b t k) -> p b t k", b=3, t=NT)
                for t in range(NT):
                    for br in range(3):
                        v = (prob if t else prob_0)[:, 4 * br:4 * br + 4, :]
                        softmax_logits(v, t, 0.125, dil[:, br, t, :])
                        shift(v, (t + 1) * P, rowmax_t[t][:, 4 * br:4 * br + 4])
                before = cb("before").rearrange("p (t k) -> p t k", t=NT)
                for t in range(NT):
                    nk = (t + 1) * P
                    p12 = prob if t else prob_0
                    for br in range(3):
                        dve.wait_ge(sem_exped, c(sem_exped))
                        last = sem_dens if br == 2 else vector_step
                        V.tensor_reduce(rowsum[:, 4 * br:4 * br + 4], p12[:, 4 * br:4 * br + 4, 0:nk], AX.X, ALU.add).then_inc(last, 1)
                        dve.wait_ge(last, c(last))
                    dve.wait_ge(sem_log_dens, c(sem_log_dens))
                    V.tensor_tensor(mixw, lse, rowmax_t[t], ALU.add).then_inc(vector_step, 1)
                    dve.wait_ge(vector_step, c(vector_step))
                    by_head = mixw.rearrange("p (b h) -> p h b", b=3)
                    V.tensor_reduce(mix1, by_head, AX.X, ALU.max).then_inc(vector_step, 1)
                    dve.wait_ge(vector_step, c(vector_step))
                    V.tensor_tensor(split(mixw, 3), split(mixw, 3), over_mid(mix1, 3), ALU.subtract).then_inc(sem_mix_shifted, 1)
                    dve.wait_ge(sem_mix_shifted, c(sem_mix_shifted))
                    dve.wait_ge(sem_mix_exps, c(sem_mix_exps))
                    V.tensor_reduce(mix1, by_head, AX.X, ALU.add).then_inc(vector_step, 1)
                    dve.wait_ge(vector_step, c(vector_step))
                    V.tensor_tensor(split(rowsum, 3), split(rowsum, 3), over_mid(mix1, 3), ALU.mult).then_inc(vector_step, 1)
                    dve.wait_ge(vector_step, c(vector_step))
                    V.reciprocal(rowsum, rowsum).then_inc(vector_step, 1)
                    dve.wait_ge(vector_step, c(vector_step))
                    V.tensor_tensor(mixw, mixw, rowsum, ALU.mult).then_inc(vector_step, 1)
                    dve.wait_ge(vector_step, c(vector_step))
                    V.tensor_tensor(p12[:, :, 0:nk], p12[:, :, 0:nk], over_last(mixw, nk), ALU.mult).then_inc(sem_probs_ready, 1)
                    dve.wait_ge(sem_probs_ready, c(sem_probs_ready))
                    if t == 0:
                        dve.wait_ge(sem_stick_logs, c(sem_stick_logs))
                        V.scalar_tensor_tensor(out=sp, in0=sz, scalar=0.0, in1=sp, op0=ALU.max, op1=ALU.add).then_inc(vector_step, 1)
                        dve.wait_ge(vector_step, c(vector_step))
                        for kt in range(NT):
                            V.scalar_tensor_tensor(out=slk[:, 4 * kt:4 * kt + 4, :], in0=sp[:, 4 * kt:4 * kt + 4, :], scalar=-1.0,
                                                   in1=over_mid(before[:, kt, :], 4), op0=ALU.mult, op1=ALU.mult).then_inc(vector_step, 1)
                            dve.wait_ge(vector_step, c(vector_step))
                        dve.sem_inc(sem_log_keep, 1)
                        c(sem_log_keep)
                        V.tensor_tensor(sz, sz, sp, ALU.subtract).then_inc(vector_step, 1)
                        dve.wait_ge(vector_step, c(vector_step))
                    else:
                        for i in range(4):
                            bank = vring.take(dve)
                            v = sz[:, 2 * i:2 * i + 2, :]
                            V.tensor_tensor(v, v, split(bank), ALU.add).then_inc(vring.empty, 1)
                            dve.wait_ge(vring.empty, c(vring.empty))
                        dve.sem_inc(sem_stick_sum, 1)
                        c(sem_stick_sum)
                    for br in range(3):
                        gather(3, t, br > 0)
                dve.wait_ge(sem_stick_exp, c(sem_stick_exp))
                for kt in range(NT):
                    v = sz[:, 4 * kt:4 * kt + 4, :]
                    V.tensor_tensor(v, v, over_mid(before[:, kt, :], 4), ALU.mult).then_inc(vector_step, 1)
                    dve.wait_ge(vector_step, c(vector_step))
                dve.sem_inc(sem_stick_weights, 1)
                c(sem_stick_weights)
                for tile in range(2):
                    bank = vring.take(dve)
                    for r in range(2):
                        rows = slice(64 * r, 64 * r + 64)
                        last = vring.empty if r else vector_step
                        V.tensor_copy(oall[rows, tile, :], bank[rows, r * T:(r + 1) * T]).then_inc(last, 1)
                        dve.wait_ge(last, c(last))
                dve.sem_inc(sem_o_all, 1)
                c(sem_o_all)
                dve.wait_ge(sem_o_rstd_b, c(sem_o_rstd_b))
                V.tensor_tensor(oall, oall, crs8, ALU.mult).then_inc(vector_step, 1)
                dve.wait_ge(vector_step, c(vector_step))
                V.tensor_tensor(oall, oall, over_last(pb("g_head"), T), ALU.mult).then_inc(sem_o_ready_b, 1)
                dve.wait_ge(sem_o_ready_b, c(sem_o_ready_b))
                dve.wait_ge(norms_in, 64 * (l + 1))
                for part in range(2):
                    if part == 0:
                        for cc in range(2):
                            for t in range(NT):
                                bank = vring.take(dve)
                                xs = x[:, t, cc * 512:(cc + 1) * 512]
                                V.scalar_tensor_tensor(out=xs, in0=xs, scalar=ALPHA, in1=bank, op0=ALU.mult, op1=ALU.add).then_inc(vring.empty, 1)
                                dve.wait_ge(vring.empty, c(vring.empty))
                    else:
                        V.scalar_tensor_tensor(out=x, in0=x, scalar=ALPHA, in1=ymoe, op0=ALU.mult, op1=ALU.add).then_inc(vector_step, 1)
                        dve.wait_ge(vector_step, c(vector_step))
                    V.tensor_reduce(mean, x, AX.X, ALU.add).then_inc(vector_step, 1)
                    dve.wait_ge(vector_step, c(vector_step))
                    V.tensor_scalar(mean, mean, 1.0 / D, None, ALU.mult).then_inc(vector_step, 1)
                    dve.wait_ge(vector_step, c(vector_step))
                    for t in range(NT):
                        last = sem_centred if t else vector_step
                        V.tensor_scalar(xc[:, t, :], x[:, t, :], mean[:, t:t + 1], None, ALU.subtract).then_inc(last, 1)
                        dve.wait_ge(last, c(last))
                    dve.wait_ge(sem_ln_rstd, c(sem_ln_rstd))
                    for t in range(NT):
                        V.scalar_tensor_tensor(out=x[:, t, :], in0=xc[:, t, :], scalar=rstd[:, t:t + 1],
                                               in1=ln_rows[:, 2 * part, :], op0=ALU.mult, op1=ALU.mult).then_inc(vector_step, 1)
                        dve.wait_ge(vector_step, c(vector_step))
                    last = sem_layer_out if part else sem_x_normed
                    V.tensor_tensor(x, x, over_mid(ln_rows[:, 2 * part + 1, :], NT), ALU.add).then_inc(last, 1)
                    dve.wait_ge(last, c(last))
                    if part:
                        break
                    for t in range(NT):
                        for j in range(2):
                            bank = vring.take(dve)
                            V.tensor_copy(xT[:, 4 * j:4 * j + 4, t * P:(t + 1) * P], split(bank, 4)).then_inc(vring.empty, 1)
                            dve.wait_ge(vring.empty, c(vring.empty))
                    dve.sem_inc(sem_xT_ready, 1)
                    c(sem_xT_ready)
                    bank = vring.take(dve)
                    V.tensor_tensor(router, split(bank[:, 0:40]), over_mid(pb("b_router"), NT), ALU.add).then_inc(vring.empty, 1)
                    dve.wait_ge(vring.empty, c(vring.empty))

                    def first_max(out, values, top, a_, b_):
                        V.tensor_reduce(top, values, AX.X, ALU.max).then_inc(vector_step, 1)
                        dve.wait_ge(vector_step, c(vector_step))
                        V.tensor_tensor(a_, values, over_last(top, 4), ALU.is_equal).then_inc(vector_step, 1)
                        dve.wait_ge(vector_step, c(vector_step))
                        V.memset(b_[:, :, 0:1], 0.0).then_inc(vector_step, 1)
                        dve.wait_ge(vector_step, c(vector_step))
                        for i in range(1, 4):
                            V.tensor_tensor(b_[:, :, i:i + 1], b_[:, :, i - 1:i], a_[:, :, i - 1:i], ALU.max).then_inc(vector_step, 1)
                            dve.wait_ge(vector_step, c(vector_step))
                        V.tensor_tensor(b_, b_, a_, ALU.mult).then_inc(vector_step, 1)
                        dve.wait_ge(vector_step, c(vector_step))
                        V.tensor_tensor(out, a_, b_, ALU.subtract).then_inc(vector_step, 1)
                        dve.wait_ge(vector_step, c(vector_step))

                    def r8(i):
                        return split(rt[:, i, 0:8])

                    top_g, top_1, top_2 = rt[:, 10, 0:2], rt[:, 10, 2:4], rt[:, 10, 4:6]
                    first_max(r8(0), router[:, :, 0:4], top_g, r8(2), r8(3))
                    V.tensor_tensor(r8(1), router[:, :, 0:4], over_last(top_g, 4), ALU.subtract).then_inc(sem_group_shifted, 1)
                    dve.wait_ge(sem_group_shifted, c(sem_group_shifted))
                    e_sel = r8(4)
                    V.tensor_tensor(e_sel, router[:, :, 4:8], over_last(r8(0)[:, :, 0], 4), ALU.mult).then_inc(vector_step, 1)
                    dve.wait_ge(vector_step, c(vector_step))
                    for gi in range(1, GROUPS):
                        V.tensor_tensor(r8(5), router[:, :, 4 + 4 * gi:8 + 4 * gi], over_last(r8(0)[:, :, gi], 4), ALU.mult).then_inc(vector_step, 1)
                        dve.wait_ge(vector_step, c(vector_step))
                        V.tensor_tensor(e_sel, e_sel, r8(5), ALU.add).then_inc(vector_step, 1)
                        dve.wait_ge(vector_step, c(vector_step))
                    first_max(r8(6), e_sel, top_1, r8(2), r8(3))
                    V.scalar_tensor_tensor(out=r8(5), in0=r8(6), scalar=NEG, in1=e_sel, op0=ALU.mult, op1=ALU.add).then_inc(vector_step, 1)
                    dve.wait_ge(vector_step, c(vector_step))
                    first_max(r8(7), r8(5), top_2, r8(2), r8(3))
                    V.tensor_tensor(rt[:, 9, 0:2], top_2, top_1, ALU.subtract).then_inc(sem_pair_shifted, 1)
                    dve.wait_ge(sem_pair_shifted, c(sem_pair_shifted))
                    dve.wait_ge(sem_group_exps, c(sem_group_exps))
                    V.tensor_reduce(rt[:, 11, 0:2], r8(1), AX.X, ALU.add).then_inc(vector_step, 1)
                    dve.wait_ge(vector_step, c(vector_step))
                    dve.wait_ge(sem_pair_exps, c(sem_pair_exps))
                    V.tensor_scalar(rt[:, 12, 0:2], rt[:, 9, 0:2], 1.0, None, ALU.add).then_inc(vector_step, 1)
                    dve.wait_ge(vector_step, c(vector_step))
                    V.tensor_tensor(rt[:, 12, 0:2], rt[:, 12, 0:2], rt[:, 11, 0:2], ALU.mult).then_inc(vector_step, 1)
                    dve.wait_ge(vector_step, c(vector_step))
                    V.reciprocal(rt[:, 12, 0:2], rt[:, 12, 0:2]).then_inc(vector_step, 1)
                    dve.wait_ge(vector_step, c(vector_step))
                    V.tensor_tensor(rt[:, 13, 0:2], rt[:, 12, 0:2], rt[:, 9, 0:2], ALU.mult).then_inc(vector_step, 1)
                    dve.wait_ge(vector_step, c(vector_step))
                    for j, one in enumerate((r8(6), r8(7))):
                        for gi in range(GROUPS):
                            V.tensor_tensor(split(chosen[:, j, :])[:, :, 4 * gi:4 * gi + 4], one,
                                            over_last(r8(0)[:, :, gi], 4), ALU.mult).then_inc(vector_step, 1)
                            dve.wait_ge(vector_step, c(vector_step))
                    V.tensor_tensor(chosen[:, 2, :], chosen[:, 0, :], chosen[:, 1, :], ALU.add).then_inc(sem_chosen, 1)
                    dve.wait_ge(sem_chosen, c(sem_chosen))
                    bank = vring.take(dve)
                    V.tensor_tensor(rank, bank[:, 0:32], chosen[:, 2, :], ALU.subtract).then_inc(vector_step, 1)
                    dve.wait_ge(vector_step, c(vector_step))
                    V.tensor_reduce(mix1[:, 0:1], bank[:, 32:48], AX.X, ALU.max).then_inc(vring.empty, 1)
                    dve.wait_ge(vring.empty, c(vring.empty))
                    V.tensor_tensor(split(rank), split(rank), over_mid(cb("first_row"), NT), ALU.add).then_inc(vector_step, 1)
                    dve.wait_ge(vector_step, c(vector_step))
                    for j in range(2):
                        V.tensor_tensor(chosen[:, 2, :], chosen[:, j, :], rank, ALU.mult).then_inc(vector_step, 1)
                        dve.wait_ge(vector_step, c(vector_step))
                        V.tensor_reduce(rows_f[:, j:4:2], split(chosen[:, 2, :]), AX.X, ALU.add).then_inc(vector_step, 1)
                        dve.wait_ge(vector_step, c(vector_step))
                    V.tensor_copy(rows_of, rows_f).then_inc(vector_step, 1)
                    dve.wait_ge(vector_step, c(vector_step))
                    V.tensor_scalar(mix1[0:1, 1:2], mix1[0:1, 0:1], CROWD, None, ALU.is_gt).then_inc(vector_step, 1)
                    dve.wait_ge(vector_step, c(vector_step))
                    V.tensor_copy(crowded, mix1[0:1, 1:2]).then_inc(sem_crowded, 1)
                    dve.wait_ge(sem_crowded, c(sem_crowded))
                    full = dve.value_load(crowded, min_val=0, max_val=1)
                    start = branch_state(c, vring, sring)
                    with dve.If(full != 0):
                        for t in range(NT):
                            for j in range(2):
                                part_of = split(chosen[:, j, :])[:, t, :]
                                gate = rt[:, 12 + j, t:t + 1]
                                if j == 0:
                                    V.tensor_scalar(gates[:, t, :], part_of, gate, None, ALU.mult).then_inc(vector_step, 1)
                                else:
                                    V.scalar_tensor_tensor(out=gates[:, t, :], in0=part_of, scalar=gate, in1=gates[:, t, :],
                                                           op0=ALU.mult, op1=ALU.add).then_inc(vector_step, 1)
                                dve.wait_ge(vector_step, c(vector_step))
                        for e in range(EXPERTS + 1):
                            if e < EXPERTS:
                                for m in range(4):
                                    dve.wait_ge(sem_hidden_silu, c(sem_hidden_silu))
                                    bank = vring.take(dve)
                                    hv = hh[e % 2][:, m, :]
                                    V.tensor_tensor(hv, hv, bank[:, 0:T], ALU.mult).then_inc(vring.empty, 1)
                                    dve.wait_ge(vring.empty, c(vring.empty))
                                dve.sem_inc(sem_hidden_ready, 1)
                                c(sem_hidden_ready)
                            if e:
                                for t in range(NT):
                                    for cc in range(2):
                                        bank = vring.take(dve)
                                        ys = ymoe[:, t, cc * 512:(cc + 1) * 512]
                                        gate = gates[:, t, e - 1:e]
                                        if e == 1:
                                            V.tensor_scalar(ys, bank, gate, None, ALU.mult).then_inc(vring.empty, 1)
                                        else:
                                            V.scalar_tensor_tensor(out=ys, in0=bank, scalar=gate, in1=ys,
                                                                   op0=ALU.mult, op1=ALU.add).then_inc(vring.empty, 1)
                                        dve.wait_ge(vring.empty, c(vring.empty))
                                dve.sem_inc(sem_hidden_used, 1)
                                c(sem_hidden_used)
                        make_up(dve, c, start, (sem_hidden_ready, sem_hidden_used, sem_rows_turned, sem_h_rows,
                                              sem_y_out), emptied=(vring,))
                    to_state(c, start, vring, sring)
                    with dve.Else():
                        def turned_in(e):
                            bank = vring.take(dve)
                            V.tensor_copy(x_turned[:, e % 2, 512:1024], bank).then_inc(vring.empty, 1)
                            dve.wait_ge(vring.empty, c(vring.empty))
                            dve.sem_inc(sem_rows_turned, 1)
                            c(sem_rows_turned)

                        turned_in(0)
                        for e in range(EXPERTS + 1):
                            if e < EXPERTS:
                                dve.wait_ge(sem_hidden_silu, c(sem_hidden_silu))
                                bank = vring.take(dve)
                                V.tensor_tensor(h_rows[:, e % 2, :], h_silu[:, e % 2, :], bank, ALU.mult)\
                                    .then_inc(vring.empty, 1)
                                dve.wait_ge(vring.empty, c(vring.empty))
                                dve.sem_inc(sem_h_rows, 1)
                                c(sem_h_rows)
                            if e + 1 < EXPERTS:
                                turned_in(e + 1)
                            if e:
                                if e >= 3:
                                    dve.wait_ge(y_rows_out[(e - 1) % 2], 16 * c(y_rows_out[(e - 1) % 2]))
                                for cc in range(2):
                                    bank = vring.take(dve)
                                    V.tensor_copy(y_out[:, (e - 1) % 2, cc * 512:(cc + 1) * 512], bank)\
                                        .then_inc(vring.empty, 1)
                                    dve.wait_ge(vring.empty, c(vring.empty))
                                dve.sem_inc(sem_y_out, 1)
                                c(sem_y_out)
                        for i in range(2):
                            dve.wait_ge(y_rows_out[i], 16 * c(y_rows_out[i]))
                        dve.wait_ge(y_rows_in, 64 * c(y_rows_in))
                        for t in range(NT):
                            V.tensor_scalar(ymoe[:, t, :], y_in[:, 2 * t, :], rt[:, 12, t:t + 1], None, ALU.mult)\
                                .then_inc(vector_step, 1)
                            dve.wait_ge(vector_step, c(vector_step))
                            V.scalar_tensor_tensor(out=ymoe[:, t, :], in0=y_in[:, 2 * t + 1, :], scalar=rt[:, 13, t:t + 1],
                                                   in1=ymoe[:, t, :], op0=ALU.mult, op1=ALU.add).then_inc(vector_step, 1)
                            dve.wait_ge(vector_step, c(vector_step))
                        make_up(dve, c, start, (sem_hidden_ready, sem_hidden_used, sem_rows_turned, sem_h_rows,
                                              sem_y_out), emptied=(vring,))


def pack(inputs):
    f = {k: np.asarray(v) for k, v in inputs.items()}

    def channels(v):
        return v.reshape(-1, P).T

    def rows(v):
        return np.broadcast_to(v.reshape(1, -1), (P, v.size))

    a, b = [], []
    for l in range(DEPTH):
        conv = f["conv_w"][l].reshape(CONV, 12, P).transpose(2, 1, 0).reshape(P, -1)
        a.append(np.concatenate([
            channels(f["norm_g"][l]), conv, channels(f["gate_b"][l]), channels(f["dn_onorm"][l]),
            channels(f["pool_scale"][l]), channels(f["q_norm"][l]), channels(f["k_norm"][l]), rows(f["a_log"][l]),
            rows(f["dt_bias"][l]), f["pool_w"][l].transpose(1, 0, 2).reshape(P, -1)], 1))
        router = np.concatenate([f["w_group_2"][l], f["w_expert_2"][l]], 1).reshape(KD, P, 20).transpose(1, 0, 2)
        b.append(np.concatenate([
            rows(f["b_forget_2"][l]), channels(f["g_cq_2"][l]), channels(f["g_ckv_2"][l]), channels(f["g_head_2"][l]),
            rows(np.concatenate([f["b_group_2"][l], f["b_expert_2"][l]])), router.reshape(P, -1),
            f["w_uq_2"][l].reshape(2, P, -1).transpose(1, 0, 2).reshape(P, -1), f["w_ukv_2"][l]], 1))
    return np.ascontiguousarray(np.stack(a)), np.ascontiguousarray(np.stack(b))


_STREAMED = ["x", "w_in", "w_branch", "w_out", "w_in_2", "w_out_2", "w1_2", "w3_2", "w2_2",
             "ln1_g_2", "ln1_b_2", "ln2_g_2", "ln2_b_2"]


def kernel(**inputs):
    import concourse.bacc as bacc
    from concourse.bass_utils import run_bass_kernel_spmd

    nc = bacc.Bacc("TRN2", target_bir_lowering=False, num_devices=1)
    arrays = {name: np.ascontiguousarray(inputs[name]) for name in _STREAMED}
    arrays["param_a"], arrays["param_b"] = pack(inputs)
    arrays["const_a"], arrays["const_b"] = constants()
    dram = {name: nc.dram_tensor(f"in_{name}", v.shape, F32, kind="ExternalInput").ap() for name, v in arrays.items()}
    dram["out"] = nc.dram_tensor("out", (1, T, D), F32, kind="ExternalOutput").ap()
    build_program(nc, dram)
    r = run_bass_kernel_spmd(nc, [{f"in_{name}": v for name, v in arrays.items()}], core_ids=[0])
    return r.results[0]["out"]
```
